# Optimizing a Trainium2 kernel written in Bass

```python
import math
import jax, jax.numpy as jnp
from jax import lax
import numpy as np

D_MODEL = 1024
BATCH = 1
SEQ = 512
DEPTH = 2

CHUNK = 64
RMS_EPS = 1e-6
DN_WIDTH = D_MODEL // 2
DN_DHEAD = 128
DN_HEADS = DN_WIDTH // DN_DHEAD
DN_CONV = 4
SA_WIDTH = D_MODEL // 4
SA_DHEAD = 64
SA_HEADS = SA_WIDTH // SA_DHEAD
SA_DKV = SA_DHEAD
IDX_HEADS = 4
IDX_DHEAD = 64
IDX_TOPK_MAX = 256
Q_BLOCK = 128
HG_WIDTH = D_MODEL // 4
HG_DHEAD = 64
HG_HEADS = HG_WIDTH // HG_DHEAD
D_MIX = DN_WIDTH + SA_WIDTH + HG_WIDTH
D_FF = 2816
FFN_CONV = 3

SPLIT_SIZES = (DN_WIDTH, DN_WIDTH, DN_WIDTH, DN_WIDTH, DN_HEADS, DN_HEADS,
               SA_WIDTH, SA_DKV, SA_DKV, IDX_HEADS * IDX_DHEAD, IDX_DHEAD, IDX_HEADS,
               HG_WIDTH, HG_WIDTH, HG_WIDTH, HG_WIDTH)
D_IN = sum(SPLIT_SIZES)
SPLIT_POINTS = tuple(int(p) for p in np.cumsum(SPLIT_SIZES)[:-1])


def rmsnorm(x, g):
    xf = x.astype(jnp.float32)
    y = xf * lax.rsqrt(jnp.mean(xf * xf, axis=-1, keepdims=True) + RMS_EPS)
    return (y * g.astype(jnp.float32)).astype(x.dtype)

def l2norm(x):
    return x * lax.rsqrt(jnp.sum(x * x, axis=-1, keepdims=True) + 1e-6)

def causal_depthwise_conv(x, w):
    K, C = w.shape
    return lax.conv_general_dilated(x, w[:, None, :].astype(x.dtype), window_strides=(1,),
                                    padding=[(K - 1, 0)],
                                    dimension_numbers=('NWC', 'WIO', 'NWC'),
                                    feature_group_count=C)

def to_chunks(t, n_heads, d_head):
    B, S = t.shape[:2]
    return t.reshape(B, S // CHUNK, CHUNK, n_heads, d_head).transpose(0, 3, 1, 2, 4)

def gate_chunks(t):
    B, S, H = t.shape
    return t.reshape(B, S // CHUNK, CHUNK, H).transpose(0, 3, 1, 2)

def from_chunks(o):
    N, B, H, C, d = o.shape
    return o.transpose(1, 0, 3, 2, 4).reshape(B, N * C, H, d)

def gated_deltanet(q, k, v, z, b, a, conv_w, a_log, dt_bias, norm_g):
    dtype = q.dtype
    Bsz, S, _ = q.shape
    qkv = jax.nn.silu(causal_depthwise_conv(jnp.concatenate([q, k, v], axis=-1), conv_w))
    q, k, v = jnp.split(qkv.astype(jnp.float32), 3, axis=-1)
    q = l2norm(to_chunks(q, DN_HEADS, DN_DHEAD)) * (DN_DHEAD ** -0.5)
    k = l2norm(to_chunks(k, DN_HEADS, DN_DHEAD))
    v = to_chunks(v, DN_HEADS, DN_DHEAD)
    beta = gate_chunks(jax.nn.sigmoid(b.astype(jnp.float32)))
    g = -jnp.exp(a_log.astype(jnp.float32)) * jax.nn.softplus(
        a.astype(jnp.float32) + dt_bias.astype(jnp.float32))
    G = jnp.cumsum(gate_chunks(g), axis=-1)
    causal = jnp.tril(jnp.ones((CHUNK, CHUNK), bool))
    strict = jnp.tril(jnp.ones((CHUNK, CHUNK), bool), k=-1)
    decay = jnp.exp(jnp.where(causal, G[..., :, None] - G[..., None, :], -jnp.inf))
    kk = jnp.einsum('bhnck,bhnsk->bhncs', k, k)
    M = jnp.where(strict, beta[..., :, None] * kk * decay, 0.0)
    eye = jnp.eye(CHUNK, dtype=jnp.float32)
    T = lax.linalg.triangular_solve(eye + M, jnp.broadcast_to(eye, M.shape),
                                    left_side=True, lower=True, unit_diagonal=True)
    u0 = jnp.einsum('bhncs,bhnsv->bhncv', T, beta[..., None] * v)
    wk = jnp.einsum('bhncs,bhnsk->bhnck', T, (beta * jnp.exp(G))[..., None] * k)
    qk = jnp.einsum('bhnck,bhnsk->bhncs', q, k) * decay
    q_dec = q * jnp.exp(G)[..., None]
    k_dec = k * jnp.exp(G[..., -1:] - G)[..., None]
    g_last = jnp.exp(G[..., -1])

    def step(state, inp):
        u0_c, w_c, qk_c, qd_c, kd_c, gl_c = inp
        u = u0_c - jnp.einsum('bhck,bhkv->bhcv', w_c, state)
        o = jnp.einsum('bhck,bhkv->bhcv', qd_c, state) + jnp.einsum('bhcs,bhsv->bhcv', qk_c, u)
        state = state * gl_c[..., None, None] + jnp.einsum('bhck,bhcv->bhkv', kd_c, u)
        return state, o

    xs = tuple(jnp.moveaxis(t, 2, 0) for t in (u0, wk, qk, q_dec, k_dec, g_last))
    s0 = jnp.zeros((Bsz, DN_HEADS, DN_DHEAD, DN_DHEAD), jnp.float32)
    _, o = lax.scan(step, s0, xs)
    o = rmsnorm(from_chunks(o), norm_g)
    o = o * jax.nn.silu(z.astype(jnp.float32).reshape(Bsz, S, DN_HEADS, DN_DHEAD))
    return o.reshape(Bsz, S, DN_WIDTH).astype(dtype)

def dsa_attention(q, k, v, qi, ki, wi):
    dtype = q.dtype
    Bsz, S, _ = q.shape
    nb = S // Q_BLOCK
    topk = min(IDX_TOPK_MAX, S // 4)
    f32 = jnp.float32
    qb_all = q.astype(f32).reshape(Bsz, nb, Q_BLOCK, SA_HEADS, SA_DHEAD).transpose(1, 0, 2, 3, 4)
    qib_all = qi.astype(f32).reshape(Bsz, nb, Q_BLOCK, IDX_HEADS, IDX_DHEAD).transpose(1, 0, 2, 3, 4)
    wib_all = (wi.astype(f32) * (IDX_HEADS ** -0.5 * IDX_DHEAD ** -0.5)).reshape(
        Bsz, nb, Q_BLOCK, IDX_HEADS).transpose(1, 0, 2, 3)
    k = k.astype(f32)
    v = v.astype(f32)
    ki = ki.astype(f32)
    key_chunk = jnp.arange(S) // CHUNK
    gather = jax.vmap(lambda t, idx: t[idx])

    def block(args):
        qb, qib, wib, blk = args
        q_chunk = (blk * Q_BLOCK + jnp.arange(Q_BLOCK)) // CHUNK
        score = jnp.einsum('bqhs,bqh->bqs',
                           jax.nn.relu(jnp.einsum('bqhd,bsd->bqhs', qib, ki)), wib)
        admissible = key_chunk[None, :] <= q_chunk[:, None]
        score = jnp.where(admissible[None], score, -jnp.inf)
        _, idx = lax.top_k(score, topk)
        k_sel = gather(k, idx)
        v_sel = gather(v, idx)
        valid = key_chunk[idx] <= q_chunk[None, :, None]
        logits = jnp.einsum('bqhd,bqkd->bqhk', qb, k_sel) * (SA_DHEAD ** -0.5)
        logits = jnp.where(valid[:, :, None, :], logits, -jnp.inf)
        p = jax.nn.softmax(logits, axis=-1)
        return jnp.einsum('bqhk,bqkd->bqhd', p, v_sel)

    o = lax.map(block, (qb_all, qib_all, wib_all, jnp.arange(nb)))
    return o.transpose(1, 0, 2, 3, 4).reshape(Bsz, S, SA_WIDTH).astype(dtype)

def hgrn2(q, f, i, g, lb, norm_g):
    dtype = q.dtype
    Bsz, S, _ = q.shape
    f32 = jnp.float32
    fg = lb + (1.0 - lb) * jax.nn.sigmoid(f.astype(f32))
    qc = to_chunks(jax.nn.silu(q.astype(f32)), HG_HEADS, HG_DHEAD)
    kc = to_chunks(1.0 - fg, HG_HEADS, HG_DHEAD)
    vc = to_chunks(i.astype(f32), HG_HEADS, HG_DHEAD)
    Bc = jnp.cumsum(to_chunks(jnp.log(fg), HG_HEADS, HG_DHEAD), axis=-2)
    q_dec = qc * jnp.exp(Bc)
    k_dec = kc * jnp.exp(Bc[..., -1:, :] - Bc)
    g_last = jnp.exp(Bc[..., -1, :])
    causal = jnp.tril(jnp.ones((CHUNK, CHUNK), bool))[..., None]

    def step(state, inp):
        q_c, k_c, v_c, b_c, qd_c, kd_c, gl_c = inp
        dec = jnp.exp(jnp.where(causal, b_c[..., :, None, :] - b_c[..., None, :, :], -jnp.inf))
        A = jnp.einsum('bhck,bhsk,bhcsk->bhcs', q_c, k_c, dec)
        o = jnp.einsum('bhck,bhkv->bhcv', qd_c, state) + jnp.einsum('bhcs,bhsv->bhcv', A, v_c)
        state = gl_c[..., :, None] * state + jnp.einsum('bhck,bhcv->bhkv', kd_c, v_c)
        return state, o

    xs = tuple(jnp.moveaxis(t, 2, 0) for t in (qc, kc, vc, Bc, q_dec, k_dec, g_last))
    s0 = jnp.zeros((Bsz, HG_HEADS, HG_DHEAD, HG_DHEAD), f32)
    _, o = lax.scan(step, s0, xs)
    o = rmsnorm(from_chunks(o), norm_g)
    o = o * jax.nn.silu(g.astype(f32).reshape(Bsz, S, HG_HEADS, HG_DHEAD))
    return o.reshape(Bsz, S, HG_WIDTH).astype(dtype)

def conv_geglu_ffn(h, w_up, conv_w, w_down):
    up = causal_depthwise_conv(h @ w_up, conv_w)
    gate, val = jnp.split(up, 2, axis=-1)
    return (jax.nn.gelu(gate, approximate=True) * val) @ w_down

def first_inputs(seed: int = 0) -> dict:
    key = jax.random.key(seed)
    ks = jax.random.split(key, 16)
    f32 = jnp.float32
    nrm = lambda k, s: jax.random.normal(k, s, f32)
    x = nrm(ks[0], (BATCH, SEQ, D_MODEL))
    w_in = nrm(ks[1], (DEPTH, D_MODEL, D_IN)) * D_MODEL ** -0.5
    dn_conv = nrm(ks[2], (DEPTH, DN_CONV, 3 * DN_WIDTH)) * DN_CONV ** -0.5
    dn_a_log = jnp.log(jax.random.uniform(ks[3], (DEPTH, DN_HEADS), f32, 1.0, 16.0))
    dt = jnp.exp(jax.random.uniform(ks[4], (DEPTH, DN_HEADS), f32,
                                    math.log(1e-3), math.log(1e-1)))
    dn_dt_bias = dt + jnp.log(-jnp.expm1(-dt))
    dn_norm = 1.0 + 0.02 * nrm(ks[5], (DEPTH, DN_DHEAD))
    hg_lb = 0.1 * nrm(ks[6], (DEPTH, HG_WIDTH))
    hg_norm = 1.0 + 0.02 * nrm(ks[7], (DEPTH, HG_DHEAD))
    w_out = nrm(ks[8], (DEPTH, D_MIX, D_MODEL)) * D_MIX ** -0.5
    g_mix_pre = 1.0 + 0.02 * nrm(ks[9], (DEPTH, D_MODEL))
    g_mix_post = 1.0 + 0.02 * nrm(ks[10], (DEPTH, D_MODEL))
    g_ffn_pre = 1.0 + 0.02 * nrm(ks[11], (DEPTH, D_MODEL))
    g_ffn_post = 1.0 + 0.02 * nrm(ks[12], (DEPTH, D_MODEL))
    ffn_w_up = nrm(ks[13], (DEPTH, D_MODEL, 2 * D_FF)) * D_MODEL ** -0.5
    ffn_conv = nrm(ks[14], (DEPTH, FFN_CONV, 2 * D_FF)) * FFN_CONV ** -0.5
    ffn_w_down = nrm(ks[15], (DEPTH, D_FF, D_MODEL)) * D_FF ** -0.5
    return {'x': x, 'w_in': w_in, 'dn_conv': dn_conv, 'dn_a_log': dn_a_log,
            'dn_dt_bias': dn_dt_bias, 'dn_norm': dn_norm, 'hg_lb': hg_lb, 'hg_norm': hg_norm,
            'w_out': w_out, 'g_mix_pre': g_mix_pre, 'g_mix_post': g_mix_post,
            'g_ffn_pre': g_ffn_pre, 'g_ffn_post': g_ffn_post, 'ffn_w_up': ffn_w_up,
            'ffn_conv': ffn_conv, 'ffn_w_down': ffn_w_down}

def first_block(x, w_in, dn_conv, dn_a_log, dn_dt_bias, dn_norm, hg_lb, hg_norm, w_out,
              g_mix_pre, g_mix_post, g_ffn_pre, g_ffn_post, ffn_w_up, ffn_conv, ffn_w_down):
    cs = jnp.cumsum(jax.nn.softmax(hg_lb.astype(jnp.float32), axis=0), axis=0)
    lower_bounds = cs - cs[0:1]
    for l in range(DEPTH):
        h = rmsnorm(x, g_mix_pre[l])
        (a_q, a_k, a_v, a_z, a_b, a_a,
         b_q, b_k, b_v, b_qi, b_ki, b_wi,
         c_q, c_f, c_i, c_g) = jnp.split(h @ w_in[l], SPLIT_POINTS, axis=-1)
        o_a = gated_deltanet(a_q, a_k, a_v, a_z, a_b, a_a, dn_conv[l], dn_a_log[l],
                             dn_dt_bias[l], dn_norm[l])
        o_b = dsa_attention(b_q, b_k, b_v, b_qi, b_ki, b_wi)
        o_c = hgrn2(c_q, c_f, c_i, c_g, lower_bounds[l], hg_norm[l])
        mix = jnp.concatenate([o_a, o_b, o_c], axis=-1) @ w_out[l]
        x = x + rmsnorm(mix, g_mix_post[l])
        h = rmsnorm(x, g_ffn_pre[l])
        x = x + rmsnorm(conv_geglu_ffn(h, ffn_w_up[l], ffn_conv[l], ffn_w_down[l]), g_ffn_post[l])
    return x


HEAD_DIM = 64
LRU_WIDTH = D_MODEL // 2
LRU_BLOCKS = LRU_WIDTH // HEAD_DIM
SB_HEADS = D_MODEL // 256
FOX_HEADS = D_MODEL // 256
SB_WIDTH = SB_HEADS * HEAD_DIM
FOX_WIDTH = FOX_HEADS * HEAD_DIM
D_MIX_2 = LRU_WIDTH + SB_WIDTH + FOX_WIDTH
CONV_WIDTH = 4
LRU_C = 8.0
N_SUB = 3
EPS = 1e-6

SPLIT_SIZES_2 = (LRU_WIDTH, LRU_WIDTH,
               SB_WIDTH, SB_WIDTH, SB_WIDTH,
               FOX_WIDTH, FOX_WIDTH, FOX_WIDTH,
               FOX_HEADS)
N_IN = sum(SPLIT_SIZES_2)
SPLIT_POINTS_2 = tuple(int(v) for v in np.cumsum(SPLIT_SIZES_2)[:-1])


def _rms(x):
    xf = x.astype(jnp.float32)
    y = xf * lax.rsqrt(jnp.mean(xf * xf, axis=-1, keepdims=True) + EPS)
    return y.astype(x.dtype)

def _swiglu(h, w_up, w_down):
    gu = h @ w_up
    g, u = jnp.split(gu, 2, axis=-1)
    return (jax.nn.silu(g) * u) @ w_down

def _causal_depthwise_conv(x, w, b):
    y = lax.conv_general_dilated(
        x, w[:, None, :], window_strides=(1,), padding=[(CONV_WIDTH - 1, 0)],
        dimension_numbers=("NWC", "WIO", "NWC"), feature_group_count=x.shape[-1])
    return y + b

def _lru_combine(left, right):
    a1, b1 = left
    a2, b2 = right
    return a1 * a2, a2 * b1 + b2

def _rg_lru(u, w_r, b_r, w_i, b_i, lam):
    B, S, _ = u.shape
    ub = u.reshape(B, S, LRU_BLOCKS, HEAD_DIM)
    r = jax.nn.sigmoid(jnp.einsum("bshi,hij->bshj", ub, w_r).reshape(B, S, LRU_WIDTH) + b_r)
    i = jax.nn.sigmoid(jnp.einsum("bshi,hij->bshj", ub, w_i).reshape(B, S, LRU_WIDTH) + b_i)
    r = r.astype(jnp.float32)
    log_a = -LRU_C * r * jax.nn.softplus(-lam.astype(jnp.float32))
    a = jnp.exp(log_a)
    mult = jnp.sqrt(-jnp.expm1(2.0 * log_a))
    bt = mult * (i.astype(jnp.float32) * u.astype(jnp.float32))
    _, h = lax.associative_scan(_lru_combine, (a, bt), axis=1)
    return h.astype(u.dtype)

def _to_heads(t, n_heads):
    B, S, _ = t.shape
    return t.reshape(B, S, n_heads, HEAD_DIM).transpose(0, 2, 1, 3)

def _from_blocks(out):
    nb, B, H, Q, Dh = out.shape
    return out.transpose(1, 0, 3, 2, 4).reshape(B, nb * Q, H * Dh)

def _stick_breaking_attention(q, k, v):
    S = q.shape[2]
    scale = HEAD_DIM ** -0.5
    key_pos = jnp.arange(S)

    def block(bi):
        start = bi * Q_BLOCK
        qb = lax.dynamic_slice_in_dim(q, start, Q_BLOCK, axis=2)
        z = jnp.einsum("bhqd,bhkd->bhqk", qb, k).astype(jnp.float32) * scale
        q_pos = start + jnp.arange(Q_BLOCK)
        past = key_pos[None, :] < q_pos[:, None]
        log_beta = jax.nn.log_sigmoid(z)
        log_1mb = jnp.where(past, jax.nn.log_sigmoid(-z), 0.0)
        after = lax.cumsum(log_1mb, axis=3, reverse=True) - log_1mb
        w = jnp.where(past, jnp.exp(log_beta + after), 0.0)
        return jnp.einsum("bhqk,bhkd->bhqd", w.astype(v.dtype), v)

    return _from_blocks(lax.map(block, jnp.arange(S // Q_BLOCK)))

def _forgetting_attention(q, k, v, log_f):
    S = q.shape[2]
    scale = HEAD_DIM ** -0.5
    key_pos = jnp.arange(S)
    F = jnp.cumsum(log_f, axis=-1)

    def block(bi):
        start = bi * Q_BLOCK
        qb = lax.dynamic_slice_in_dim(q, start, Q_BLOCK, axis=2)
        Fq = lax.dynamic_slice_in_dim(F, start, Q_BLOCK, axis=2)
        logits = jnp.einsum("bhqd,bhkd->bhqk", qb, k).astype(jnp.float32) * scale
        logits = logits + Fq[..., :, None] - F[..., None, :]
        q_pos = start + jnp.arange(Q_BLOCK)
        causal = key_pos[None, :] <= q_pos[:, None]
        logits = jnp.where(causal, logits, -jnp.inf)
        p = jax.nn.softmax(logits, axis=-1)
        return jnp.einsum("bhqk,bhkd->bhqd", p.astype(v.dtype), v)

    return _from_blocks(lax.map(block, jnp.arange(S // Q_BLOCK)))

def _mixer(h, w_in, b_fgate, conv_w, conv_b, w_rgate, b_rgate, w_igate, b_igate,
           lru_lambda, g_qk, g_mix_out, w_out):
    proj = h @ w_in
    (lru_x, lru_g, sb_q, sb_k, sb_v, fx_q, fx_k, fx_v, fx_f) = jnp.split(proj, SPLIT_POINTS_2, axis=-1)

    u = _causal_depthwise_conv(lru_x, conv_w, conv_b)
    y_lru = _rg_lru(u, w_rgate, b_rgate, w_igate, b_igate, lru_lambda) * jax.nn.gelu(lru_g)

    y_sb = _stick_breaking_attention(_to_heads(sb_q, SB_HEADS), _to_heads(sb_k, SB_HEADS),
                                     _to_heads(sb_v, SB_HEADS))

    fq = _rms(_to_heads(fx_q, FOX_HEADS)) * g_qk[0]
    fk = _rms(_to_heads(fx_k, FOX_HEADS)) * g_qk[1]
    log_f = jax.nn.log_sigmoid(fx_f.astype(jnp.float32) + b_fgate.astype(jnp.float32))
    y_fox = _forgetting_attention(fq, fk, _to_heads(fx_v, FOX_HEADS), log_f.transpose(0, 2, 1))

    y = jnp.concatenate([_rms(y_lru), _rms(y_sb), _rms(y_fox)], axis=-1) * g_mix_out
    return y @ w_out

def second_inputs(seed: int = 0) -> dict:
    key = jax.random.key(seed)
    ks = jax.random.split(key, 20)
    f32 = jnp.float32
    nrm = lambda k, shape, s: jax.random.normal(k, shape, f32) * s
    x = jax.random.normal(ks[0], (BATCH, SEQ, D_MODEL), f32)
    c = jax.random.normal(ks[1], (BATCH, D_MODEL), f32)
    w_ada = nrm(ks[2], (DEPTH, D_MODEL, N_SUB * 3 * D_MODEL), 0.1 * D_MODEL ** -0.5)
    b_ada = nrm(ks[3], (DEPTH, N_SUB * 3 * D_MODEL), 0.01)
    g_norm = 1.0 + nrm(ks[4], (DEPTH, N_SUB, D_MODEL), 0.05)
    w_ffn_up = nrm(ks[5], (DEPTH, 2, D_MODEL, 2 * D_FF), D_MODEL ** -0.5)
    w_ffn_down = nrm(ks[6], (DEPTH, 2, D_FF, D_MODEL), D_FF ** -0.5)
    w_in = nrm(ks[7], (DEPTH, D_MODEL, N_IN), D_MODEL ** -0.5)
    b_fgate = 3.0 + nrm(ks[8], (DEPTH, FOX_HEADS), 0.1)
    conv_w = nrm(ks[9], (DEPTH, CONV_WIDTH, LRU_WIDTH), CONV_WIDTH ** -0.5)
    conv_b = nrm(ks[10], (DEPTH, LRU_WIDTH), 0.01)
    w_rgate = nrm(ks[11], (DEPTH, LRU_BLOCKS, HEAD_DIM, HEAD_DIM), HEAD_DIM ** -0.5)
    b_rgate = nrm(ks[12], (DEPTH, LRU_WIDTH), 0.01)
    w_igate = nrm(ks[13], (DEPTH, LRU_BLOCKS, HEAD_DIM, HEAD_DIM), HEAD_DIM ** -0.5)
    b_igate = nrm(ks[14], (DEPTH, LRU_WIDTH), 0.01)
    a_c = jax.random.uniform(ks[15], (DEPTH, LRU_WIDTH), f32, 0.9, 0.999)
    s = a_c ** (1.0 / LRU_C)
    lru_lambda = jnp.log(s) - jnp.log1p(-s)
    g_qk = 1.0 + nrm(ks[16], (DEPTH, 2, HEAD_DIM), 0.05)
    g_mix_out = 1.0 + nrm(ks[17], (DEPTH, D_MIX_2), 0.05)
    w_out = nrm(ks[18], (DEPTH, D_MIX_2, D_MODEL), D_MIX_2 ** -0.5)
    return {"x": x, "c": c, "w_ada": w_ada, "b_ada": b_ada, "g_norm": g_norm,
            "w_ffn_up": w_ffn_up, "w_ffn_down": w_ffn_down, "w_in": w_in,
            "b_fgate": b_fgate, "conv_w": conv_w, "conv_b": conv_b,
            "w_rgate": w_rgate, "b_rgate": b_rgate, "w_igate": w_igate,
            "b_igate": b_igate, "lru_lambda": lru_lambda, "g_qk": g_qk,
            "g_mix_out": g_mix_out, "w_out": w_out}

def second_block(x, c, w_ada, b_ada, g_norm, w_ffn_up, w_ffn_down, w_in, b_fgate, conv_w,
              conv_b, w_rgate, b_rgate, w_igate, b_igate, lru_lambda, g_qk, g_mix_out, w_out):
    B = x.shape[0]
    c_act = jax.nn.silu(c)
    for l in range(DEPTH):
        mod = (c_act @ w_ada[l] + b_ada[l]).reshape(B, N_SUB, 3, D_MODEL)

        def norm_mod(h, j):
            shift = mod[:, j, 0][:, None, :]
            scale = mod[:, j, 1][:, None, :]
            return _rms(h) * g_norm[l, j] * (1.0 + scale) + shift

        def gate(j):
            return (1.0 + mod[:, j, 2])[:, None, :]

        x = x + 0.5 * gate(0) * _swiglu(norm_mod(x, 0), w_ffn_up[l, 0], w_ffn_down[l, 0])
        x = x + gate(1) * _mixer(norm_mod(x, 1), w_in[l], b_fgate[l], conv_w[l], conv_b[l],
                                 w_rgate[l], b_rgate[l], w_igate[l], b_igate[l],
                                 lru_lambda[l], g_qk[l], g_mix_out[l], w_out[l])
        x = x + 0.5 * gate(2) * _swiglu(norm_mod(x, 2), w_ffn_up[l, 1], w_ffn_down[l, 1])
    return x


def setup_inputs(seed=0):
    out = dict(first_inputs(seed))
    for name, value in second_inputs(seed + 1).items():
        if name != "x":
            out[name + "_2"] = value
    return out


def reference(
    x, w_in, dn_conv, dn_a_log, dn_dt_bias, dn_norm, hg_lb, hg_norm, w_out, g_mix_pre,
    g_mix_post, g_ffn_pre, g_ffn_post, ffn_w_up, ffn_conv, ffn_w_down, c_2, w_ada_2, b_ada_2,
    g_norm_2, w_ffn_up_2, w_ffn_down_2, w_in_2, b_fgate_2, conv_w_2, conv_b_2, w_rgate_2,
    b_rgate_2, w_igate_2, b_igate_2, lru_lambda_2, g_qk_2, g_mix_out_2, w_out_2,
):
    x = first_block(
        x, w_in, dn_conv, dn_a_log, dn_dt_bias, dn_norm, hg_lb, hg_norm, w_out, g_mix_pre,
        g_mix_post, g_ffn_pre, g_ffn_post, ffn_w_up, ffn_conv, ffn_w_down,
    )
    return second_block(
        x, c_2, w_ada_2, b_ada_2, g_norm_2, w_ffn_up_2, w_ffn_down_2, w_in_2, b_fgate_2,
        conv_w_2, conv_b_2, w_rgate_2, b_rgate_2, w_igate_2, b_igate_2, lru_lambda_2, g_qk_2,
        g_mix_out_2, w_out_2,
    )


_drawn_inputs = setup_inputs


def setup_inputs(seed=0):
    import zlib

    import numpy as np

    out = dict(_drawn_inputs(seed))
    spreads = {}
    factors = {'hg_lb': 7.337,
     'hg_norm': 2.996,
     'b_fgate_2': 34.216,
     'conv_b_2': 2.889,
     'b_rgate_2': 57.214,
     'b_igate_2': 32.888,
     'g_qk_2': 3.513}
    for name, (base, spread) in spreads.items():
        noise = np.random.default_rng([zlib.crc32(name.encode()), seed]).standard_normal(out[name].shape)
        drawn = base * np.exp(spread * noise) if base else spread * noise
        out[name] = __import__('jax').numpy.asarray(drawn.astype(out[name].dtype))
    for name, factor in factors.items():
        out[name] = (out[name] * factor).astype(out[name].dtype)
    return out
```

```python
from contextlib import ExitStack, contextmanager

import concourse.bass as bass
from concourse import mybir

F32 = mybir.dt.float32
I32 = mybir.dt.int32
ALU = mybir.AluOpType
ACT = mybir.ActivationFunctionType
AX = mybir.AxisListType.X

P = 128
T = 512
NT = T // P
D = 1024
KD = D // P
DEPTH = 2
C = 64
NC = T // C
F = 2816
NF = F // P
EPS = 1e-6
NEG = -1e30
OUTSIDE = -3.0e38
TAKEN = -3.4e38
TOPK = 128
LEVELS = (1, 2, 4, 8, 16, 32)

DNQ, DNK, DNV, DNZ, DNBA = 0, 512, 1024, 1536, 2048
SAQ, SAK, SAV, SAQI, SAKI, SAWI = 2056, 2312, 2376, 2440, 2696, 2760
HGQ, HGF, HGI, HGG = 2764, 3020, 3276, 3532
LRX, LRG, SBQ, SBK, SBV, FXQ, FXK, FXV, FXF = 0, 512, 1024, 1280, 1536, 1792, 2048, 2304, 2560

FFN_SLOTS = 2 * NF
SLOTS_1 = 16 + 4 + FFN_SLOTS
ADA_SLOTS = 36
SLOTS_2 = ADA_SLOTS + 10 + 4 + 2 * FFN_SLOTS

A_TAP, A_G = 0, 2 * 2 * NF
B_TAP, B_DNC, B_DNN, B_HGN, B_LB = 0, 2 * NF, 2 * NF + 48, 2 * NF + 49, 2 * NF + 50
A2_G, A2_ADA = 0, 24
B2_CW, B2_CB, B2_BR, B2_BI, B2_LAM, B2_GM, B2_QK, B2_C = 0, 16, 20, 24, 28, 32, 40, 42


class Event:

    def __init__(self, nc, ctx, name):
        self.sem = ctx.enter_context(nc.semaphore(name))
        self.name = name
        self.seen = {}

    def restart(self, key):
        self.seen[key] = [0, 0]

    def next(self, eng, n=1):
        at = self.seen.setdefault(id(eng), [0, 0])
        at[1] += n
        eng.wait_ge(self.sem, at[0] + at[1])

    def ring(self, eng, depth):
        at = self.seen.setdefault(id(eng), [0, 0])
        at[1] += 1
        if isinstance(at[0], int) and at[0] + at[1] <= depth:
            return
        eng.wait_ge(self.sem, at[0] + (at[1] - depth))


class Order:

    def __init__(self, eng, event):
        self.eng, self.event = eng, event

    def __call__(self, ins):
        ins.then_inc(self.event.sem, 1)
        self.event.next(self.eng)


@contextmanager
def loop(eng, times, per):
    base = {}
    for e in per:
        at = e.seen.setdefault(id(eng), [0, 0])
        base[e] = at[0] + at[1]
    with eng.Fori(0, times) as i:
        for e, n in per.items():
            e.seen[id(eng)] = [i * n + base[e], 0]
        yield i
        for e, n in per.items():
            assert e.seen[id(eng)][1] == n, (e.name, e.seen[id(eng)][1], n)
    for e, n in per.items():
        e.seen[id(eng)] = [base[e] + times * n, 0]


def program(nc, a, out):
    ctx = ExitStack()
    with ctx:
        def sb(name, *shape, dt=F32):
            return ctx.enter_context(nc.sbuf_tensor(name, list(shape), dt))

        def ev(name):
            return Event(nc, ctx, name)

        ps = ctx.enter_context(nc.psum_tensor("ps", [P, 8, 512], F32))
        xT = sb("xT", P, KD, T)
        hT = sb("hT", P, KD, T)
        wring = sb("wring", P, 2, 2, 8, P)
        sq = sb("sq", P, 4, T)
        std = sb("std", P, T)
        rstd = sb("rstd", P, T)
        ident = sb("ident", P, P)
        ones = sb("ones", P, 512)
        bdones = sb("bdones", P, P)
        bdcausal = sb("bdcausal", P, P)
        level = sb("level", P, 6, P)
        negtri = sb("negtri", P, P)
        negones = sb("negones", P, P)
        strict = sb("strict", P, P)
        causaladd = sb("causaladd", P, T)
        chunkadd = sb("chunkadd", P, P)
        reset = sb("reset", P, T)
        hsel = sb("hsel", 4, 4, P)
        epsc = sb("epsc", P, 1)
        prow = sb("prow", P, 2, 2, 2, P)
        pall = sb("pall", P, 2, 2, 2, P)
        par = sb("par", P, 2, P)
        tiny = sb("tiny", 4, 2, 8)
        head = sb("head", 4, 8)
        lbs = sb("lbs", P, 2, 2)
        lb = sb("lb", P, 2, 2)
        hgw = sb("hgw", P, 16)
        cact = sb("cact", P, 8)
        cs = sb("cs", P, 8)
        wsm = sb("wsm", P, 8, 4)
        arena = sb("arena", P, 31600)

        at = [0]

        def take(*shape):
            n = 1
            for s in shape:
                n *= s
            v = arena[:, at[0]:at[0] + n]
            at[0] += n
            assert at[0] <= 31600, at[0]
            if len(shape) == 1:
                return v
            names = "abcd"[:len(shape)]
            return v.rearrange(f"p ({' '.join(names)}) -> p {' '.join(names)}",
                               **{m: s for m, s in zip(names, shape)})

        actT = arena[:, 0:NF * T].rearrange("p (k t) -> p k t", k=NF)
        at[0] = NF * T
        conv = take(2, 2, T)
        end_ffn = at[0]

        at[0] = 0
        dnT = take(12, T)
        zT = take(4, T)
        saq = take(2, T)
        sak = take(T)
        saqi = take(2, T)
        saki = take(T)
        sav = take(NT, 64)
        sawi = take(NT, 4)
        hgq = take(2, T)
        hgf = take(2, T)
        hgg = take(2, T)
        hgi = take(NT, 256)
        oT = take(8, T)
        bet = take(T)
        gg = take(T)
        mixbase = at[0]
        cbuf = take(2, T)
        lg = take(2, T)
        pr = take(2, T)
        pT = take(2, NT, P)
        mx = take(2, 2)
        sm = take(2, 2)
        rl = take(4, T)
        score = take(3, T)
        m8 = take(2, 8)
        at[0] = mixbase
        take(2, T)
        gtmp = take(T)
        gcol = take(NT, 8)
        egcol = take(NT, 4)
        begcol = take(NT, 4)
        dec = take(NT, P)
        eg = take(T)
        mt = take(NT, P)
        kb = take(NT, P)
        vb = take(NT, P)
        kdc = take(NT)
        kd = take(4, NT, P)
        Tm = take(NT, P)
        Rm = take(NT, P)
        Xm = take(NT, P)
        Cm = take(NT, P)
        egl = take(4, NC)
        u = take(2, 4, P)
        S = take(4, P)
        qkm = hT[:, 4:8, :].rearrange("p h (t c) -> p h t c", t=NT)
        oraw = hT[:, 0:4, :]
        at[0] = mixbase
        hs1 = take(T)
        hk = take(T)
        hb = take(T)
        he = take(T)
        qe = take(T)
        ke = take(T)
        hqd = take(2, T)
        hkd = take(T)
        kdt = take(2, NT, P)
        Ah = take(4, NT, P)
        hS = take(NC, 2, 64)
        hgl = take(2, NC)
        ho = take(2, T)

        at[0] = 0
        uT = take(4, T)
        gT = take(4, T)
        sbq = take(2, T)
        sbk = take(2, T)
        fxq = take(2, T)
        fxk = take(2, T)
        vtok = take(NT, T)
        o2 = take(8, T)
        base2 = at[0]
        take(2, T)
        lg2 = take(2, T)
        pr2 = take(2, T)
        pT2 = take(2, NT, P)
        mx2 = take(2, 2)
        sm2 = take(2, 2)
        Lb = take(NT, T)
        sbt = take(T)
        wsb = take(2, T)
        fF = take(T)
        fneg = take(T)
        fsel = take(4, T)
        ftmp = take(T)
        rt = take(T)
        it = take(T)
        tt = take(T)
        rec = take(T)
        aa = take(T)
        bt = take(T)
        wg = take(2, 4, P)
        mod = take(72)
        coefA = take(3, 8)
        gatec = take(3, 8)
        ada_end = at[0]
        modP = sb("modP", P, 72)
        cA = sb("cA", P, 3, 8)
        cG = sb("cG", P, 3, 8)

        w_loaded = [ev("w_loaded0"), ev("w_loaded1")]
        w_free = ev("w_free")
        slot_open = ev("slot_open")
        x_loaded = ev("x_loaded")
        p_loaded = ev("p_loaded")
        const_ready = ev("const_ready")
        rows_clear = ev("rows_clear")
        xt_done = ev("xt_done")
        xt_copied = ev("xt_copied")
        pt_done = ev("pt_done")
        pt_copied = ev("pt_copied")
        layer_end = ev("layer_end")
        layer_go = ev("layer_go")
        tick = ev("tick")
        out_tr = ev("out_tr")
        out_cp = ev("out_cp")
        out_done = ev("out_done")
        dve_order = ev("dve_order")
        act_order = ev("act_order")
        pool_order = ev("pool_order")
        par_ready = ev("par_ready")
        mm_done = ev("mm_done")
        mm_free = ev("mm_free")
        sq_ready = ev("sq_ready")
        sq_used = ev("sq_used")
        std_done = ev("std_done")
        rec_done = ev("rec_done")
        h_ready = ev("h_ready")
        y_ready = ev("y_ready")
        x_ready = ev("x_ready")
        small_done = ev("small_done")
        small_copied = ev("small_copied")
        conv_done = ev("conv_done")
        silu_done = ev("silu_done")
        act_in = ev("act_in")
        act_gelu = ev("act_gelu")
        act_ready = ev("act_ready")
        down_done = ev("down_done")
        ix_done = ev("ix_done")
        ix_relu = ev("ix_relu")
        ix_used = ev("ix_used")
        lg_done = ev("lg_done")
        lg_max = ev("lg_max")
        at_exp = ev("at_exp")
        at_norm = ev("at_norm")
        at_turn = ev("at_turn")
        at_copied = ev("at_copied")
        at_pv = ev("at_pv")
        at_out = ev("at_out")
        g_in = ev("g_in")
        g_abs = ev("g_abs")
        g_soft = ev("g_soft")
        g_cum = ev("g_cum")
        g_turn = ev("g_turn")
        g_cols = ev("g_cols")
        g_ecol = ev("g_ecol")
        dn_q = ev("dn_q")
        dn_bc = ev("dn_bc")
        dn_sub = ev("dn_sub")
        dn_exp = ev("dn_exp")
        dn_gram = ev("dn_gram")
        dn_bc_used = ev("dn_bc_used")
        dn_turn = ev("dn_turn")
        dn_turned = ev("dn_turned")
        dn_r = ev("dn_r")
        dn_rt = ev("dn_rt")
        dn_t = ev("dn_t")
        dn_c = ev("dn_c")
        dn_x = ev("dn_x")
        dn_xc = ev("dn_xc")
        dn_y = ev("dn_y")
        dn_upd = ev("dn_upd")
        dn_kb = ev("dn_kb")
        dn_u = ev("dn_u")
        rc_ws = ev("rc_ws")
        rc_u = ev("rc_u")
        rc_o = ev("rc_o")
        rc_ds = ev("rc_ds")
        rc_s = ev("rc_s")
        rc_oc = ev("rc_oc")
        hg_sig = ev("hg_sig")
        hg_f = ev("hg_f")
        hg_ln = ev("hg_ln")
        hg_b = ev("hg_b")
        hg_sub = ev("hg_sub")
        hg_exp = ev("hg_exp")
        hg_qk = ev("hg_qk")
        hg_gram = ev("hg_gram")
        hg_pred = ev("hg_pred")
        hg_dec = ev("hg_dec")
        hg_edec = ev("hg_edec")
        hg_kd = ev("hg_kd")
        hg_turn = ev("hg_turn")
        hg_turned = ev("hg_turned")
        hg_ds = ev("hg_ds")
        hg_s = ev("hg_s")
        hg_o = ev("hg_o")
        hg_oc = ev("hg_oc")
        mix_ready = ev("mix_ready")
        c_act = ev("c_act")
        mod_done = ev("mod_done")
        fx_raw = ev("fx_raw")
        g_gelu = ev("g_gelu")
        lr_gates = ev("lr_gates")
        lr_sig = ev("lr_sig")
        lr_tanh = ev("lr_tanh")
        lr_b = ev("lr_b")
        lr_y = ev("lr_y")
        sb_z = ev("sb_z")
        sb_sp = ev("sb_sp")
        sb_l = ev("sb_l")
        sb_p = ev("sb_p")
        sb_min = ev("sb_min")
        sb_exp = ev("sb_exp")
        sb_w = ev("sb_w")
        sb_pv = ev("sb_pv")
        sb_out = ev("sb_out")
        sb_used = ev("sb_used")
        ff_in = ev("ff_in")
        ff_ln = ev("ff_ln")
        ff_sel = ev("ff_sel")
        small2_copied = ev("small2_copied")
        small_loaded = ev("small_loaded")
        scoped = [dve_order, act_order, pool_order, par_ready, mm_done, mm_free, sq_ready, sq_used, std_done,
                  rec_done, h_ready, y_ready, x_ready, small_done, small_copied, conv_done, silu_done,
                  act_in, act_gelu, act_ready, down_done, ix_done, ix_relu, ix_used, lg_done, lg_max, at_exp,
                  at_norm, at_turn, at_copied, at_pv, at_out, g_in, g_abs, g_soft, g_cum, g_turn, g_cols,
                  g_ecol, dn_q, dn_bc, dn_sub, dn_exp, dn_gram, dn_bc_used, dn_turn, dn_turned, dn_r, dn_rt,
                  dn_t, dn_c, dn_x, dn_xc, dn_y, dn_upd, dn_kb, dn_u, rc_ws, rc_u, rc_o, rc_ds, rc_s, rc_oc,
                  hg_sig, hg_f, hg_ln, hg_b, hg_sub, hg_exp, hg_qk, hg_gram, hg_pred, hg_dec, hg_edec, hg_kd,
                  hg_turn, hg_turned, hg_ds, hg_s, hg_o, hg_oc, mix_ready, c_act, mod_done, fx_raw, g_gelu,
                  lr_gates, lr_sig, lr_tanh, lr_b, lr_y, sb_z, sb_sp, sb_l, sb_p, sb_min, sb_exp, sb_w,
                  sb_pv, sb_out, sb_used, ff_in, ff_ln, ff_sel, small2_copied]

        x_in = a["x"]
        ada = a["w_ada_2"].rearrange("l (k p) f -> l p k f", p=P)
        w1 = a["w_in"].rearrange("l (k p) f -> l p k f", p=P)
        wo1 = a["w_out"].rearrange("l (k p) f -> l p k f", p=P)
        up1 = a["ffn_w_up"].rearrange("l (k p) f -> l p k f", p=P)
        dn1 = a["ffn_w_down"]
        w2 = a["w_in_2"].rearrange("l (k p) f -> l p k f", p=P)
        wo2 = a["w_out_2"].rearrange("l (k p) f -> l p k f", p=P)
        up2 = a["w_ffn_up_2"].rearrange("l j (k p) f -> l j p k f", p=P)
        dn2 = a["w_ffn_down_2"]

        block = ctx.enter_context(nc.Block())

        @block.sync
        def _(sp):
            order = [0]

            def begin(l, before, per):
                order[0] = [l * per + before, 0]

            def slot(halves, i=None, per=0):
                base, n = order[0]
                p = n % 2
                pos = base + n if i is None else base + n + i * per
                sp.wait_ge(w_free.sem, pos + 1)
                sp.sem_inc(slot_open.sem, 1)
                for dst, src in halves(p):
                    sp.dma_start(dst, src).then_inc(w_loaded[p].sem, 16)
                order[0][1] += 1

            def cols(src, c0, c1, n=P):
                return lambda p: [(wring[:, p, 0, :, 0:n], src[:, :, c0:c0 + n]),
                                  (wring[:, p, 1, :, 0:n], src[:, :, c1:c1 + n])]

            def ffn(up, down):
                with sp.Fori(0, NF // 2) as i:
                    for j in range(2):
                        slot(lambda p: [(wring[:, p, h, :, :],
                                         up[:, :, bass.ds(i * (2 * P) + (j * P + h * F), P)])
                                        for h in range(2)], i, 2)
                order[0][1] += NF - 2
                with sp.Fori(0, NF // 2) as i:
                    for j in range(2):
                        slot(lambda p: [(wring[:, p, h, 0:4, :].rearrange("p a b -> p (a b)"),
                                         down[bass.ds(i * (2 * P) + j * P, P), h * 512:(h + 1) * 512])
                                        for h in range(2)], i, 2)
                order[0][1] += NF - 2

            def at_layer(src, l):
                return src[bass.ds(l, 1)].rearrange("l p k f -> (l p) k f")

            sp.dma_start(arena[:, 0:NT * D].rearrange("p (n d) -> p n d", n=NT),
                         x_in.rearrange("b (n p) d -> p (b n) d", p=P)).then_inc(x_loaded.sem, 16)
            with sp.Fori(0, DEPTH) as l:
                begin(l, 0, SLOTS_1)
                w = at_layer(w1, l)
                slot(cols(w, SAQ, SAQ + P))
                slot(cols(w, SAQI, SAQI + P))
                slot(cols(w, SAK, SAKI, 64))
                slot(lambda p: [(wring[:, p, 0, :, 0:8], w[:, :, DNBA:DNBA + 8]),
                                (wring[:, p, 1, :, 0:64], w[:, :, SAV:SAV + 64])])
                for c in range(DNQ, DNBA, 2 * P):
                    slot(cols(w, c, c + P))
                for c in (HGQ, HGF, HGG, HGI):
                    slot(cols(w, c, c + P))
                wo = at_layer(wo1, l)
                for c in range(0, D, 2 * P):
                    slot(cols(wo, c, c + P))
                ffn(at_layer(up1, l), dn1[bass.ds(l, 1)].rearrange("l f d -> (l f) d"))
            with sp.Fori(0, DEPTH) as l:
                begin(l, DEPTH * SLOTS_1, SLOTS_2)
                wa = at_layer(ada, l)
                with sp.Fori(0, ADA_SLOTS // 2) as i:
                    for j in range(2):
                        slot(lambda p: [(wring[:, p, h, :, :],
                                         wa[:, :, bass.ds(i * (4 * P) + (2 * j + h) * P, P)])
                                        for h in range(2)], i, 2)
                order[0][1] += ADA_SLOTS - 2
                up = [up2[bass.ds(l, 1), j].rearrange("l p k f -> (l p) k f") for j in range(2)]
                dn = [dn2[bass.ds(l, 1), j].rearrange("l f d -> (l f) d") for j in range(2)]
                ffn(up[0], dn[0])
                w = at_layer(w2, l)
                for c in (SBQ, SBK, FXQ, FXK, LRX, LRX + 2 * P, LRG, LRG + 2 * P, SBV, FXV):
                    slot(cols(w, c, c + P))
                wo = at_layer(wo2, l)
                for c in range(0, D, 2 * P):
                    slot(cols(wo, c, c + P))
                ffn(up[1], dn[1])
            sp.wait_ge(out_cp.sem, 2 * NT)
            sp.dma_start(out.rearrange("b (n p) d -> p (b n) d", p=P),
                         arena[:, 0:NT * D].rearrange("p (n d) -> p n d", n=NT)).then_inc(out_done.sem, 16)
            sp.wait_ge(out_done.sem, 16)

        @block.gpsimd
        def _(g):
            for ap, v in ((prow[:], 0.0), (ident[:], 0.0), (ones[:], 1.0), (bdones[:], 0.0), (level[:], 0.0),
                          (negtri[:], -1.0), (negones[:], -1.0), (strict[:], 1.0), (causaladd[:], 0.0),
                          (chunkadd[:], 0.0), (reset[:], 1.0), (hsel[:], 0.0), (epsc[:], EPS)):
                g.memset(ap, v).then_inc(rows_clear.sem, 1)
            rows_clear.next(g, 13)
            last = []

            def rows(dst, src):
                g.dma_start(dst, src).then_inc(p_loaded.sem, 16)
                last.append(1)

            for l in range(DEPTH):
                A, B = prow[:, 0, l, 0, :], prow[:, 0, l, 1, :]
                fc = a["ffn_conv"][l].rearrange("t (j p) -> (t j) p", p=P)
                rows(A[A_TAP:A_G, :], fc[0:4 * NF, :])
                for n, key in enumerate(("g_mix_pre", "g_mix_post", "g_ffn_pre", "g_ffn_post")):
                    rows(A[A_G + 8 * n:A_G + 8 * n + 8, :], a[key][l].rearrange("(k p) -> k p", p=P))
                rows(B[B_TAP:B_DNC, :], fc[4 * NF:6 * NF, :])
                rows(B[B_DNC:B_DNN, :], a["dn_conv"][l].rearrange("t (j p) -> (t j) p", p=P))
                rows(B[B_DNN:B_DNN + 1, :], a["dn_norm"][l:l + 1, :])
                for h in range(2):
                    rows(B[B_HGN:B_HGN + 1, 64 * h:64 * h + 64], a["hg_norm"][l:l + 1, :])
                rows(B[B_LB:B_LB + 4, :], a["hg_lb"].rearrange("l (j p) -> (l j) p", p=P))
                A, B = prow[:, 1, l, 0, :], prow[:, 1, l, 1, :]
                rows(A[A2_G:A2_G + 24, :], a["g_norm_2"][l].rearrange("j (k p) -> (j k) p", p=P))
                rows(A[A2_ADA:A2_ADA + 72, :], a["b_ada_2"][l].rearrange("(k p) -> k p", p=P))
                rows(B[B2_CW:B2_CW + 16, :], a["conv_w_2"][l].rearrange("t (j p) -> (t j) p", p=P))
                for at_, key in ((B2_CB, "conv_b_2"), (B2_BR, "b_rgate_2"), (B2_BI, "b_igate_2"),
                                 (B2_LAM, "lru_lambda_2"), (B2_GM, "g_mix_out_2")):
                    n = 8 if at_ == B2_GM else 4
                    rows(B[at_:at_ + n, :], a[key][l].rearrange("(k p) -> k p", p=P))
                for h in range(2):
                    rows(B[B2_QK:B2_QK + 2, 64 * h:64 * h + 64], a["g_qk_2"][l])
                rows(B[B2_C:B2_C + 8, :], a["c_2"].rearrange("b (k p) -> (b k) p", p=P))
                rows(tiny[:, l, 0:1], a["dn_a_log"][l].rearrange("(h o) -> h o", o=1))
                rows(tiny[:, l, 1:2], a["dn_dt_bias"][l].rearrange("(h o) -> h o", o=1))
                rows(tiny[:, l, 2:3], a["b_fgate_2"][l].rearrange("(h o) -> h o", o=1))
            g.wait_ge(p_loaded.sem, 16 * len(last))

            def select(v, op, fill, base, ch, pat):
                g.affine_select(out=v, in_=v, compare_op=op, fill=fill, base=base,
                                pattern=pat, channel_multiplier=ch).then_inc(pool_order.sem, 1)
                pool_order.next(g)

            def put(ap, v):
                g.memset(ap, v).then_inc(pool_order.sem, 1)
                pool_order.next(g)

            select(ident[:], ALU.not_equal, 1.0, 0, 1, [[-1, P]])
            for h in range(2):
                put(bdones[64 * h:64 * h + 64, 64 * h:64 * h + 64], 1.0)
            g.tensor_copy(bdcausal[:], bdones[:]).then_inc(pool_order.sem, 1)
            pool_order.next(g)
            select(bdcausal[:], ALU.is_ge, 0.0, 0, -1, [[1, P]])
            for i, L in enumerate(LEVELS):
                n = P // (2 * L)
                v = level[:, i, :].rearrange("p (n o c) -> p n o c", o=2, c=L)[:, :, 1, :]
                put(v, 1.0)
                select(v, ALU.is_ge, 0.0, 0, 1, [[-2 * L, n], [0, L]])
                select(v, ALU.is_ge, 0.0, L - 1, -1, [[2 * L, n], [0, L]])
            select(negtri[:], ALU.is_ge, 0.0, 0, 1, [[-1, P]])
            select(strict[:], ALU.is_gt, 0.0, 0, -1, [[1, P]])
            select(causaladd[:, 384:512], ALU.is_ge, NEG, 0, 1, [[-1, P]])
            put(chunkadd[0:64, 64:128], NEG)
            put(reset[:, :].rearrange("p (n c) -> p n c", c=C)[:, :, 0:1], 0.0)
            for h in range(4):
                select(hsel[:, h, :], ALU.not_equal, 1.0, -h, 1, [[0, P]])
            g.drain().then_inc(const_ready.sem, 1)

            def turn(n):
                g.wait_ge(layer_end.sem, n)
                g.sem_inc(tick.sem, 1)
                g.wait_ge(tick.sem, 1)
                for s in scoped:
                    g.sem_clear(s.sem)
                g.sem_inc(layer_go.sem, 1)

            turn(3)
            with g.Fori(0, DEPTH) as l:
                g.dma_start(wsm[:, :, :], w1[bass.ds(l, 1)].rearrange("l p k f -> (l p) k f")[:, :, SAWI:SAWI + 4])\
                    .then_inc(small_loaded.sem, 16)
                g.wait_ge(small_loaded.sem, l * 16 + 16)
                turn(l * 3 + 6)
            with g.Fori(0, DEPTH) as l:
                g.dma_start(wsm[:, :, :], w2[bass.ds(l, 1)].rearrange("l p k f -> (l p) k f")[:, :, FXF:FXF + 4])\
                    .then_inc(small_loaded.sem, 16)
                for n, key in enumerate(("w_rgate_2", "w_igate_2")):
                    for o in range(2):
                        g.wait_ge(h_ready.sem, 16)
                        src = a[key][bass.ds(l, 1)].rearrange("l (j e) i o -> e i (l j) o", e=2)[o]
                        g.dma_start(wg[64 * o:64 * o + 64, n, :, 64 * o:64 * o + 64], src)\
                            .then_inc(small_loaded.sem, 16)
                g.wait_ge(small_loaded.sem, l * 80 + (16 * DEPTH + 80))
                turn(l * 3 + 12)

        @block.scalar
        def _(s):
            link = Order(s, act_order)
            n_sq = [0]
            n_norm = [0]

            def begin():
                for x in scoped:
                    x.restart(id(s))
                n_sq[0] = n_norm[0] = 0

            def end(go):
                s.drain().then_inc(layer_end.sem, 1)
                s.wait_ge(layer_go.sem, go)

            def norm(srcs, n, before=None):
                for k, src in enumerate(srcs):
                    if before:
                        before(k)
                    if n_sq[0] >= 4:
                        s.wait_ge(sq_used.sem, n_sq[0] - 3)
                    s.activation(sq[:, n_sq[0] % 4, :], src, ACT.Square).then_inc(sq_ready.sem, 1)
                    n_sq[0] += 1
                s.wait_ge(sq_used.sem, n_sq[0])
                if n_norm[0]:
                    s.wait_ge(rec_done.sem, n_norm[0])
                n_norm[0] += 1
                s.activation(std[:, :], ps[:, 7, :], ACT.Sqrt, bias=epsc[:, 0:1], scale=1.0 / n)\
                    .then_inc(std_done.sem, 1)

            def softmax(lgb, prb, mxb, smb, pTb):
                def exp(i):
                    lg_max.next(s)
                    K = (i // 4 + 1) * P
                    s.activation(prb[:, i % 2, 0:K], lgb[:, i % 2, 0:K], ACT.Exp,
                                 bias=mxb[:, i % 2, 1:2], accum_out=smb[:, i % 2, 0:1])\
                        .then_inc(at_exp.sem, 1)

                def copy(i):
                    at_turn.next(s)
                    K = (i // 4 + 1) * P
                    s.activation(pTb[:, i % 2, :, :].rearrange("p a b -> p (a b)")[:, 0:K],
                                 ps[:, 6, 0:K], ACT.Copy).then_inc(at_copied.sem, 1)

                for i in range(17):
                    if i < 16:
                        exp(i)
                    if i >= 1:
                        copy(i - 1)

            def ffn(func):
                with loop(s, NF // 2, {act_in: 2}) as i:
                    for j in range(2):
                        act_in.next(s)
                        s.activation(conv[:, 0, j, :], conv[:, 0, j, :], func).then_inc(act_gelu.sem, 1)

            def gates_softplus(dst, tmp, bias):
                link(s.activation(tmp[0:4, :], dst[0:4, :], ACT.Abs))
                link(s.activation(tmp[0:4, :], tmp[0:4, :], ACT.Exp, scale=-1.0))

            s.wait_ge(const_ready.sem, 1)
            s.wait_ge(pt_copied.sem, 9)
            link(s.activation(hgw[:, 8:12], hgw[:, 4:8], ACT.Exp))
            s.activation(cact[:, :], cs[:, :], ACT.Silu).then_inc(c_act.sem, 1)
            end(1)

            with s.Fori(0, DEPTH) as l:
                begin()
                par_ready.next(s)
                norm([xT[:, k, :] for k in range(KD)], D)
                for j in range(12):
                    conv_done.next(s)
                    s.activation(dnT[:, j, :], cbuf[:, j % 2, :], ACT.Silu).then_inc(silu_done.sem, 1)
                for j in range(4):
                    conv_done.next(s)
                    s.activation(zT[:, j, :], zT[:, j, :], ACT.Silu).then_inc(silu_done.sem, 1)
                for j in range(2):
                    conv_done.next(s)
                    s.activation(hgq[:, j, :], hgq[:, j, :], ACT.Silu).then_inc(silu_done.sem, 1)
                conv_done.next(s, 2)
                for j in range(2):
                    conv_done.next(s)
                    s.activation(hgg[:, j, :], hgg[:, j, :], ACT.Silu).then_inc(silu_done.sem, 1)

                for t in range(1, NT):
                    for h in range(4):
                        ix_done.next(s)
                        if t > 1 and h == 0:
                            ix_used.next(s)
                        s.activation(rl[:, h, 0:(t + 1) * P], ps[:, 4 + h % 2, 0:(t + 1) * P], ACT.Relu)\
                            .then_inc(ix_relu.sem, 1)
                softmax(lg, pr, mx, sm, pT)

                g_in.next(s)
                link(s.activation(head[:, 3:4], head[:, 0:1], ACT.Exp))
                link(s.activation(gtmp[0:4, :], gg[0:4, :], ACT.Abs))
                link(s.activation(gtmp[0:4, :], gtmp[0:4, :], ACT.Exp, scale=-1.0))
                link(s.activation(gtmp[0:4, :], gtmp[0:4, :], ACT.Ln, bias=1.0))
                s.activation(bet[0:4, :], bet[0:4, :], ACT.Sigmoid).then_inc(g_soft.sem, 1)
                g_cols.next(s)
                s.activation(egcol[:, :, :], gcol[:, :, 0:4], ACT.Exp).then_inc(g_ecol.sem, 1)
                for h in range(4):
                    norm([dnT[:, h, :]], 1)
                    norm([dnT[:, 4 + h, :]], 1)
                    dn_sub.next(s)
                    s.activation(eg[:, :], ps[:, 4, :], ACT.Exp).then_inc(dn_exp.sem, 1)
                    s.activation(dec[:, :, :], dec[:, :, :], ACT.Exp).then_inc(dn_exp.sem, 1)
                    for i in range(5):
                        dn_x.next(s)
                        s.activation(Xm[:, :, :].rearrange("p a b -> p (a b)"), ps[:, 4, :], ACT.Copy)\
                            .then_inc(dn_xc.sem, 1)
                for c in range(NC):
                    rc_o.next(s)
                    s.activation(oraw[:, :, c * C:(c + 1) * C],
                                 ps[:, 5 + 2 * (c % 2), 0:256].rearrange("p (h c) -> p h c", h=4),
                                 ACT.Copy).then_inc(rc_oc.sem, 1)
                rc_oc.next(s, NC)
                for h in range(4):
                    norm([oraw[:, h, :]], P)

                for q in range(2):
                    hg_f.next(s)
                    s.activation(hk[:, :], hgf[:, q, :], ACT.Sigmoid, scale=-1.0).then_inc(hg_sig.sem, 1)
                    s.activation(hs1[:, :], hgf[:, q, :], ACT.Sigmoid).then_inc(hg_sig.sem, 1)
                    hg_ln.next(s)
                    s.activation(hs1[:, :], hs1[:, :], ACT.Ln).then_inc(hg_b.sem, 1)
                    for i in range(6):
                        hg_sub.next(s)
                        s.activation(he[:, :], he[:, :], ACT.Exp).then_inc(hg_exp.sem, 1)
                    hg_dec.next(s)
                    link(s.activation(hs1[:, :], hb[:, :], ACT.Exp))
                    s.activation(he[:, :], he[:, :], ACT.Exp).then_inc(hg_edec.sem, 1)
                for q in range(2):
                    hg_oc.next(s)
                    norm([ho[:, q, :]], C)

                norm([hT[:, k, :] for k in range(KD)], D, lambda k: y_ready.next(s))
                norm([xT[:, k, :] for k in range(KD)], D, lambda k: x_ready.next(s))
                ffn(ACT.Gelu_apprx_tanh)
                tiles = [7, 0, 1, 2, 3, 4, 5, 6]
                norm([hT[:, k, :] for k in tiles], D, lambda k: y_ready.next(s))
                end(l + 2)

            with s.Fori(0, DEPTH) as l:
                begin()
                par_ready.next(s)
                norm([xT[:, k, :] for k in range(KD)], D)
                ffn(ACT.Silu)
                norm([xT[:, k, :] for k in range(KD)], D, lambda k: x_ready.next(s))
                for j in range(4):
                    fx_raw.next(s)
                    norm([(fxq if j < 2 else fxk)[:, j % 2, :]], 64)
                for j in range(4):
                    conv_done.next(s)
                    s.activation(gT[:, j, :], gT[:, j, :], ACT.Gelu_apprx_tanh).then_inc(g_gelu.sem, 1)
                link(s.activation(hgw[:, 0:4], par[:, 1, B2_LAM:B2_LAM + 4], ACT.Abs))
                s.activation(hgw[:, 4:8], hgw[:, 0:4], ACT.Exp, scale=-1.0).then_inc(g_abs.sem, 1)
                for j in range(4):
                    lr_gates.next(s)
                    if j:
                        lr_b.next(s)
                    s.activation(rt[:, :], ps[:, 4, :], ACT.Sigmoid, bias=par[:, 1, B2_BR + j:B2_BR + j + 1])\
                        .then_inc(act_order.sem, 1)
                    s.activation(it[:, :], ps[:, 5, :], ACT.Sigmoid, bias=par[:, 1, B2_BI + j:B2_BI + j + 1])\
                        .then_inc(lr_sig.sem, 1)
                    act_order.next(s)
                    g_soft.next(s) if j == 0 else None
                    link(s.activation(tt[:, :], rt[:, :], ACT.Tanh, scale=hgw[:, 12 + j:13 + j]))
                    s.activation(rt[:, :], tt[:, :], ACT.Sqrt).then_inc(lr_tanh.sem, 1)
                lr_y.next(s)
                norm([uT[:, j, :] for j in range(4)], 512)
                for h in range(4):
                    for b in range(NT):
                        N = T - b * P
                        sb_z.next(s)
                        if h or b:
                            sb_l.next(s)
                        link(s.activation(sbt[:, 0:N], ps[:, 4 + b % 2, 0:N], ACT.Abs))
                        link(s.activation(sbt[:, 0:N], sbt[:, 0:N], ACT.Exp, scale=-1.0))
                        s.activation(sbt[:, 0:N], sbt[:, 0:N], ACT.Ln, bias=1.0).then_inc(sb_sp.sem, 1)
                    for b in range(NT):
                        N = T - b * P
                        sb_min.next(s)
                        s.activation(wsb[:, b % 2, 0:N], wsb[:, b % 2, 0:N], ACT.Exp).then_inc(sb_exp.sem, 1)
                sb_out.next(s, 4)
                norm([o2[:, 4 + j, :] for j in range(2)], 256)
                ff_in.next(s)
                link(s.activation(ftmp[0:4, :], fF[0:4, :], ACT.Abs))
                link(s.activation(ftmp[0:4, :], ftmp[0:4, :], ACT.Exp, scale=-1.0))
                s.activation(ftmp[0:4, :], ftmp[0:4, :], ACT.Ln, bias=1.0).then_inc(ff_ln.sem, 1)
                softmax(lg2, pr2, mx2, sm2, pT2)
                at_out.next(s, 16)
                norm([o2[:, 6 + j, :] for j in range(2)], 256)
                norm([xT[:, k, :] for k in range(KD)], D, lambda k: x_ready.next(s))
                ffn(ACT.Silu)
                end(l + 4)

        @block.tensor
        def _(pe):
            order = [None]
            n_mm = [0]
            n_sq = [0]
            n_norm = [0]

            def begin(l, before, per):
                for x in scoped:
                    x.restart(id(pe))
                order[0] = [l * per + before, 0]
                n_mm[0] = n_sq[0] = n_norm[0] = 0

            def end(go):
                pe.drain().then_inc(layer_end.sem, 1)
                pe.wait_ge(layer_go.sem, go)

            def loaded(i=None, per=0):
                base, n = order[0]
                p = n % 2
                pos = base + (n - p) if i is None else base + (n - p) + i * per
                pe.wait_ge(w_loaded[p].sem, pos * 16 + 32)
                order[0][1] += 1
                return p

            def bank():
                mm_free.next(pe)
                b = n_mm[0] % 4
                n_mm[0] += 1
                return b

            def tile(p, half, M=P, src=None):
                b = bank()
                for k in range(KD):
                    m = pe.matmul(ps[0:M, b, :], wring[:, p, half, k, 0:M], (src or hT)[:, k, :],
                                  start=k == 0, stop=k == KD - 1)
                m.then_inc(mm_done.sem, 1)
                return m

            def pair(src=None, M=P):
                p = loaded()
                tile(p, 0, M, src)
                b = bank()
                for k in range(KD):
                    m = pe.matmul(ps[0:M, b, :], wring[:, p, 1, k, 0:M], (src if src is not None else hT)[:, k, :],
                                  start=k == 0, stop=k == KD - 1)
                m.then_inc(mm_done.sem, 1)
                pe.drain().then_inc(w_free.sem, 1)

            def norm(n, lhsT=None):
                for k in range(n):
                    sq_ready.next(pe)
                    if k == 0 and n_norm[0]:
                        pe.wait_ge(std_done.sem, n_norm[0])
                    pe.matmul(ps[:, 7, :], ones[:, 0:P] if lhsT is None else lhsT, sq[:, n_sq[0] % 4, :],
                              start=k == 0, stop=k == n - 1).then_inc(sq_used.sem, 1)
                    n_sq[0] += 1
                n_norm[0] += 1

            def attention(q, k, v, extra=None, mask_first=None):
                def finish(i):
                    t, h = i // 4, i % 4
                    r, prb, pTb = 64 * (h % 2), (pr2 if extra else pr), (pT2 if extra else pT)
                    at_norm.next(pe)
                    if i >= 1:
                        pe.wait_ge(at_copied.sem, i)
                    for kt in range(t + 1):
                        m = pe.transpose(ps[:, 6, kt * P:(kt + 1) * P], prb[:, i % 2, kt * P:(kt + 1) * P], ident[:])
                    m.then_inc(at_turn.sem, 1)
                    at_copied.next(pe)
                    if i >= 1:
                        pe.wait_ge(at_out.sem, i)
                    for kt in range(t + 1):
                        m = pe.matmul(ps[r:r + 64, 7, 0:P], v(kt, h), pTb[:, i % 2, kt, :],
                                      start=kt == 0, stop=kt == t)
                    m.then_inc(at_pv.sem, 1)

                for i in range(17):
                    if i < 16:
                        t, h = i // 4, i % 4
                        r, K = 64 * (h % 2), (t + 1) * P
                        if i >= 2:
                            pe.wait_ge(lg_max.sem, i - 1)
                        m = pe.matmul(ps[:, 4 + i % 2, 0:K], q(h)[r:r + 64, t * P:(t + 1) * P], k(h)[r:r + 64, 0:K],
                                      start=True, stop=extra is None)
                        if extra:
                            pe.matmul(ps[:, 4 + i % 2, 0:K], fsel[0:4, h, t * P:(t + 1) * P], ones[0:4, 0:K],
                                      start=False, stop=False)
                            m = pe.matmul(ps[:, 4 + i % 2, 0:K], hsel[:, h, :], fneg[0:4, 0:K],
                                          start=False, stop=True)
                        m.then_inc(lg_done.sem, 1)
                    if i >= 1:
                        finish(i - 1)

            def ffn():
                with loop(pe, NF // 2, {mm_free: 4}) as i:
                    for j in range(2):
                        p = loaded(i, 2)
                        for half in range(2):
                            b = bank()
                            for k in range(KD):
                                m = pe.matmul(ps[:, b, :], wring[:, p, half, k, :], hT[:, k, :],
                                              start=k == 0, stop=k == KD - 1)
                            m.then_inc(mm_done.sem, 1)
                        pe.drain().then_inc(w_free.sem, 1)
                order[0][1] += NF - 2
                base = mm_free.seen[id(pe)]
                pe.wait_ge(mm_free.sem, base[0] + base[1] + 4)

                def down(i, j, first, last, turns=None):
                    p = loaded(turns, 2)
                    act_ready.next(pe)
                    k = 2 * i + j
                    rhs = actT[:, k, :] if isinstance(k, int) else \
                        arena[:, bass.ds(i * (2 * T) + j * T, T)]
                    for d in range(KD):
                        m = pe.matmul(ps[:, d, :], wring[:, p, d // 4, d % 4, :], rhs, start=first, stop=last)
                        if last:
                            m.then_inc(down_done.sem, 1)
                    pe.drain().then_inc(w_free.sem, 1)

                for j in range(2):
                    down(0, j, j == 0, False)
                with loop(pe, NF // 2 - 2, {act_ready: 2}) as i:
                    for j in range(2):
                        down(i + 1, j, False, False, i)
                order[0][1] += NF - 4 - 2
                for j in range(2):
                    down(NF // 2 - 1, j, False, j == 1)

            pe.sem_inc(w_free.sem, 2)
            pe.wait_ge(const_ready.sem, 1)
            for n in range(8):
                pe.transpose(ps[:, 4 + n % 4, 0:P] if n < 4 else ps[:, 4 + n % 4, P:2 * P],
                             prow[:, n // 4, (n // 2) % 2, n % 2, :], ident[:]).then_inc(pt_done.sem, 1)
            pe.wait_ge(x_loaded.sem, 16)
            xs = arena[:, 0:NT * D].rearrange("p (n d) -> p n d", n=NT)
            for k in range(KD):
                if k >= 4:
                    pe.wait_ge(xt_copied.sem, k - 3)
                for n in range(NT):
                    m = pe.transpose(ps[:, k % 4, n * P:(n + 1) * P], xs[:, n, k * P:(k + 1) * P], ident[:])
                m.then_inc(xt_done.sem, 1)
            end(1)

            with pe.Fori(0, DEPTH) as l:
                begin(l, 0, SLOTS_1)
                norm(KD)
                h_ready.next(pe, KD)
                pair()
                pair()
                pair(M=64)
                p = loaded()
                pe.wait_ge(small_loaded.sem, l * 16 + 16)
                for o in range(2):
                    for k in range(KD):
                        pe.matmul(ps[0:4, 4 + o, :], wring[:, p, 0, k, 4 * o:4 * o + 4], hT[:, k, :],
                                  start=k == 0, stop=k == KD - 1)
                for n in range(NT):
                    for k in range(KD):
                        pe.matmul(ps[:, 6, 68 * n:68 * n + 64], hT[:, k, n * P:(n + 1) * P],
                                  wring[:, p, 1, k, 0:64], start=k == 0, stop=k == KD - 1)
                    for k in range(KD):
                        pe.matmul(ps[:, 6, 68 * n + 64:68 * n + 68], hT[:, k, n * P:(n + 1) * P],
                                  wsm[:, k, :], start=k == 0, stop=k == KD - 1)
                pe.drain().then_inc(w_free.sem, 1)
                pe.sem_inc(small_done.sem, 1)
                for n in range(11):
                    pair()
                p = loaded()
                for n in range(NT):
                    b = bank()
                    for half in range(2):
                        for k in range(KD):
                            m = pe.matmul(ps[:, b, half * P:(half + 1) * P], hT[:, k, n * P:(n + 1) * P],
                                          wring[:, p, half, k, :], start=k == 0, stop=k == KD - 1)
                    m.then_inc(mm_done.sem, 1)
                pe.drain().then_inc(w_free.sem, 1)

                small_copied.next(pe)
                n = 0
                for t in range(1, NT):
                    for h in range(4):
                        if n >= 2:
                            pe.wait_ge(ix_relu.sem, n - 1)
                        n += 1
                        r, K = 64 * (h % 2), (t + 1) * P
                        pe.matmul(ps[:, 4 + h % 2, 0:K], saqi[r:r + 64, h // 2, t * P:(t + 1) * P],
                                  saki[r:r + 64, 0:K], start=True, stop=True).then_inc(ix_done.sem, 1)
                pe.wait_ge(ix_relu.sem, n)
                attention(lambda h: saq[:, h // 2, :], lambda h: sak, lambda kt, h: sav[:, kt, :])

                g_cum.next(pe)
                pe.wait_ge(at_copied.sem, 16)
                for n in range(NT):
                    for o, src in enumerate((gg, bet)):
                        m = pe.matmul(ps[:, 6, 8 * n + 4 * o:8 * n + 4 * o + 4], src[0:4, n * P:(n + 1) * P],
                                      ident[0:4, 0:4], start=True, stop=True)
                m.then_inc(g_turn.sem, 1)
                pe.wait_ge(at_out.sem, 16)
                for h in range(4):
                    q, k, v = dnT[:, h, :], dnT[:, 4 + h, :], dnT[:, 8 + h, :]
                    norm(1)
                    norm(1)
                    if h:
                        dn_u.next(pe)
                    pe.matmul(ps[:, 4, :], hsel[:, h, :], gg[0:4, :], start=True, stop=True)
                    pe.matmul(ps[:, 5, :], hsel[:, h, :], bet[0:4, :], start=True, stop=True).then_inc(dn_bc.sem, 1)
                    dn_q.next(pe)
                    g_cols.next(pe) if h == 0 else None
                    for n in range(NT):
                        m = pe.matmul(ps[:, 6, n * P:(n + 1) * P], k[:, n * P:(n + 1) * P], k[:, n * P:(n + 1) * P],
                                      start=True, stop=True)
                    m.then_inc(dn_gram.sem, 1)
                    pe.wait_ge(std_done.sem, n_norm[0])
                    for n in range(NT):
                        m = pe.matmul(ps[:, 7, n * P:(n + 1) * P], k[:, n * P:(n + 1) * P], q[:, n * P:(n + 1) * P],
                                      start=True, stop=True)
                    m.then_inc(dn_gram.sem, 1)
                    dn_bc_used.next(pe)
                    for n in range(NT):
                        m = pe.transpose(ps[:, 4, n * P:(n + 1) * P], k[:, n * P:(n + 1) * P], ident[:])
                    m.then_inc(dn_turn.sem, 1)
                    for n in range(NT):
                        m = pe.transpose(ps[:, 5, n * P:(n + 1) * P], v[:, n * P:(n + 1) * P], ident[:])
                    m.then_inc(dn_turn.sem, 1)
                    dn_r.next(pe)
                    for n in range(NT):
                        m = pe.transpose(ps[:, 6, n * P:(n + 1) * P], Rm[:, n, :], ident[:])
                    m.then_inc(dn_rt.sem, 1)
                    dn_turned.next(pe)
                    dn_t.next(pe)
                    for i in range(1, 6):
                        dn_c.next(pe)
                        for n in range(NT):
                            m = pe.matmul(ps[:, 4, n * P:(n + 1) * P], Cm[:, n, :], Tm[:, n, :], start=True, stop=True)
                        m.then_inc(dn_x.sem, 1)
                        dn_xc.next(pe)
                        if i < 5:
                            for n in range(NT):
                                m = pe.matmul(ps[:, 5, n * P:(n + 1) * P], Rm[:, n, :], Xm[:, n, :],
                                              start=True, stop=True)
                        for n in range(NT):
                            m = pe.matmul(ps[:, 6, n * P:(n + 1) * P], Xm[:, n, :], Rm[:, n, :],
                                          start=True, stop=True)
                        m.then_inc(dn_y.sem, 1)
                        dn_upd.next(pe)
                    for n in range(NT):
                        pe.matmul(ps[:, 4, n * P:(n + 1) * P], Rm[:, n, :], vb[:, n, :], start=True, stop=True)
                    for n in range(NT):
                        m = pe.matmul(ps[:, 5, n * P:(n + 1) * P], kb[:, n, :], Rm[:, n, :], start=True, stop=True)
                    m.then_inc(dn_kb.sem, 1)
                dn_u.next(pe)
                for c in range(NC):
                    r, n, par_ = C * (c % 2), c // 2, c % 2
                    if c == 0:
                        rc_s.next(pe)
                    for h in range(4):
                        m = pe.matmul(ps[r:r + C, 4, h * P:(h + 1) * P], dnT[:, 4 + h, c * C:(c + 1) * C], S[:, h, :],
                                      start=True, stop=True)
                    m.then_inc(rc_ws.sem, 1)
                    rc_u.next(pe)
                    if c >= 2:
                        pe.wait_ge(rc_oc.sem, c - 1)
                    bo = 5 + 2 * (c % 2)
                    for h in range(4):
                        pe.matmul(ps[:, bo, h * C:(h + 1) * C], S[:, h, :], dnT[:, h, c * C:(c + 1) * C],
                                  start=True, stop=False)
                        m = pe.matmul(ps[:, bo, h * C:(h + 1) * C], u[r:r + C, par_, h, :],
                                      qkm[r:r + C, h, n, r:r + C], start=False, stop=True)
                    m.then_inc(rc_o.sem, 1)
                    for h in range(4):
                        m = pe.matmul(ps[:, 6, h * P:(h + 1) * P], kd[r:r + C, h, n, :], u[r:r + C, par_, h, :],
                                      start=True, stop=True)
                    m.then_inc(rc_ds.sem, 1)
                    rc_s.next(pe)
                pe.wait_ge(rc_oc.sem, NC)
                for h in range(4):
                    norm(1)

                for q in range(2):
                    for i in range(7):
                        hg_qk.next(pe)
                        for h in range(2):
                            g_ = 7 * 2 * q + 2 * i + h
                            if g_ >= 2:
                                pe.wait_ge(hg_pred.sem, g_ - 1)
                            r = 64 * h
                            for n in range(NT):
                                m = pe.matmul(ps[:, 4 + h, n * P:(n + 1) * P], ke[r:r + 64, n * P:(n + 1) * P],
                                              qe[r:r + 64, n * P:(n + 1) * P], start=True, stop=True)
                            m.then_inc(hg_gram.sem, 1)
                    hg_kd.next(pe)
                    for n in range(NT):
                        m = pe.transpose(ps[:, 6, n * P:(n + 1) * P], hkd[:, n * P:(n + 1) * P], ident[:])
                    m.then_inc(hg_turn.sem, 1)
                    hg_turned.next(pe)
                pe.wait_ge(hg_pred.sem, 28)
                for c in range(NC):
                    r, n = C * (c % 2), c // 2
                    for h in range(4):
                        ro, q = 64 * (h % 2), h // 2
                        m = pe.matmul(ps[ro:ro + 64, 4 + c % 2, (c // 2) * P + q * 64:(c // 2) * P + q * 64 + 64],
                                      kdt[r:r + C, q, n, ro:ro + 64], hgi[r:r + C, n, h * 64:h * 64 + 64],
                                      start=True, stop=True)
                m.then_inc(hg_ds.sem, 1)
                hg_s.next(pe)
                for q in range(2):
                    for n in range(NT):
                        for h in (2 * q, 2 * q + 1):
                            r = 64 * (h % 2)
                            pe.matmul(ps[r:r + 64, 4 + q, n * P:(n + 1) * P], hgi[:, n, h * 64:h * 64 + 64],
                                      Ah[:, h, n, :], start=True, stop=False)
                            for c in (2 * n, 2 * n + 1):
                                m = pe.matmul(ps[r:r + 64, 4 + q, c * C:(c + 1) * C], hS[r:r + 64, c, q, :],
                                              hqd[r:r + 64, q, c * C:(c + 1) * C], start=False, stop=c % 2 == 1)
                    m.then_inc(hg_o.sem, 1)
                norm(1, bdones[:])
                norm(1, bdones[:])

                mix_ready.next(pe)
                for n in range(4):
                    pair(src=oT)
                norm(KD)
                norm(KD)
                h_ready.next(pe, KD)
                ffn()
                norm(KD)
                end(l + 2)

            with pe.Fori(0, DEPTH) as l:
                begin(l, DEPTH * SLOTS_1, SLOTS_2)
                with pe.Fori(0, ADA_SLOTS // 2) as i:
                    for j in range(2):
                        p = loaded(i, 2)
                        for half in range(2):
                            for k in range(KD):
                                pe.matmul(ps[:, 4, bass.ds(i * 4 + (2 * j + half), 1)],
                                          wring[:, p, half, k, :], cact[:, k:k + 1],
                                          start=k == 0, stop=k == KD - 1)
                        pe.drain().then_inc(w_free.sem, 1)
                order[0][1] += ADA_SLOTS - 2
                pe.drain().then_inc(mod_done.sem, 1)
                norm(KD)
                h_ready.next(pe, KD)
                ffn()
                norm(KD)
                h_ready.next(pe, KD)
                pair()
                pair()
                pair()
                norm(1, bdones[:])
                norm(1, bdones[:])
                pair()
                norm(1, bdones[:])
                norm(1, bdones[:])
                for n in range(4):
                    pair()
                p, p_ = loaded(), loaded()
                for n in range(NT):
                    b = bank()
                    for s_ in range(2):
                        for half in range(2):
                            for k in range(KD):
                                c0 = (2 * s_ + half) * P
                                m = pe.matmul(ps[:, b, c0:c0 + P], hT[:, k, n * P:(n + 1) * P],
                                              wring[:, (p, p_)[s_], half, k, :], start=k == 0, stop=k == KD - 1)
                    m.then_inc(mm_done.sem, 1)
                pe.drain().then_inc(w_free.sem, 2)
                pe.wait_ge(small_loaded.sem, l * 80 + (16 * DEPTH + 80))
                for k in range(KD):
                    m = pe.matmul(ps[0:4, 4, :], wsm[:, k, :], hT[:, k, :], start=k == 0, stop=k == KD - 1)
                m.then_inc(small_done.sem, 1)
                small2_copied.next(pe)
                for j in range(4):
                    if j:
                        lr_sig.next(pe)
                    pe.matmul(ps[:, 4, :], wg[:, 0, j, :], uT[:, j, :], start=True, stop=True)
                    pe.matmul(ps[:, 5, :], wg[:, 1, j, :], uT[:, j, :], start=True, stop=True)\
                        .then_inc(lr_gates.sem, 1)
                lr_sig.next(pe)
                norm(4)
                pe.wait_ge(std_done.sem, n_norm[0])
                for h in range(4):
                    r, q = 64 * (h % 2), h // 2
                    for b in range(NT):
                        N = T - b * P
                        sb_used.ring(pe, 2)
                        pe.matmul(ps[:, 4 + b % 2, 0:N], sbk[r:r + 64, q, b * P:(b + 1) * P], sbq[r:r + 64, q, b * P:T],
                                  start=True, stop=True).then_inc(sb_z.sem, 1)
                    sb_l.next(pe, NT)
                    for b in range(NT):
                        N = T - b * P
                        sb_min.ring(pe, 1)
                        pe.matmul(ps[:, 6, 0:N], sbk[r:r + 64, q, b * P:(b + 1) * P], sbq[r:r + 64, q, b * P:T],
                                  start=True, stop=False)
                        for j in range(b, NT):
                            m = pe.matmul(ps[:, 6, (j - b) * P:N], negtri[:] if j == b else negones[:],
                                          Lb[:, j, 0:T - j * P], start=False, stop=j == NT - 1)
                        m.then_inc(sb_p.sem, 1)
                        sb_w.next(pe)
                        if b == 0:
                            sb_out.ring(pe, 1)
                        pe.matmul(ps[r:r + 64, 7, b * P:T], vtok[:, b, h * 64:h * 64 + 64], wsb[:, b % 2, 0:N],
                                  start=b == 0, stop=b == NT - 1).then_inc(sb_pv.sem, 1)
                sb_out.ring(pe, 1)
                norm(2)
                ff_sel.next(pe)
                pe.wait_ge(std_done.sem, n_norm[0])
                attention(lambda h: fxq[:, h // 2, :], lambda h: fxk[:, h // 2, :],
                          lambda kt, h: vtok[:, kt, 256 + h * 64:256 + h * 64 + 64], extra=True)
                pe.wait_ge(at_out.sem, 16)
                norm(2)
                mix_ready.next(pe)
                for n in range(4):
                    pair(src=o2)
                norm(KD)
                h_ready.next(pe, KD)
                ffn()
                end(l + 4)

            for n in range(2 * NT):
                if n >= 4:
                    pe.wait_ge(out_cp.sem, n - 3)
                for k in range(4):
                    m = pe.transpose(ps[:, n % 4, k * P:(k + 1) * P],
                                     xT[:, 4 * (n % 2) + k, (n // 2) * P:(n // 2 + 1) * P], ident[:])
                m.then_inc(out_tr.sem, 1)

        @block.vector
        def _(v):
            link = Order(v, dve_order)

            def begin():
                for x in scoped:
                    x.restart(id(v))
                n_mm[0] = 0
                v.sem_inc(mm_free.sem, 4)

            def end(go):
                v.drain().then_inc(layer_end.sem, 1)
                v.wait_ge(layer_go.sem, go)

            def settle():
                v.drain()

            n_mm = [0]

            def filled():
                mm_done.next(v)
                b = n_mm[0] % 4
                n_mm[0] += 1
                return b

            def root():
                v.drain()
                std_done.next(v)
                v.reciprocal(rstd[:, :], std[:, :]).then_inc(rec_done.sem, 1)
                rec_done.next(v)

            def pre_norm(g, shift=None):
                root()
                for k in range(KD):
                    i = v.scalar_tensor_tensor(hT[:, k, :], xT[:, k, :], g(k), rstd[:, :], ALU.mult, ALU.mult)
                    if shift is None:
                        i.then_inc(h_ready.sem, 1)
                if shift is not None:
                    v.drain()
                    for k in range(KD):
                        v.tensor_scalar(hT[:, k, :], hT[:, k, :], shift(k), None, ALU.add).then_inc(h_ready.sem, 1)

            def post_norm(g):
                root()
                for k in range(KD):
                    v.scalar_tensor_tensor(hT[:, k, :], hT[:, k, :], g(k), rstd[:, :], ALU.mult, ALU.mult)
                v.drain()
                for k in range(KD):
                    v.tensor_tensor(xT[:, k, :], xT[:, k, :], hT[:, k, :], ALU.add).then_inc(x_ready.sem, 1)
                v.drain()

            def taps(dst, b, w, n, bias=None):
                if bias is None:
                    link(v.tensor_scalar(dst, ps[:, b, :], w(n - 1), None, ALU.mult))
                else:
                    link(v.tensor_scalar(dst, ps[:, b, :], w(n - 1), bias, ALU.mult, ALU.add))
                for s_ in range(1, n):
                    i = v.scalar_tensor_tensor(dst[:, s_:T], ps[:, b, 0:T - s_], w(n - 1 - s_), dst[:, s_:T],
                                               ALU.mult, ALU.add)
                    if s_ < n - 1:
                        link(i)
                return i

            def free():
                v.drain().then_inc(mm_free.sem, 1)

            def softmax(lgb, prb, mxb, smb, mask, dst):
                def top(i):
                    t, h = i // 4, i % 4
                    K = (t + 1) * P
                    lg_done.next(v)
                    if i >= 2:
                        v.wait_ge(at_exp.sem, i - 1)
                    link(v.tensor_tensor(lgb[:, i % 2, 0:K], ps[:, 4 + i % 2, 0:K], mask(t), ALU.add))
                    link(v.tensor_reduce(mxb[:, i % 2, 0:1], lgb[:, i % 2, 0:K], AX, ALU.max))
                    v.tensor_scalar(mxb[:, i % 2, 1:2], mxb[:, i % 2, 0:1], -1.0, None, ALU.mult)\
                        .then_inc(lg_max.sem, 1)

                def scale(i):
                    K = (i // 4 + 1) * P
                    at_exp.next(v)
                    link(v.reciprocal(smb[:, i % 2, 1:2], smb[:, i % 2, 0:1]))
                    v.tensor_scalar(prb[:, i % 2, 0:K], prb[:, i % 2, 0:K], smb[:, i % 2, 1:2], None, ALU.mult)\
                        .then_inc(at_norm.sem, 1)
                    at_pv.next(v)
                    t, h = i // 4, i % 4
                    r = 64 * (h % 2)
                    v.tensor_copy(dst[r:r + 64, h // 2, t * P:(t + 1) * P], ps[r:r + 64, 7, 0:P])\
                        .then_inc(at_out.sem, 1)

                for i in range(17):
                    if i < 16:
                        top(i)
                    if i >= 1:
                        scale(i - 1)

            def ffn(tap=None):
                def w(i, j, h):
                    def at_(s_):
                        o = (A_TAP + 2 * NF * s_ if s_ < 2 else P + B_TAP) + h * NF + j
                        return par[:, :, :].rearrange("p a b -> p (a b)")[:, bass.ds(i * 2 + o, 1)]
                    return at_

                with loop(v, NF // 2, {mm_done: 4, dve_order: 8 if tap else 0, act_gelu: 2}) as i:
                    for j in range(2):
                        for h in range(2):
                            b = filled()
                            if tap:
                                taps(conv[:, h, j, :], b, w(i, j, h), 3)
                            else:
                                v.tensor_copy(conv[:, h, j, :], ps[:, b, :])
                            free()
                        v.sem_inc(act_in.sem, 1)
                    for j in range(2):
                        act_gelu.next(v)
                        v.tensor_tensor(arena[:, bass.ds(i * (2 * T) + j * T, T)], conv[:, 0, j, :], conv[:, 1, j, :],
                                        ALU.mult).then_inc(act_ready.sem, 1)
                    v.drain()

            for n in range(8):
                v.wait_ge(pt_done.sem, 8)
                src = ps[:, 4 + n % 4, 0:P] if n < 4 else ps[:, 4 + n % 4, P:2 * P]
                v.tensor_copy(pall[:, n // 4, (n // 2) % 2, n % 2, :], src).then_inc(pt_copied.sem, 1)
            v.wait_ge(pt_copied.sem, 8)
            link(v.tensor_copy(hgw[:, 0:4], pall[:, 0, 0, 1, B_LB:B_LB + 4]))
            v.tensor_copy(cs[:, :], pall[:, 1, 0, 1, B2_C:B2_C + 8])
            link(v.tensor_tensor(hgw[:, 12:14], hgw[:, 0:2], hgw[:, 2:4], ALU.max))
            for o in range(2):
                v.tensor_tensor(hgw[:, 4 + 2 * o:6 + 2 * o], hgw[:, 2 * o:2 * o + 2], hgw[:, 12:14], ALU.subtract)
            v.drain().then_inc(pt_copied.sem, 1)
            for k in range(KD):
                v.wait_ge(xt_done.sem, k + 1)
                v.tensor_copy(xT[:, k, :], ps[:, k % 4, :]).then_inc(xt_copied.sem, 1)
            v.wait_ge(c_act.sem, 1)
            link(v.tensor_tensor(hgw[:, 12:14], hgw[:, 8:10], hgw[:, 10:12], ALU.add))
            link(v.reciprocal(hgw[:, 12:14], hgw[:, 12:14]))
            for o in range(2):
                v.tensor_tensor(hgw[:, 4 + 2 * o:6 + 2 * o], hgw[:, 8 + 2 * o:10 + 2 * o], hgw[:, 12:14], ALU.mult)
            v.drain()
            link(v.tensor_tensor(hgw[:, 14:16], hgw[:, 4:6], hgw[:, 6:8], ALU.add))
            v.tensor_tensor(lbs[:, 0, :], hgw[:, 4:6], hgw[:, 4:6], ALU.subtract)
            v.tensor_tensor(lbs[:, 1, :], hgw[:, 14:16], hgw[:, 4:6], ALU.subtract)
            end(1)

            def flat(n):
                return par[:, n // P, n % P:n % P + 1]

            with v.Fori(0, DEPTH) as l:
                begin()
                v.tensor_copy(par[:, :, :], pall[:, 0, bass.ds(l, 1), :, :].rearrange("p o a b -> p (o a) b"))
                v.tensor_copy(lb[:, 0, :], lbs[:, bass.ds(l, 1), :].rearrange("p o a -> p (o a)"))
                v.tensor_copy(head[:, 0:3], tiny[:, bass.ds(l, 1), 0:3].rearrange("p o a -> p (o a)"))
                v.memset(S[:, :, :], 0.0)
                v.drain()
                link(v.tensor_scalar(lb[:, 1, :], lb[:, 0, :], -1.0, 1.0, ALU.mult, ALU.add))
                v.drain().then_inc(par_ready.sem, 1)
                pre_norm(lambda k: par[:, 0, A_G + k:A_G + k + 1])

                for j in range(2):
                    b = filled()
                    v.tensor_scalar(saq[:, j, :], ps[:, b, :], 0.125, None, ALU.mult)
                    free()
                for j in range(2):
                    b = filled()
                    v.tensor_copy(saqi[:, j, :], ps[:, b, :])
                    free()
                for dst in (sak, saki):
                    b = filled()
                    v.tensor_copy(dst[0:64, :], ps[0:64, b, :])
                    v.tensor_copy(dst[64:128, :], ps[0:64, b, :])
                    free()
                small_done.next(v)
                v.tensor_copy(bet[0:4, :], ps[0:4, 4, :])
                v.tensor_scalar(gg[0:4, :], ps[0:4, 5, :], head[:, 1:2], None, ALU.add)
                small = ps[:, 6, 0:4 * 68].rearrange("p (n c) -> p n c", n=NT)
                v.tensor_copy(sav[:, :, :], small[:, :, 0:64])
                v.tensor_scalar(sawi[:, :, :], small[:, :, 64:68], 0.0625, None, ALU.mult)
                for j in range(12):
                    b = filled()
                    if j >= 2:
                        v.wait_ge(silu_done.sem, j - 1)
                    taps(cbuf[:, j % 2, :], b, lambda s_: par[:, 1, B_DNC + 12 * s_ + j:B_DNC + 12 * s_ + j + 1], 4)
                    free()
                    v.sem_inc(conv_done.sem, 1)
                for dst in [zT[:, j, :] for j in range(4)] + [hgq[:, j, :] for j in range(2)] + \
                        [hgf[:, j, :] for j in range(2)] + [hgg[:, j, :] for j in range(2)]:
                    b = filled()
                    v.tensor_copy(dst, ps[:, b, :])
                    free()
                    v.sem_inc(conv_done.sem, 1)
                for n in range(NT):
                    b = filled()
                    v.tensor_copy(hgi[:, n, :], ps[:, b, 0:256])
                    free()
                v.wait_ge(silu_done.sem, 20)
                v.sem_inc(small_copied.sem, 1)

                for t in range(1, NT):
                    K = (t + 1) * P
                    sc = score[:, t - 1, 0:K]
                    ix_relu.next(v, 4)
                    link(v.tensor_scalar(sc, rl[:, 0, 0:K], sawi[:, t, 0:1], None, ALU.mult))
                    for h in range(1, 4):
                        i = v.scalar_tensor_tensor(sc, rl[:, h, 0:K], sawi[:, t, h:h + 1], sc, ALU.mult, ALU.add)
                        link(i)
                    v.sem_inc(ix_used.sem, 1)
                    link(v.memset(score[0:64, t - 1, t * P + 64:K], OUTSIDE))
                    for n in range(TOPK // 8):
                        link(v.max(m8[:, n % 2, :], sc))
                        link(v.match_replace(sc, m8[:, n % 2, :], sc, TAKEN))
                    link(v.tensor_scalar(sc, sc, 0.5 * (TAKEN + OUTSIDE), NEG, ALU.is_gt, ALU.mult))
                softmax(lg, pr, mx, sm, lambda t: score[:, t - 1, 0:(t + 1) * P] if t else chunkadd[:],
                        oT[:, 4:6, :])

                v.sem_inc(g_in.sem, 1)
                g_soft.next(v)
                link(v.tensor_scalar(head[:, 3:4], head[:, 3:4], -1.0, None, ALU.mult))
                link(v.scalar_tensor_tensor(gg[0:4, :], gg[0:4, :], 0.0, gtmp[0:4, :], ALU.max, ALU.add))
                link(v.tensor_scalar(gg[0:4, :], gg[0:4, :], head[:, 3:4], None, ALU.mult))
                v.tensor_tensor_scan(gg[0:4, :], reset[0:4, :], gg[0:4, :], 0.0, ALU.mult, ALU.add)\
                    .then_inc(g_cum.sem, 1)
                g_turn.next(v)
                v.tensor_copy(gcol[:, :, :], ps[:, 6, 0:32].rearrange("p (n c) -> p n c", n=NT))\
                    .then_inc(g_cols.sem, 1)
                g_ecol.next(v)
                g_cols.next(v)
                link(v.tensor_tensor(begcol[:, :, :], egcol[:, :, :], gcol[:, :, 4:8], ALU.mult))
                for h in range(4):
                    q, k, vv = dnT[:, h, :], dnT[:, 4 + h, :], dnT[:, 8 + h, :]
                    root()
                    v.scalar_tensor_tensor(q, q, P ** -0.5, rstd[:, :], ALU.mult, ALU.mult)
                    root()
                    link(v.tensor_tensor(k, k, rstd[:, :], ALU.mult))
                    v.sem_inc(dn_q.sem, 1)
                    dn_bc.next(v)
                    for n in range(NT):
                        v.tensor_scalar(dec[:, n, :], ps[:, 4, n * P:(n + 1) * P], gcol[:, n, h:h + 1], 0.0,
                                        ALU.subtract, ALU.min)
                    v.drain().then_inc(dn_sub.sem, 1)
                    dn_exp.next(v, 2)
                    link(v.tensor_tensor(dec[:, :, :], dec[:, :, :],
                                         bdcausal[:, None, :].broadcast_to([P, NT, P]), ALU.mult))
                    v.tensor_copy(kdc[0:64, :, None], dec[0:64, :, 63:64])
                    v.tensor_copy(kdc[64:128, :, None], dec[64:128, :, 127:128])
                    v.tensor_copy(egl[:, h, :, None], eg[:, :].rearrange("p (n c) -> p n c", c=C)[:, :, C - 1:C])
                    dn_gram.next(v)
                    link(v.tensor_tensor(mt[:, :, :].rearrange("p a b -> p (a b)"), ps[:, 6, :],
                                         dec[:, :, :].rearrange("p a b -> p (a b)"), ALU.mult))
                    link(v.tensor_tensor(mt[:, :, :].rearrange("p a b -> p (a b)"), ps[:, 5, :],
                                         mt[:, :, :].rearrange("p a b -> p (a b)"), ALU.mult))
                    dn_gram.next(v)
                    v.tensor_tensor(qkm[:, h, :, :].rearrange("p a b -> p (a b)"), ps[:, 7, :],
                                    dec[:, :, :].rearrange("p a b -> p (a b)"), ALU.mult)
                    v.drain().then_inc(dn_bc_used.sem, 1)
                    link(v.tensor_tensor(Cm[:, :, :], mt[:, :, :], level[:, 0:1, :].broadcast_to([P, NT, P]), ALU.mult))
                    link(v.tensor_tensor(Rm[:, :, :], ident[:, None, :].broadcast_to([P, NT, P]), Cm[:, :, :],
                                         ALU.subtract))
                    v.sem_inc(dn_r.sem, 1)
                    v.tensor_tensor(q, q, eg[:, :], ALU.mult)
                    dn_turn.next(v)
                    for n in range(NT):
                        v.tensor_scalar(kd[:, h, n, :], ps[:, 4, n * P:(n + 1) * P], kdc[:, n:n + 1], None, ALU.mult)
                        v.tensor_scalar(kb[:, n, :], ps[:, 4, n * P:(n + 1) * P], begcol[:, n, h:h + 1], None, ALU.mult)
                    dn_turn.next(v)
                    for n in range(NT):
                        v.tensor_scalar(vb[:, n, :], ps[:, 5, n * P:(n + 1) * P], gcol[:, n, 4 + h:5 + h], None,
                                        ALU.mult)
                    v.drain().then_inc(dn_turned.sem, 1)
                    dn_rt.next(v)
                    v.tensor_copy(Tm[:, :, :].rearrange("p a b -> p (a b)"), ps[:, 6, :]).then_inc(dn_t.sem, 1)
                    dn_t.next(v)
                    for i in range(1, 6):
                        link(v.tensor_tensor(Cm[:, :, :], mt[:, :, :],
                                             level[:, i:i + 1, :].broadcast_to([P, NT, P]), ALU.mult))
                        v.sem_inc(dn_c.sem, 1)
                        dn_y.next(v)
                        if i < 5:
                            v.tensor_tensor(Tm[:, :, :].rearrange("p a b -> p (a b)"),
                                            Tm[:, :, :].rearrange("p a b -> p (a b)"), ps[:, 5, :], ALU.subtract)
                        v.tensor_tensor(Rm[:, :, :].rearrange("p a b -> p (a b)"),
                                        Rm[:, :, :].rearrange("p a b -> p (a b)"), ps[:, 6, :], ALU.subtract)
                        v.drain().then_inc(dn_upd.sem, 1)
                    dn_kb.next(v)
                    v.tensor_copy(vv, ps[:, 4, :])
                    v.tensor_copy(k, ps[:, 5, :])
                    v.drain().then_inc(dn_u.sem, 1)
                v.sem_inc(rc_s.sem, 1)
                for c in range(NC):
                    r, n, par_ = C * (c % 2), c // 2, c % 2
                    u0 = dnT[r:r + C, 8:12, n * P:(n + 1) * P]
                    rc_ws.next(v)
                    v.tensor_tensor(u[r:r + C, par_, :, :], u0,
                                    ps[r:r + C, 4, :].rearrange("p (h c) -> p h c", h=4), ALU.subtract)\
                        .then_inc(rc_u.sem, 1)
                    rc_ds.next(v)
                    for h in range(4):
                        v.scalar_tensor_tensor(S[:, h, :], S[:, h, :], egl[:, h, c:c + 1],
                                               ps[:, 6, h * P:(h + 1) * P], ALU.mult, ALU.add)
                    v.drain().then_inc(rc_s.sem, 1)
                v.wait_ge(rc_oc.sem, NC)
                for h in range(4):
                    root()
                    link(v.scalar_tensor_tensor(oraw[:, h, :], oraw[:, h, :], par[:, 1, B_DNN:B_DNN + 1], rstd[:, :],
                                                ALU.mult, ALU.mult))
                    v.tensor_tensor(oT[:, h, :], oraw[:, h, :], zT[:, h, :], ALU.mult)
                v.drain()

                v.memset(Ah[:, :, :, :], 0.0)
                v.memset(qe[:, :], 0.0)
                v.memset(ke[:, :], 0.0)
                v.drain()
                for q in range(2):
                    v.sem_inc(hg_f.sem, 1)
                    hg_sig.next(v, 2)
                    v.tensor_scalar(hk[:, :], hk[:, :], lb[:, 1, q:q + 1], None, ALU.mult)
                    link(v.tensor_scalar(hs1[:, :], hs1[:, :], lb[:, 1, q:q + 1], lb[:, 0, q:q + 1], ALU.mult, ALU.add))
                    v.tensor_scalar(hs1[:, :], hs1[:, :], 2.0 ** -63, None, ALU.max).then_inc(hg_ln.sem, 1)
                    hg_b.next(v)
                    link(v.tensor_tensor_scan(hb[:, :], reset[:, :], hs1[:, :], 0.0, ALU.mult, ALU.add))
                    for i, L in enumerate(LEVELS):
                        b4 = hb[:, :].rearrange("p (n o c) -> p n o c", o=2, c=L)
                        e4 = he[:, :].rearrange("p (n o c) -> p n o c", o=2, c=L)
                        ref = b4[:, :, 0, L - 1:L].broadcast_to([P, T // (2 * L), L])
                        v.tensor_tensor(e4[:, :, 1, :], b4[:, :, 1, :], ref, ALU.subtract)
                        v.tensor_tensor(e4[:, :, 0, :], ref, b4[:, :, 0, :], ALU.subtract)
                        v.drain()
                        v.sem_inc(hg_sub.sem, 1)
                        hg_exp.next(v)
                        if q or i:
                            hg_gram.next(v, 2)
                        q4 = qe[:, :].rearrange("p (n o c) -> p n o c", o=2, c=L)
                        k4 = ke[:, :].rearrange("p (n o c) -> p n o c", o=2, c=L)
                        v.tensor_tensor(q4[:, :, 1, :], hgq[:, q, :].rearrange("p (n o c) -> p n o c", o=2, c=L)[:, :, 1, :],
                                        e4[:, :, 1, :], ALU.mult)
                        v.tensor_tensor(k4[:, :, 0, :], hk[:, :].rearrange("p (n o c) -> p n o c", o=2, c=L)[:, :, 0, :],
                                        e4[:, :, 0, :], ALU.mult)
                        v.drain().then_inc(hg_qk.sem, 1)
                        v.wait_ge(hg_gram.sem, 14 * q + 2 * i + 2)
                        for h in range(2):
                            v.copy_predicated(Ah[:, 2 * q + h, :, :].rearrange("p a b -> p a b"),
                                              level[:, i:i + 1, :].bitcast(I32).broadcast_to([P, NT, P]),
                                              ps[:, 4 + h, :].rearrange("p (a b) -> p a b", a=NT))\
                                .then_inc(hg_pred.sem, 1)
                    hg_gram.next(v, 2)
                    v.tensor_copy(qe[:, :], hgq[:, q, :])
                    v.tensor_copy(ke[:, :], hk[:, :])
                    v.drain().then_inc(hg_qk.sem, 1)
                    v.wait_ge(hg_gram.sem, 14 * q + 14)
                    for h in range(2):
                        v.copy_predicated(Ah[:, 2 * q + h, :, :].rearrange("p a b -> p a b"),
                                          ident[:, None, :].bitcast(I32).broadcast_to([P, NT, P]),
                                          ps[:, 4 + h, :].rearrange("p (a b) -> p a b", a=NT))\
                            .then_inc(hg_pred.sem, 1)
                    b3 = hb[:, :].rearrange("p (n c) -> p n c", c=C)
                    v.tensor_tensor(he[:, :].rearrange("p (n c) -> p n c", c=C),
                                    b3[:, :, C - 1:C].broadcast_to([P, NC, C]), b3, ALU.subtract)
                    v.drain().then_inc(hg_dec.sem, 1)
                    hg_edec.next(v)
                    v.tensor_tensor(hqd[:, q, :], hgq[:, q, :], hs1[:, :], ALU.mult)
                    v.tensor_copy(hgl[:, q, :, None], hs1[:, :].rearrange("p (n c) -> p n c", c=C)[:, :, C - 1:C])
                    v.tensor_tensor(hkd[:, :], hk[:, :], he[:, :], ALU.mult).then_inc(hg_kd.sem, 1)
                    hg_turn.next(v)
                    v.tensor_copy(kdt[:, q, :, :].rearrange("p a b -> p (a b)"), ps[:, 6, :])
                    v.drain().then_inc(hg_turned.sem, 1)
                hg_ds.next(v)
                link(v.memset(hS[:, 0, :, :], 0.0))
                for c in range(1, NC):
                    for q in range(2):
                        i = v.scalar_tensor_tensor(
                            hS[:, c, q, :], hS[:, c - 1, q, :], hgl[:, q, c - 1:c],
                            ps[:, 4 + (c - 1) % 2, ((c - 1) // 2) * P + q * 64:((c - 1) // 2) * P + q * 64 + 64],
                            ALU.mult, ALU.add)
                    link(i)
                v.drain().then_inc(hg_s.sem, 1)
                for q in range(2):
                    hg_o.next(v)
                    v.tensor_copy(ho[:, q, :], ps[:, 4 + q, :]).then_inc(hg_oc.sem, 1)
                hg_oc.next(v, 2)
                for q in range(2):
                    root()
                    link(v.scalar_tensor_tensor(ho[:, q, :], ho[:, q, :], par[:, 1, B_HGN:B_HGN + 1], rstd[:, :],
                                                ALU.mult, ALU.mult))
                    v.tensor_tensor(oT[:, 6 + q, :], ho[:, q, :], hgg[:, q, :], ALU.mult)
                v.drain().then_inc(mix_ready.sem, 1)

                for k in range(KD):
                    b = filled()
                    v.tensor_copy(hT[:, k, :], ps[:, b, :])
                    free()
                    v.sem_inc(y_ready.sem, 1)
                post_norm(lambda k: par[:, 0, A_G + 8 + k:A_G + 9 + k])
                pre_norm(lambda k: par[:, 0, A_G + 16 + k:A_G + 17 + k])
                ffn(True)
                for n, k in enumerate((7, 0, 1, 2, 3, 4, 5, 6)):
                    if n == 0:
                        down_done.next(v, 8)
                    v.tensor_copy(hT[:, k, :], ps[:, k, :]).then_inc(y_ready.sem, 1)
                v.drain()
                post_norm(lambda k: par[:, 0, A_G + 24 + k:A_G + 25 + k])
                end(l + 2)

            def gated(src, j, k):
                return v.scalar_tensor_tensor(xT[:, k, :], src, cG[:, j, k:k + 1], xT[:, k, :], ALU.mult, ALU.add)

            with v.Fori(0, DEPTH) as l:
                begin()
                v.tensor_copy(par[:, :, :], pall[:, 1, bass.ds(l, 1), :, :].rearrange("p o a b -> p (o a) b"))
                v.tensor_copy(head[:, 0:3], tiny[:, bass.ds(l, 1), 0:3].rearrange("p o a -> p (o a)"))
                v.drain().then_inc(par_ready.sem, 1)
                mod_done.next(v)
                link(v.tensor_tensor(modP[:, :], ps[:, 4, 0:72], par[:, 0, A2_ADA:A2_ADA + 72], ALU.add))
                m4 = modP[:, :].rearrange("p (j w k) -> p j w k", j=3, w=3)
                v.tensor_scalar(cA[:, :, :], m4[:, :, 1, :], 1.0, None, ALU.add)
                v.tensor_scalar(cG[:, :, :], m4[:, :, 2, :], 1.0, None, ALU.add)
                v.drain()
                v.tensor_tensor(cA[:, :, :], cA[:, :, :],
                                par[:, 0, A2_G:A2_G + 24].rearrange("p (j k) -> p j k", j=3), ALU.mult)
                for j in (0, 2):
                    v.tensor_scalar(cG[:, j, :], cG[:, j, :], 0.5, None, ALU.mult)
                v.drain()

                def mod_norm(j):
                    pre_norm(lambda k: cA[:, j, k:k + 1], lambda k: modP[:, 24 * j + k:24 * j + k + 1])

                mod_norm(0)
                ffn()
                down_done.next(v, 8)
                for k in (7, 0, 1, 2, 3, 4, 5, 6):
                    gated(ps[:, k, :], 0, k)
                v.memset(wg[:, :, :, :], 0.0)
                v.drain()
                for k in range(KD):
                    v.sem_inc(x_ready.sem, 1)
                mod_norm(1)
                for j in range(2):
                    b = filled()
                    v.tensor_scalar(sbq[:, j, :], ps[:, b, :], 0.125, None, ALU.mult)
                    free()
                for j in range(2):
                    b = filled()
                    v.tensor_copy(sbk[:, j, :], ps[:, b, :])
                    free()

                def fx_norm(j):
                    dst = (fxq if j < 2 else fxk)[:, j % 2, :]
                    root()
                    g_ = par[:, 1, B2_QK + j // 2:B2_QK + j // 2 + 1]
                    link(v.scalar_tensor_tensor(dst, dst, g_, rstd[:, :], ALU.mult, ALU.mult))
                    if j < 2:
                        link(v.tensor_scalar(dst, dst, 0.125, None, ALU.mult))

                for m in range(2):
                    for j in range(2):
                        b = filled()
                        v.tensor_copy((fxk if m else fxq)[:, j, :], ps[:, b, :])
                        free()
                    v.sem_inc(fx_raw.sem, 1)
                    fx_norm(2 * m)
                    v.sem_inc(fx_raw.sem, 1)
                    fx_norm(2 * m + 1)
                for j in range(4):
                    b = filled()
                    taps(uT[:, j, :], b, lambda s_: par[:, 1, B2_CW + 4 * s_ + j:B2_CW + 4 * s_ + j + 1], 4,
                         par[:, 1, B2_CB + j:B2_CB + j + 1])
                    free()
                for j in range(4):
                    b = filled()
                    v.tensor_copy(gT[:, j, :], ps[:, b, :])
                    free()
                    v.sem_inc(conv_done.sem, 1)
                for n in range(NT):
                    b = filled()
                    v.tensor_copy(vtok[:, n, :], ps[:, b, :])
                    free()
                small_done.next(v)
                v.tensor_scalar(fF[0:4, :], ps[0:4, 4, :], head[:, 2:3], None, ALU.add)
                v.drain()
                v.sem_inc(small2_copied.sem, 1)

                g_abs.next(v)
                x_, z_, z2, sr = hgw[:, 4:8], hgw[:, 8:12], hgw[:, 0:4], hgw[:, 12:16]
                link(v.tensor_scalar(z_, x_, 2.0, None, ALU.add))
                link(v.reciprocal(z_, z_))
                link(v.tensor_tensor(z_, z_, x_, ALU.mult))
                link(v.tensor_tensor(z2, z_, z_, ALU.mult))
                link(v.tensor_scalar(sr, z2, 1.0 / 15, 1.0 / 13, ALU.mult, ALU.add))
                for o in (11, 9, 7, 5, 3, 1):
                    link(v.tensor_tensor(sr, sr, z2, ALU.mult))
                    link(v.tensor_scalar(sr, sr, 1.0 / o, None, ALU.add))
                link(v.tensor_tensor(sr, sr, z_, ALU.mult))
                link(v.tensor_scalar(z_, par[:, 1, B2_LAM:B2_LAM + 4], -1.0, 0.0, ALU.mult, ALU.max))
                link(v.tensor_scalar(sr, sr, 8.0, None, ALU.mult))
                link(v.scalar_tensor_tensor(sr, z_, 4.0, sr, ALU.mult, ALU.add))
                v.sem_inc(g_soft.sem, 1)
                g_gelu.next(v, 4)
                for j in range(4):
                    lr_tanh.next(v)
                    lr_sig.next(v)
                    link(v.tensor_scalar(rec[:, :], tt[:, :], 1.0, None, ALU.add))
                    link(v.reciprocal(rec[:, :], rec[:, :]))
                    v.tensor_scalar(aa[:, :], rec[:, :], 2.0, -1.0, ALU.mult, ALU.add)
                    link(v.scalar_tensor_tensor(bt[:, :], rt[:, :], 2.0, rec[:, :], ALU.mult, ALU.mult))
                    link(v.tensor_tensor(bt[:, :], bt[:, :], it[:, :], ALU.mult))
                    v.sem_inc(lr_b.sem, 1)
                    link(v.tensor_tensor(bt[:, :], bt[:, :], uT[:, j, :], ALU.mult))
                    link(v.tensor_tensor_scan(rec[:, :], aa[:, :], bt[:, :], 0.0, ALU.mult, ALU.add))
                    link(v.tensor_tensor(uT[:, j, :], rec[:, :], gT[:, j, :], ALU.mult))
                v.sem_inc(lr_y.sem, 1)

                def out_norm(srcs, first):
                    root()
                    for j, src in enumerate(srcs):
                        v.scalar_tensor_tensor(o2[:, first + j, :], src,
                                               par[:, 1, B2_GM + first + j:B2_GM + first + j + 1], rstd[:, :],
                                               ALU.mult, ALU.mult)
                    v.drain()

                out_norm([uT[:, j, :] for j in range(4)], 0)
                for h in range(4):
                    r, q = 64 * (h % 2), h // 2
                    for b in range(NT):
                        N = T - b * P
                        sb_sp.next(v)
                        link(v.scalar_tensor_tensor(Lb[:, b, 0:N], ps[:, 4 + b % 2, 0:N], 0.0, sbt[:, 0:N],
                                                    ALU.max, ALU.add))
                        v.sem_inc(sb_used.sem, 1)
                        v.tensor_tensor(Lb[:, b, 0:P], Lb[:, b, 0:P], strict[:], ALU.mult).then_inc(sb_l.sem, 1)
                    for b in range(NT):
                        N = T - b * P
                        sb_p.next(v)
                        if b >= 2:
                            v.wait_ge(sb_pv.sem, NT * h + b - 1)
                        v.tensor_scalar(wsb[:, b % 2, 0:N], ps[:, 6, 0:N], 0.0, None, ALU.min)\
                            .then_inc(sb_min.sem, 1)
                        sb_exp.next(v)
                        link(v.tensor_tensor(wsb[:, b % 2, 0:P], wsb[:, b % 2, 0:P], strict[:], ALU.mult))
                        v.sem_inc(sb_w.sem, 1)
                    sb_pv.next(v, NT)
                    v.tensor_copy(o2[r:r + 64, 4 + q, :], ps[r:r + 64, 7, :]).then_inc(sb_out.sem, 1)
                sb_out.next(v, 4)
                out_norm([o2[:, 4 + j, :] for j in range(2)], 4)
                v.sem_inc(ff_in.sem, 1)
                ff_ln.next(v)
                link(v.scalar_tensor_tensor(fF[0:4, :], fF[0:4, :], 0.0, ftmp[0:4, :], ALU.min, ALU.subtract))
                link(v.tensor_tensor_scan(fF[0:4, :], ones[0:4, :], fF[0:4, :], 0.0, ALU.mult, ALU.add))
                v.tensor_scalar(fneg[0:4, :], fF[0:4, :], -1.0, None, ALU.mult)
                for h in range(4):
                    v.tensor_scalar(fsel[0:4, h, :], fF[0:4, :], ident[0:4, h:h + 1], None, ALU.mult)
                v.drain().then_inc(ff_sel.sem, 1)
                softmax(lg2, pr2, mx2, sm2, lambda t: causaladd[:, (NT - 1 - t) * P:T], o2[:, 6:8, :])
                v.drain()
                out_norm([o2[:, 6 + j, :] for j in range(2)], 6)
                v.sem_inc(mix_ready.sem, 1)
                for k in range(KD):
                    b = filled()
                    gated(ps[:, b, :], 1, k)
                    free()
                    v.sem_inc(x_ready.sem, 1)
                mod_norm(2)
                ffn()
                down_done.next(v, 8)
                for k in range(KD):
                    gated(ps[:, k, :], 2, k)
                end(l + 4)

            res = arena[:, 0:NT * D].rearrange("p (n d) -> p n d", n=2 * NT)
            for n in range(2 * NT):
                v.wait_ge(out_tr.sem, n + 1)
                v.tensor_copy(res[:, n, :], ps[:, n % 4, :]).then_inc(out_cp.sem, 1)
            v.wait_ge(out_cp.sem, 2 * NT)


_INS = ["x", "w_in", "dn_conv", "dn_a_log", "dn_dt_bias", "dn_norm", "hg_lb", "hg_norm", "w_out", "g_mix_pre",
        "g_mix_post", "g_ffn_pre", "g_ffn_post", "ffn_w_up", "ffn_conv", "ffn_w_down", "c_2", "w_ada_2",
        "b_ada_2", "g_norm_2", "w_ffn_up_2", "w_ffn_down_2", "w_in_2", "b_fgate_2", "conv_w_2", "conv_b_2",
        "w_rgate_2", "b_rgate_2", "w_igate_2", "b_igate_2", "lru_lambda_2", "g_qk_2", "g_mix_out_2", "w_out_2"]


def kernel(**inputs):
    import numpy as _np
    import concourse.bacc as _bacc
    from concourse import mybir as _mybir
    from concourse.bass_utils import run_bass_kernel_spmd as _run

    nc = _bacc.Bacc("TRN2", target_bir_lowering=False, num_devices=1)
    arrays, args = {}, {}
    for name in _INS:
        arr = _np.ascontiguousarray(inputs[name])
        arrays[f"in_{name}"] = arr
        args[name] = nc.dram_tensor(f"in_{name}", arr.shape, _mybir.dt.from_np(arr.dtype), kind="ExternalInput").ap()
    res = nc.dram_tensor("out_x", (1, T, D), _mybir.dt.float32, kind="ExternalOutput").ap()
    program(nc, args, res)
    r = _run(nc, [arrays], core_ids=[0])
    return r.results[0]["out_x"]
```

```python
from contextlib import ExitStack, contextmanager

import concourse.bass as bass
from concourse import mybir

F32 = mybir.dt.float32
F32R = mybir.dt.float32r
I32 = mybir.dt.int32
ALU = mybir.AluOpType
ACT = mybir.ActivationFunctionType
AX = mybir.AxisListType.X

P = 128
T = 512
NT = T // P
D = 1024
KD = D // P
DEPTH = 2
C = 64
NC = T // C
F = 2816
NF = F // P
EPS = 1e-6
NEG = -1e30
OUTSIDE = -3.0e38
TAKEN = -3.4e38
TOPK = 128
LEVELS = (1, 2, 4, 8, 16, 32)

DNQ, DNK, DNV, DNZ, DNBA = 0, 512, 1024, 1536, 2048
SAQ, SAK, SAV, SAQI, SAKI, SAWI = 2056, 2312, 2376, 2440, 2696, 2760
HGQ, HGF, HGI, HGG = 2764, 3020, 3276, 3532
LRX, LRG, SBQ, SBK, SBV, FXQ, FXK, FXV, FXF = 0, 512, 1024, 1280, 1536, 1792, 2048, 2304, 2560

OUT_SLOTS = KD // 2
FFN_SLOTS = 2 * NF
SLOTS_1 = 16 + OUT_SLOTS + FFN_SLOTS
SLOTS_2 = 10 + OUT_SLOTS + 2 * FFN_SLOTS

ADA = 9 * D
ADA_W = 512
NA = ADA // ADA_W
NA_PROJ = 5

PARAM_LOADS = 25

A_TAP, A_G = 0, 2 * 2 * NF
B_TAP, B_DNC, B_DNN, B_HGN, B_LB = 0, 2 * NF, 2 * NF + 48, 2 * NF + 49, 2 * NF + 50
A2_G, A2_ADA = 0, 24
B2_CW, B2_CB, B2_BR, B2_BI, B2_LAM, B2_GM, B2_QK, B2_C = 0, 16, 20, 24, 28, 32, 40, 42


class Event:

    def __init__(self, nc, ctx, name):
        self.sem = ctx.enter_context(nc.semaphore(name))
        self.name = name
        self.seen = {}

    def restart(self, key):
        self.seen[key] = [0, 0]

    def next(self, eng, n=1):
        at = self.seen.setdefault(id(eng), [0, 0])
        at[1] += n
        eng.wait_ge(self.sem, at[0] + at[1])

    def ring(self, eng, depth):
        at = self.seen.setdefault(id(eng), [0, 0])
        at[1] += 1
        if isinstance(at[0], int) and at[0] + at[1] <= depth:
            return
        eng.wait_ge(self.sem, at[0] + (at[1] - depth))


class Order:

    def __init__(self, eng, event):
        self.eng, self.event = eng, event

    def __call__(self, ins):
        ins.then_inc(self.event.sem, 1)
        self.event.next(self.eng)


@contextmanager
def loop(eng, times, per):
    base = {}
    for e in per:
        at = e.seen.setdefault(id(eng), [0, 0])
        base[e] = at[0] + at[1]
    with eng.Fori(0, times) as i:
        for e, n in per.items():
            e.seen[id(eng)] = [i * n + base[e], 0]
        yield i
        for e, n in per.items():
            assert e.seen[id(eng)][1] == n, (e.name, e.seen[id(eng)][1], n)
    for e, n in per.items():
        e.seen[id(eng)] = [base[e] + times * n, 0]


def program(nc, a, out):
    ctx = ExitStack()
    with ctx:
        def sb(name, *shape, dt=F32):
            return ctx.enter_context(nc.sbuf_tensor(name, list(shape), dt))

        def ev(name):
            return Event(nc, ctx, name)

        ps = ctx.enter_context(nc.psum_tensor("ps", [P, 8, 512], F32))
        xT = sb("xT", P, KD, T)
        at_h = (nc.sbuf_base + 31) // 32 * 32
        hT = sb("hT", P, KD, T)
        hh = nc.alloc_sbuf_tensor_at("hh", [P, KD, T], F32R, offset=at_h)
        wring = sb("wring", P, 2, 2, 8, P)
        sq = sb("sq", P, 4, T)
        std = sb("std", P, T)
        rstd = sb("rstd", P, T)
        ident = sb("ident", P, P)
        stair = sb("stair", P, 63)
        ones = sb("ones", P, 512)
        bdones = sb("bdones", P, P)
        bdcausal = sb("bdcausal", P, P)
        level = sb("level", P, 6, P)
        negtri = sb("negtri", P, P)
        negones = sb("negones", P, P)
        strict = sb("strict", P, P)
        causaladd = sb("causaladd", P, T)
        chunkadd = sb("chunkadd", P, P)
        reset = sb("reset", P, T)
        hsel = sb("hsel", 4, 4, P)
        epsc = sb("epsc", P, 1)
        wada = sb("wada", P, 2, ADA_W)
        ada_sum = sb("ada_sum", P, ADA_W)
        mods = sb("mods", P, 2, ADA // P)
        pall = sb("pall", P, 2, 2, 2, P)
        par = sb("par", P, 2, P)
        tiny = sb("tiny", 4, 2, 8)
        head = sb("head", 4, 8)
        lbs = sb("lbs", P, 2, 2)
        lb = sb("lb", P, 2, 2)
        hgw = sb("hgw", P, 16)
        cact = sb("cact", P, 8)
        cs = sb("cs", P, 8)
        wsm = sb("wsm", P, 8, 4)
        wsh = sb("wsh", P, 8, 4, dt=F32R)
        wsl = sb("wsl", P, 8, 4, dt=F32R)
        AN = 30720
        at_a = (nc.sbuf_base + 31) // 32 * 32
        arena = sb("arena", P, AN)

        def rounded(name, at_, *shape):
            return nc.alloc_sbuf_tensor_at(name, [P, *shape], F32R, offset=at_a + 4 * at_)

        ah = rounded("ah", 0, NF * T)
        al = rounded("al", NF * T, NF * T)
        hl = rounded("hl", AN - 2 * KD * T, KD, T)
        wh = rounded("wh", AN - KD * T, 2, 8, P)
        wl = rounded("wl", AN - KD * T // 2, 2, 8, P)
        conv = sq[:, :, :].rearrange("p (h j) t -> p h j t", h=2)

        at = [0]

        def take(*shape):
            n = 1
            for s in shape:
                n *= s
            v = arena[:, at[0]:at[0] + n]
            at[0] += n
            assert at[0] <= AN, at[0]
            if len(shape) == 1:
                return v
            names = "abcd"[:len(shape)]
            return v.rearrange(f"p ({' '.join(names)}) -> p {' '.join(names)}",
                               **{m: s for m, s in zip(names, shape)})

        prow = arena[:, NT * D:NT * D + 8 * P].rearrange("p (b l g c) -> p b l g c", b=2, l=2, g=2)

        at[0] = 0
        dnT = take(12, T)
        zT = take(4, T)
        saq = take(2, T)
        sak = take(T)
        saqi = take(2, T)
        saki = take(T)
        sav = take(NT, 64)
        sawi = take(NT, 4)
        hgq = take(2, T)
        hgf = take(2, T)
        hgg = take(2, T)
        hgi = take(NT, 256)
        oT = take(8, T)
        bet = take(T)
        gg = take(T)
        mixbase = at[0]
        cbuf = take(2, T)
        m8 = take(2, 8)
        lg = take(2, T)
        pr = take(2, T)
        pT = take(2, NT, P)
        mx = take(2, 2)
        sm = take(2, 2)
        rl, score = oT[:, 4:8, :], oT[:, 0:3, :]
        at[0] = mixbase
        take(2, T)
        gtmp = take(T)
        gcol = take(NT, 8)
        egcol = take(NT, 4)
        begcol = take(NT, 4)
        dec = take(NT, P)
        eg = take(T)
        mt = take(NT, P)
        kb = take(NT, P)
        vb = take(NT, P)
        kdc = take(NT)
        kd = take(4, NT, P)
        Tm = take(NT, P)
        Rm = take(NT, P)
        Xm = take(NT, P)
        Cm = [take(NT, P), oT[:, 6, :].rearrange("p (n c) -> p n c", n=NT)]
        egl = take(4, NC)
        u = take(2, 4, P)
        S = take(4, P)
        qkm = hT[:, 4:8, :].rearrange("p h (t c) -> p h t c", t=NT)
        oraw = hT[:, 0:4, :]
        at[0] = mixbase
        hs1 = take(T)
        hk = take(T)
        hb = take(T)
        he = [take(T), dnT[:, 0, :]]
        qe = [take(T), dnT[:, 1, :]]
        ke = [take(T), dnT[:, 2, :]]
        hqd = take(2, T)
        hkd = take(T)
        kdt = take(2, NT, P)
        Ah = take(4, NT, P)
        hS = take(NC, 2, 64)
        hgl = take(2, NC)
        ho = take(2, T)

        at[0] = 0
        uT = take(4, T)
        gT = take(4, T)
        sbq = take(2, T)
        sbk = take(2, T)
        fxq = take(2, T)
        fxk = take(2, T)
        vtok = take(NT, T)
        o2 = take(8, T)
        wg = take(2, 4, P)
        lg2 = take(2, T)
        pr2 = take(2, T)
        pT2 = take(2, NT, P)
        mx2 = take(2, 2)
        sm2 = take(2, 2)
        Lb = take(NT, T)
        sbt = take(NT, T)
        wsb = take(2, T)
        fF = take(T)
        fneg = take(T)
        fsel = take(4, T)
        ftmp = take(T)
        rt = take(T)
        it = take(T)
        tt = take(T)
        rec = take(T)
        aa = take(T)
        bt = take(T)
        modP = sb("modP", P, 72)
        cA = sb("cA", P, 3, 8)
        cG = sb("cG", P, 3, 8)

        w_loaded = [ev("w_loaded0"), ev("w_loaded1")]
        w_free = [ev("w_free0"), ev("w_free1")]
        slot_open = ev("slot_open")
        w_hi = ev("w_hi")
        w_lo = ev("w_lo")
        h_sum = ev("h_sum")
        h_hi = ev("h_hi")
        small_hi = ev("small_hi")
        ada_loaded = [ev("ada_loaded0"), ev("ada_loaded1")]
        ada_open = ev("ada_open")
        ada_ready = ev("ada_ready")
        ada_used = ev("ada_used")
        small_lo = ev("small_lo")
        x_loaded = ev("x_loaded")
        p_loaded = ev("p_loaded")
        const_ready = ev("const_ready")
        rows_clear = ev("rows_clear")
        xt_done = ev("xt_done")
        xt_copied = ev("xt_copied")
        pt_done = ev("pt_done")
        pt_copied = ev("pt_copied")
        layer_end = ev("layer_end")
        layer_go = ev("layer_go")
        tick = ev("tick")
        out_tr = ev("out_tr")
        out_cp = ev("out_cp")
        out_done = ev("out_done")
        dve_order = ev("dve_order")
        act_order = ev("act_order")
        pool_order = ev("pool_order")
        par_ready = ev("par_ready")
        mm_done = ev("mm_done")
        mm_free = ev("mm_free")
        bc_done = ev("bc_done")
        bc_used = ev("bc_used")
        sq_ready = ev("sq_ready")
        sq_used = ev("sq_used")
        std_done = ev("std_done")
        rec_done = ev("rec_done")
        h_ready = ev("h_ready")
        y_ready = ev("y_ready")
        x_ready = ev("x_ready")
        small_done = ev("small_done")
        small_copied = ev("small_copied")
        conv_done = ev("conv_done")
        silu_done = ev("silu_done")
        act_in = ev("act_in")
        act_gelu = ev("act_gelu")
        act_ready = ev("act_ready")
        down_done = ev("down_done")
        ix_go = ev("ix_go")
        ix_done = ev("ix_done")
        ix_relu = ev("ix_relu")
        ix_used = ev("ix_used")
        lg_done = ev("lg_done")
        lg_max = ev("lg_max")
        at_exp = ev("at_exp")
        at_norm = ev("at_norm")
        at_turn = ev("at_turn")
        at_copied = ev("at_copied")
        at_pv = ev("at_pv")
        at_out = ev("at_out")
        g_in = ev("g_in")
        g_abs = ev("g_abs")
        g_soft = ev("g_soft")
        g_cum = ev("g_cum")
        g_turn = ev("g_turn")
        g_cols = ev("g_cols")
        g_ecol = ev("g_ecol")
        dn_q = ev("dn_q")
        dn_bc = ev("dn_bc")
        dn_sub = ev("dn_sub")
        dn_exp = ev("dn_exp")
        dn_gram = ev("dn_gram")
        dn_bc_used = ev("dn_bc_used")
        dn_turn = ev("dn_turn")
        dn_turned = ev("dn_turned")
        dn_r = ev("dn_r")
        dn_rt = ev("dn_rt")
        dn_t = ev("dn_t")
        dn_c = ev("dn_c")
        dn_x = ev("dn_x")
        dn_xc = ev("dn_xc")
        dn_y = ev("dn_y")
        dn_yt = ev("dn_yt")
        dn_updt = ev("dn_updt")
        dn_upd = ev("dn_upd")
        dn_kb = ev("dn_kb")
        dn_u = ev("dn_u")
        rc_ws = ev("rc_ws")
        rc_u = ev("rc_u")
        rc_o = ev("rc_o")
        rc_ds = ev("rc_ds")
        rc_s = ev("rc_s")
        rc_oc = ev("rc_oc")
        hg_sig = ev("hg_sig")
        hg_f = ev("hg_f")
        hg_ln = ev("hg_ln")
        hg_b = ev("hg_b")
        hg_sub = ev("hg_sub")
        hg_exp = ev("hg_exp")
        hg_qk = ev("hg_qk")
        hg_gram = ev("hg_gram")
        hg_pred = ev("hg_pred")
        hg_dec = ev("hg_dec")
        hg_edec = ev("hg_edec")
        hg_kd = ev("hg_kd")
        hg_turn = ev("hg_turn")
        hg_turned = ev("hg_turned")
        hg_ds = ev("hg_ds")
        hg_s = ev("hg_s")
        hg_o = ev("hg_o")
        hg_oc = ev("hg_oc")
        mix_ready = ev("mix_ready")
        c_act = ev("c_act")
        mod_done = ev("mod_done")
        fx_raw = ev("fx_raw")
        g_gelu = ev("g_gelu")
        lr_gates = ev("lr_gates")
        lr_sig = ev("lr_sig")
        lr_tanh = ev("lr_tanh")
        lr_b = ev("lr_b")
        lr_y = ev("lr_y")
        sb_z = ev("sb_z")
        sb_sp = ev("sb_sp")
        sb_l = ev("sb_l")
        sb_p = ev("sb_p")
        sb_min = ev("sb_min")
        sb_exp = ev("sb_exp")
        sb_w = ev("sb_w")
        sb_pv = ev("sb_pv")
        sb_out = ev("sb_out")
        sb_used = ev("sb_used")
        ff_in = ev("ff_in")
        ff_ln = ev("ff_ln")
        ff_sel = ev("ff_sel")
        small2_copied = ev("small2_copied")
        small_loaded = ev("small_loaded")
        scoped = [dn_yt, dn_updt, bc_done, bc_used, ix_go, ada_ready, ada_used, w_hi, w_lo, h_sum, h_hi, small_hi, small_lo,
                  dve_order, act_order, pool_order, par_ready, mm_done, mm_free, sq_ready, sq_used, std_done,
                  rec_done, h_ready, y_ready, x_ready, small_done, small_copied, conv_done, silu_done,
                  act_in, act_gelu, act_ready, down_done, ix_done, ix_relu, ix_used, lg_done, lg_max, at_exp,
                  at_norm, at_turn, at_copied, at_pv, at_out, g_in, g_abs, g_soft, g_cum, g_turn, g_cols,
                  g_ecol, dn_q, dn_bc, dn_sub, dn_exp, dn_gram, dn_bc_used, dn_turn, dn_turned, dn_r, dn_rt,
                  dn_t, dn_c, dn_x, dn_xc, dn_y, dn_upd, dn_kb, dn_u, rc_ws, rc_u, rc_o, rc_ds, rc_s, rc_oc,
                  hg_sig, hg_f, hg_ln, hg_b, hg_sub, hg_exp, hg_qk, hg_gram, hg_pred, hg_dec, hg_edec, hg_kd,
                  hg_turn, hg_turned, hg_ds, hg_s, hg_o, hg_oc, mix_ready, c_act, mod_done, fx_raw, g_gelu,
                  lr_gates, lr_sig, lr_tanh, lr_b, lr_y, sb_z, sb_sp, sb_l, sb_p, sb_min, sb_exp, sb_w,
                  sb_pv, sb_out, sb_used, ff_in, ff_ln, ff_sel, small2_copied]

        x_in = a["x"]
        ada = a["w_ada_2"].rearrange("l (k p) f -> l p k f", p=P)
        w1 = a["w_in"].rearrange("l (k p) f -> l p k f", p=P)
        wo1 = a["w_out"].rearrange("l (k p) f -> l p k f", p=P)
        up1 = a["ffn_w_up"].rearrange("l (k p) f -> l p k f", p=P)
        dn1 = a["ffn_w_down"]
        w2 = a["w_in_2"].rearrange("l (k p) f -> l p k f", p=P)
        wo2 = a["w_out_2"].rearrange("l (k p) f -> l p k f", p=P)
        up2 = a["w_ffn_up_2"].rearrange("l j (k p) f -> l j p k f", p=P)
        dn2 = a["w_ffn_down_2"]

        block = ctx.enter_context(nc.Block())

        @block.sync
        def _(sp):
            place = [0, 0]

            def begin(turns):
                place[:] = [turns, 0]

            def slot(halves, i=None):
                p = place[1] % 2
                turn = place[0] + place[1] // 2
                if i is not None:
                    turn = turn + i
                sp.wait_ge(w_free[p].sem, turn + 1)
                sp.sem_inc(slot_open.sem, 1)
                for dst, src in halves(p):
                    sp.dma_start(dst, src).then_inc(w_loaded[p].sem, 16)
                if len(halves(p)) == 2:
                    sp.sem_inc(w_loaded[p].sem, 16)
                place[1] += 1

            def cols(src, c0, c1, n=P):
                return lambda p: [(wring[:, p, 0, :, 0:n], src[:, :, c0:c0 + n]),
                                  (wring[:, p, 1, :, 0:n], src[:, :, c1:c1 + n])]

            def ffn(up, down):
                with sp.Fori(0, NF // 2) as i:
                    for j in range(2):
                        slot(lambda p: [(wring[:, p, h, :, :],
                                         up[:, :, bass.ds(i * (2 * P) + (j * P + h * F), P)])
                                        for h in range(2)], i)
                place[1] += NF - 2
                with sp.Fori(0, NF // 2) as i:
                    for j in range(2):
                        slot(lambda p: [(wring[:, p, 0, 4 * h:4 * h + 4, :].rearrange("p a b -> p (a b)"),
                                         down[bass.ds(i * (2 * P) + j * P, P), h * 512:(h + 1) * 512])
                                        for h in range(2)], i)
                place[1] += NF - 2

            def at_layer(src, l):
                return src[bass.ds(l, 1)].rearrange("l p k f -> (l p) k f")

            sp.dma_start(arena[:, 0:NT * D].rearrange("p (n d) -> p n d", n=NT),
                         x_in.rearrange("b (n p) d -> p (b n) d", p=P)).then_inc(x_loaded.sem, 16)
            sp.wait_ge(rows_clear.sem, 1)

            def rows(dst, src):
                sp.dma_start(dst, src).then_inc(p_loaded.sem, 16)

            for l in range(DEPTH):
                A, B = prow[:, 0, l, 0, :], prow[:, 0, l, 1, :]
                fc = a["ffn_conv"][l].rearrange("t (j p) -> (t j) p", p=P)
                rows(A[A_TAP:A_G, :], fc[0:4 * NF, :])
                for n, key in enumerate(("g_mix_pre", "g_mix_post", "g_ffn_pre", "g_ffn_post")):
                    rows(A[A_G + 8 * n:A_G + 8 * n + 8, :], a[key][l].rearrange("(k p) -> k p", p=P))
                rows(B[B_TAP:B_DNC, :], fc[4 * NF:6 * NF, :])
                rows(B[B_DNC:B_DNN, :], a["dn_conv"][l].rearrange("t (j p) -> (t j) p", p=P))
                rows(B[B_DNN:B_DNN + 1, :], a["dn_norm"][l:l + 1, :])
                for h in range(2):
                    rows(B[B_HGN:B_HGN + 1, 64 * h:64 * h + 64], a["hg_norm"][l:l + 1, :])
                rows(B[B_LB:B_LB + 4, :], a["hg_lb"].rearrange("l (j p) -> (l j) p", p=P))
                A, B = prow[:, 1, l, 0, :], prow[:, 1, l, 1, :]
                rows(A[A2_G:A2_G + 24, :], a["g_norm_2"][l].rearrange("j (k p) -> (j k) p", p=P))
                rows(A[A2_ADA:A2_ADA + 72, :], a["b_ada_2"][l].rearrange("(k p) -> k p", p=P))
                rows(B[B2_CW:B2_CW + 16, :], a["conv_w_2"][l].rearrange("t (j p) -> (t j) p", p=P))
                for at_, key in ((B2_CB, "conv_b_2"), (B2_BR, "b_rgate_2"), (B2_BI, "b_igate_2"),
                                 (B2_LAM, "lru_lambda_2"), (B2_GM, "g_mix_out_2")):
                    n = 8 if at_ == B2_GM else 4
                    rows(B[at_:at_ + n, :], a[key][l].rearrange("(k p) -> k p", p=P))
                for h in range(2):
                    rows(B[B2_QK:B2_QK + 2, 64 * h:64 * h + 64], a["g_qk_2"][l])
                rows(B[B2_C:B2_C + 8, :], a["c_2"].rearrange("b (k p) -> (b k) p", p=P))
                rows(tiny[:, l, 0:1], a["dn_a_log"][l].rearrange("(h o) -> h o", o=1))
                rows(tiny[:, l, 1:2], a["dn_dt_bias"][l].rearrange("(h o) -> h o", o=1))
                rows(tiny[:, l, 2:3], a["b_fgate_2"][l].rearrange("(h o) -> h o", o=1))

            with sp.Fori(0, DEPTH) as l:
                begin(l * (SLOTS_1 // 2))
                w = at_layer(w1, l)
                slot(cols(w, SAQ, SAQ + P))
                slot(cols(w, SAQI, SAQI + P))
                slot(cols(w, SAK, SAKI, 64))
                slot(lambda p: [(wring[:, p, 0, :, 0:8], w[:, :, DNBA:DNBA + 8]),
                                (wring[:, p, 1, :, 0:64], w[:, :, SAV:SAV + 64]),
                                (wring[:, p, 1, :, 64:68], w[:, :, SAWI:SAWI + 4])])
                for c in range(DNQ, DNBA, 2 * P):
                    slot(cols(w, c, c + P))
                for c in (HGQ, HGF, HGG, HGI):
                    slot(cols(w, c, c + P))
                wo = at_layer(wo1, l)
                for c in range(0, D, 2 * P):
                    slot(cols(wo, c, c + P))
                ffn(at_layer(up1, l), dn1[bass.ds(l, 1)].rearrange("l f d -> (l f) d"))
            with sp.Fori(0, DEPTH) as l:
                begin(l * (SLOTS_2 // 2) + DEPTH * SLOTS_1 // 2)
                up = [up2[bass.ds(l, 1), j].rearrange("l p k f -> (l p) k f") for j in range(2)]
                dn = [dn2[bass.ds(l, 1), j].rearrange("l f d -> (l f) d") for j in range(2)]
                ffn(up[0], dn[0])
                w = at_layer(w2, l)
                for c in (SBQ, SBK, FXQ, FXK, LRX, LRX + 2 * P, LRG, LRG + 2 * P, SBV, FXV):
                    slot(cols(w, c, c + P))
                wo = at_layer(wo2, l)
                for c in range(0, D, 2 * P):
                    slot(cols(wo, c, c + P))
                ffn(up[1], dn[1])
            sp.wait_ge(out_cp.sem, 2 * NT)
            sp.dma_start(out.rearrange("b (n p) d -> p (b n) d", p=P),
                         arena[:, 0:NT * D].rearrange("p (n d) -> p n d", n=NT)).then_inc(out_done.sem, 16)
            sp.wait_ge(out_done.sem, 16)

        @block.gpsimd
        def _(g):
            for ap, v in ((prow[:], 0.0), (ident[:], 0.0), (ones[:], 1.0), (bdones[:], 0.0), (level[:], 0.0),
                          (negtri[:], -1.0), (negones[:], -1.0), (strict[:], 1.0), (causaladd[:], 0.0),
                          (chunkadd[:], 0.0), (reset[:], 1.0), (hsel[:], 0.0), (epsc[:], EPS), (stair[:], 0.0)):
                g.memset(ap, v).then_inc(rows_clear.sem, 1)
            rows_clear.next(g, 14)
            def select(v, op, fill, base, ch, pat):
                g.affine_select(out=v, in_=v, compare_op=op, fill=fill, base=base,
                                pattern=pat, channel_multiplier=ch).then_inc(pool_order.sem, 1)
                pool_order.next(g)

            def put(ap, v):
                g.memset(ap, v).then_inc(pool_order.sem, 1)
                pool_order.next(g)

            select(ident[:], ALU.not_equal, 1.0, 0, 1, [[-1, P]])
            g.sem_inc(const_ready.sem, 1)
            put(stair[:, 31:32], 1.0)
            for h in range(2):
                put(bdones[64 * h:64 * h + 64, 64 * h:64 * h + 64], 1.0)
            g.tensor_copy(bdcausal[:], bdones[:]).then_inc(pool_order.sem, 1)
            pool_order.next(g)
            select(bdcausal[:], ALU.is_ge, 0.0, 0, -1, [[1, P]])
            for i, L in enumerate(LEVELS):
                n = P // (2 * L)
                v = level[:, i, :].rearrange("p (n o c) -> p n o c", o=2, c=L)[:, :, 1, :]
                put(v, 1.0)
                select(v, ALU.is_ge, 0.0, 0, 1, [[-2 * L, n], [0, L]])
                select(v, ALU.is_ge, 0.0, L - 1, -1, [[2 * L, n], [0, L]])
            select(negtri[:], ALU.is_ge, 0.0, 0, 1, [[-1, P]])
            select(strict[:], ALU.is_gt, 0.0, 0, -1, [[1, P]])
            select(causaladd[:, 384:512], ALU.is_ge, NEG, 0, 1, [[-1, P]])
            put(chunkadd[0:64, 64:128], NEG)
            put(reset[:, :].rearrange("p (n c) -> p n c", c=C)[:, :, 0:1], 0.0)
            for h in range(4):
                select(hsel[:, h, :], ALU.not_equal, 1.0, -h, 1, [[0, P]])
            g.drain().then_inc(const_ready.sem, 1)

            def turn(n):
                g.wait_ge(layer_end.sem, n)
                g.sem_inc(tick.sem, 1)
                g.wait_ge(tick.sem, 1)
                for s in scoped:
                    g.sem_clear(s.sem)
                g.sem_inc(layer_go.sem, 1)

            def modulation(l):
                src = ada[bass.ds(l, 1)].rearrange("l p k f -> (l p) k f")

                def load(k, col):
                    g.dma_start(wada[:, k % 2, :], src[:, k, col]).then_inc(ada_loaded[k % 2].sem, 16)

                def block(i, last=False):
                    steps = [i * (2 * KD - 1)]

                    def link(ins):
                        ins.then_inc(pool_order.sem, 1)
                        steps[0] = steps[0] + 1
                        g.wait_ge(pool_order.sem, steps[0])

                    for k in range(KD):
                        if k < KD - 1:
                            load(k + 1, bass.ds(i * ADA_W, ADA_W))
                        elif not last:
                            load(0, bass.ds(i * ADA_W + ADA_W, ADA_W))
                        w, c_ = wada[:, k % 2, :], cact[:, k:k + 1].broadcast_to([P, ADA_W])
                        if k == 0:
                            g.wait_ge(ada_used.sem, i + 1)
                            g.sem_inc(ada_open.sem, 1)
                        g.wait_ge(ada_loaded[k % 2].sem, l * (8 * NA * KD) + i * (8 * KD) + 16 * (k // 2 + 1))
                        link(g.tensor_tensor(w if k else ada_sum[:, :], w, c_, ALU.mult))
                        if k:
                            link(g.tensor_tensor(ada_sum[:, :], ada_sum[:, :], w, ALU.add))
                    g.sem_inc(ada_ready.sem, 1)

                g.sem_inc(ada_used.sem, 1)
                load(0, slice(0, ADA_W))
                with g.Fori(0, NA - 1) as i:
                    block(i)
                block(NA - 1, last=True)

            turn(3)
            with g.Fori(0, DEPTH) as l:
                modulation(l)
                turn(l * 3 + 6)
            with g.Fori(0, DEPTH) as l:
                g.dma_start(wsm[:, :, :], w2[bass.ds(l, 1)].rearrange("l p k f -> (l p) k f")[:, :, FXF:FXF + 4])\
                    .then_inc(small_loaded.sem, 16)
                for n, key in enumerate(("w_rgate_2", "w_igate_2")):
                    for o in range(2):
                        g.wait_ge(h_ready.sem, 16)
                        src = a[key][bass.ds(l, 1)].rearrange("l (j e) i o -> e i (l j) o", e=2)[o]
                        g.dma_start(wg[64 * o:64 * o + 64, n, :, 64 * o:64 * o + 64], src)\
                            .then_inc(small_loaded.sem, 16)
                g.wait_ge(small_loaded.sem, l * 80 + 80)
                turn(l * 3 + 12)

        @block.scalar
        def _(s):
            link = Order(s, act_order)
            n_sq = [0]
            n_norm = [0]

            place = [0, 0, 0]
            n_split = [0]

            def begin(turns):
                for x in scoped:
                    x.restart(id(s))
                mm_done.seen[id(s)][1] = 1
                n_sq[0] = n_norm[0] = 0
                place[:] = [turns, 0, 0]
                n_split[0] = 0

            def split(i=None, whole=False):
                p, half = place[1] % 2, place[2]
                if half == 0:
                    turn = place[0] + place[1] // 2
                    s.wait_ge(w_loaded[p].sem, (turn + 1 if i is None else turn + i + 1) * 48)
                mm_done.ring(s, 2)
                s.activation(wh[:, n_split[0] % 2, :, :], wring[:, p, half, :, :], ACT.Copy).then_inc(w_hi.sem, 1)
                n_split[0] += 1
                place[1] += 1 if half or whole else 0
                place[2] = 0 if half or whole else 1

            def parts(shift=None):
                for k in range(KD):
                    h_sum.next(s)
                    if shift is None:
                        s.activation(hh[:, k, :], sq[:, k % 4, :], ACT.Copy).then_inc(h_hi.sem, 1)
                    else:
                        s.activation(hh[:, k, :], sq[:, k % 4, :], ACT.Identity, bias=shift(k))\
                            .then_inc(h_hi.sem, 1)

            def end(go):
                s.drain().then_inc(layer_end.sem, 1)
                s.wait_ge(layer_go.sem, go)

            def norm(srcs, n, before=None, rows=False):
                for k, src in enumerate(srcs):
                    if before:
                        before(k)
                    if n_sq[0] >= 4:
                        s.wait_ge(sq_used.sem, n_sq[0] - 3)
                    s.activation(sq[:, n_sq[0] % 4, :], src, ACT.Square).then_inc(sq_ready.sem, 1)
                    n_sq[0] += 1
                s.wait_ge(sq_used.sem, n_sq[0])
                if n_norm[0]:
                    s.wait_ge(rec_done.sem, n_norm[0])
                n_norm[0] += 1
                R, N = (NT * len(srcs), P) if rows else (P, T)
                s.activation(std[0:R, 0:N], ps[0:R, 7, 0:N], ACT.Sqrt, bias=epsc[0:R, 0:1], scale=1.0 / n)\
                    .then_inc(std_done.sem, 1)

            def softmax(lgb, prb, mxb, smb, pTb):
                def exp(i):
                    lg_max.next(s)
                    K = (i // 4 + 1) * P
                    s.activation(prb[:, i % 2, 0:K], lgb[:, i % 2, 0:K], ACT.Exp,
                                 bias=mxb[:, i % 2, 1:2], accum_out=smb[:, i % 2, 0:1])\
                        .then_inc(at_exp.sem, 1)

                def copy(i):
                    at_turn.next(s)
                    K = (i // 4 + 1) * P
                    s.activation(pTb[:, i % 2, :, :].rearrange("p a b -> p (a b)")[:, 0:K],
                                 ps[:, 6, 0:K], ACT.Copy).then_inc(at_copied.sem, 1)

                for i in range(17):
                    if i < 16:
                        exp(i)
                    if i >= 1:
                        copy(i - 1)

            def ffn(func):
                with loop(s, NF // 2, {act_in: 2, mm_done: 4}) as i:
                    split(i)
                    split(i)
                    split(i)
                    act_in.next(s)
                    s.activation(conv[:, 0, 0, :], conv[:, 0, 0, :], func).then_inc(act_gelu.sem, 1)
                    split(i)
                    act_in.next(s)
                    s.activation(conv[:, 0, 1, :], conv[:, 0, 1, :], func).then_inc(act_gelu.sem, 1)
                place[1] += NF - 2 + 1
                place[2] = 0
                with loop(s, NF // 2 - 1, {mm_done: 2}) as i:
                    split(i, whole=True)
                    split(i, whole=True)
                place[1] += NF - 2 - 2
                split(whole=True)

            def gates_softplus(dst, tmp, bias):
                link(s.activation(tmp[0:4, :], dst[0:4, :], ACT.Abs))
                link(s.activation(tmp[0:4, :], tmp[0:4, :], ACT.Exp, scale=-1.0))

            s.wait_ge(const_ready.sem, 2)
            s.wait_ge(pt_copied.sem, 9)
            link(s.activation(hgw[:, 8:12], hgw[:, 4:8], ACT.Exp))
            s.activation(cact[:, :], cs[:, :], ACT.Silu).then_inc(c_act.sem, 1)
            end(1)

            with s.Fori(0, DEPTH) as l:
                begin(l * (SLOTS_1 // 2))
                split()
                par_ready.next(s)
                norm([xT[:, k, :] for k in range(KD)], D)
                parts()
                for j in range(9):
                    split()
                def relu(j):
                    if 0 <= j < 12:
                        ix_done.next(s)
                        if j and j % 4 == 0:
                            ix_used.next(s)
                        K = (j // 4 + 2) * P
                        s.activation(rl[:, j % 4, 0:K], ps[:, 4 + 2 * (j % 2), 0:K], ACT.Relu)\
                            .then_inc(ix_relu.sem, 1)

                for j in range(12):
                    split()
                    conv_done.next(s)
                    s.activation(dnT[:, j, :], cbuf[:, j % 2, :], ACT.Silu).then_inc(silu_done.sem, 1)
                    relu(j - 2)
                for j in range(4):
                    split()
                    conv_done.next(s)
                    s.activation(zT[:, j, :], zT[:, j, :], ACT.Silu).then_inc(silu_done.sem, 1)
                    relu(j + 10)
                for j in range(2):
                    split()
                    conv_done.next(s)
                    s.activation(hgq[:, j, :], hgq[:, j, :], ACT.Silu).then_inc(silu_done.sem, 1)
                for j in range(2):
                    split()
                conv_done.next(s, 2)
                for j in range(2):
                    split()
                    conv_done.next(s)
                    s.activation(hgg[:, j, :], hgg[:, j, :], ACT.Silu).then_inc(silu_done.sem, 1)

                softmax(lg, pr, mx, sm, pT)

                g_in.next(s)
                link(s.activation(head[:, 3:4], head[:, 0:1], ACT.Exp))
                link(s.activation(gtmp[0:4, :], gg[0:4, :], ACT.Abs))
                link(s.activation(gtmp[0:4, :], gtmp[0:4, :], ACT.Exp, scale=-1.0))
                link(s.activation(gtmp[0:4, :], gtmp[0:4, :], ACT.Ln, bias=1.0))
                s.activation(bet[0:4, :], bet[0:4, :], ACT.Sigmoid).then_inc(g_soft.sem, 1)
                g_cols.next(s)
                s.activation(egcol[:, :, :], gcol[:, :, 0:4], ACT.Exp).then_inc(g_ecol.sem, 1)
                norm([dnT[:, j, :] for j in range(8)], 1, rows=True)
                for h in range(4):
                    dn_sub.next(s)
                    s.activation(eg[:, :], ps[:, 4, :], ACT.Exp).then_inc(dn_exp.sem, 1)
                    s.activation(dec[:, :, :], dec[:, :, :], ACT.Exp).then_inc(dn_exp.sem, 1)
                    for i in range(5):
                        dn_x.next(s)
                        s.activation(Xm[:, :, :].rearrange("p a b -> p (a b)"), ps[:, 4, :], ACT.Copy)\
                            .then_inc(dn_xc.sem, 1)
                for c in range(NC):
                    rc_o.next(s)
                    s.activation(oraw[:, :, c * C:(c + 1) * C],
                                 ps[:, 5 + 2 * (c % 2), 0:256].rearrange("p (h c) -> p h c", h=4),
                                 ACT.Copy).then_inc(rc_oc.sem, 1)
                rc_oc.next(s, NC)
                norm([oraw[:, h, :] for h in range(4)], P, rows=True)

                for q in range(2):
                    hg_f.next(s)
                    s.activation(hk[:, :], hgf[:, q, :], ACT.Sigmoid, scale=-1.0).then_inc(hg_sig.sem, 1)
                    s.activation(hs1[:, :], hgf[:, q, :], ACT.Sigmoid).then_inc(hg_sig.sem, 1)
                    hg_ln.next(s)
                    s.activation(hs1[:, :], hs1[:, :], ACT.Ln).then_inc(hg_b.sem, 1)
                    for i in range(6):
                        hg_sub.next(s)
                        e = he[(7 * q + i) % 2]
                        s.activation(e, e, ACT.Exp).then_inc(hg_exp.sem, 1)
                    hg_dec.next(s)
                    link(s.activation(hs1[:, :], hb[:, :], ACT.Exp))
                    s.activation(he[q], he[q], ACT.Exp).then_inc(hg_edec.sem, 1)
                for q in range(2):
                    hg_oc.next(s)
                    norm([ho[:, q, :]], C)

                norm([hT[:, k, :] for k in range(KD)], D, lambda k: y_ready.next(s))
                place[1] += OUT_SLOTS
                mm_done.seen[id(s)][1] += KD
                split()
                norm([xT[:, k, :] for k in range(KD)], D, lambda k: x_ready.next(s))
                parts()
                ffn(ACT.Gelu_apprx_tanh)
                tiles = [7, 0, 1, 2, 3, 4, 5, 6]
                norm([hT[:, k, :] for k in tiles], D, lambda k: y_ready.next(s))
                end(l + 2)

            with s.Fori(0, DEPTH) as l:
                begin(l * (SLOTS_2 // 2) + DEPTH * SLOTS_1 // 2)
                split()
                par_ready.next(s)
                norm([xT[:, k, :] for k in range(KD)], D)
                parts(lambda k: modP[:, k:k + 1])
                ffn(ACT.Silu)
                s.wait_ge(small_loaded.sem, l * 80 + 16)
                s.activation(wsh[:, :, :], wsm[:, :, :], ACT.Copy).then_inc(small_hi.sem, 1)
                norm([xT[:, k, :] for k in range(KD)], D, lambda k: x_ready.next(s))
                split()
                parts(lambda k: modP[:, 24 + k:25 + k])
                for j in range(7):
                    split()
                for j in range(4):
                    if j == 2:
                        split()
                        split()
                    fx_raw.next(s)
                    norm([(fxq if j < 2 else fxk)[:, j % 2, :]], 64)
                for j in range(4):
                    split()
                for j in range(4):
                    split()
                    conv_done.next(s)
                    s.activation(gT[:, j, :], gT[:, j, :], ACT.Gelu_apprx_tanh).then_inc(g_gelu.sem, 1)
                for j in range(2):
                    split()
                link(s.activation(hgw[:, 0:4], par[:, 1, B2_LAM:B2_LAM + 4], ACT.Abs))
                s.activation(hgw[:, 4:8], hgw[:, 0:4], ACT.Exp, scale=-1.0).then_inc(g_abs.sem, 1)
                for j in range(4):
                    lr_gates.next(s)
                    if j:
                        lr_b.next(s)
                    s.activation(rt[:, :], ps[:, 4, :], ACT.Sigmoid, bias=par[:, 1, B2_BR + j:B2_BR + j + 1])\
                        .then_inc(act_order.sem, 1)
                    s.activation(it[:, :], ps[:, 5, :], ACT.Sigmoid, bias=par[:, 1, B2_BI + j:B2_BI + j + 1])\
                        .then_inc(lr_sig.sem, 1)
                    act_order.next(s)
                    g_soft.next(s) if j == 0 else None
                    link(s.activation(tt[:, :], rt[:, :], ACT.Tanh, scale=hgw[:, 12 + j:13 + j]))
                    s.activation(rt[:, :], tt[:, :], ACT.Sqrt).then_inc(lr_tanh.sem, 1)
                lr_y.next(s)
                norm([uT[:, j, :] for j in range(4)], 512)
                for h in range(4):
                    if h:
                        sb_l.next(s, NT)
                    for b in range(NT):
                        N = T - b * P
                        sb_z.next(s)
                        link(s.activation(sbt[:, b, 0:N], ps[:, b, 0:N], ACT.Abs))
                        link(s.activation(sbt[:, b, 0:N], sbt[:, b, 0:N], ACT.Exp, scale=-1.0))
                    for b in range(NT):
                        N = T - b * P
                        s.activation(sbt[:, b, 0:N], sbt[:, b, 0:N], ACT.Ln, bias=1.0).then_inc(sb_sp.sem, 1)
                    for b in range(NT):
                        N = T - b * P
                        sb_min.next(s)
                        s.activation(wsb[:, b % 2, 0:N], wsb[:, b % 2, 0:N], ACT.Exp).then_inc(sb_exp.sem, 1)
                sb_out.next(s, 4)
                norm([o2[:, 4 + j, :] for j in range(2)], 256)
                ff_in.next(s)
                link(s.activation(ftmp[0:4, :], fF[0:4, :], ACT.Abs))
                link(s.activation(ftmp[0:4, :], ftmp[0:4, :], ACT.Exp, scale=-1.0))
                s.activation(ftmp[0:4, :], ftmp[0:4, :], ACT.Ln, bias=1.0).then_inc(ff_ln.sem, 1)
                softmax(lg2, pr2, mx2, sm2, pT2)
                at_out.next(s, 16)
                norm([o2[:, 6 + j, :] for j in range(2)], 256)
                place[1] += OUT_SLOTS
                mm_done.seen[id(s)][1] += KD
                split()
                norm([xT[:, k, :] for k in range(KD)], D, lambda k: x_ready.next(s))
                parts(lambda k: modP[:, 48 + k:49 + k])
                ffn(ACT.Silu)
                end(l + 4)

        @block.tensor
        def _(pe):
            place = [0, 0]
            n_split = [0]
            n_mm = [0]
            n_sq = [0]
            n_norm = [0]

            def begin(turns):
                for x in scoped:
                    x.restart(id(pe))
                place[:] = [turns, 0]
                n_split[0] = n_mm[0] = n_sq[0] = n_norm[0] = n_mod[0] = 0
                pe.sem_inc(mm_done.sem, 1)

            def end(go):
                pe.drain().then_inc(layer_end.sem, 1)
                pe.wait_ge(layer_go.sem, go)

            def loaded(i=None):
                p = place[1] % 2
                turn = place[0] + place[1] // 2
                pe.wait_ge(w_loaded[p].sem, (turn + 1 if i is None else turn + i + 1) * 48)
                place[1] += 1
                return p

            def parts_ready():
                w_lo.next(pe)
                n_split[0] += 1
                return (n_split[0] - 1) % 2

            def product(dst, w, h, wlo, hlo, first=True, last=True):
                pe.matmul(dst, w, h, start=first, stop=False)
                pe.matmul(dst, w, hlo, start=False, stop=False)
                return pe.matmul(dst, wlo, h, start=False, stop=last)

            def bank():
                mm_free.next(pe)
                b = n_mm[0] % 4
                n_mm[0] += 1
                return b

            def tile(M=P, first=False, beside=None):
                w, b = parts_ready(), bank()
                for c, b_ in [(0, b)] if beside is None else [(M, beside), (0, b)]:
                    for k in range(KD):
                        if first:
                            h_ready.next(pe)
                        m = product(ps[0:M, b_, :], wh[:, w, k, c:c + M], hh[:, k, :],
                                    wl[:, w, k, c:c + M], hl[:, k, :], k == 0, k == KD - 1)
                m.then_inc(mm_done.sem, 1)

            def token_tile(N):
                w, b = parts_ready(), bank()
                for n in range(NT):
                    for k in range(KD):
                        m = product(ps[:, b, N * n:N * n + N], hh[:, k, n * P:(n + 1) * P], wh[:, w, k, 0:N],
                                    hl[:, k, n * P:(n + 1) * P], wl[:, w, k, 0:N], k == 0, k == KD - 1)
                m.then_inc(mm_done.sem, 1)

            def out_pair(src):
                p = loaded()
                for half in range(2):
                    b = bank()
                    for k in range(KD):
                        m = pe.matmul(ps[:, b, :], wring[:, p, half, k, :], src[:, k, :],
                                      start=k == 0, stop=k == KD - 1)
                    m.then_inc(mm_done.sem, 1)
                pe.drain().then_inc(w_free[p].sem, 1)

            def norm(n, lhsT=None):
                for k in range(n):
                    sq_ready.next(pe)
                    if k == 0 and n_norm[0]:
                        pe.wait_ge(std_done.sem, n_norm[0])
                    pe.matmul(ps[:, 7, :], ones[:, 0:P] if lhsT is None else lhsT, sq[:, n_sq[0] % 4, :],
                              start=k == 0, stop=k == n - 1).then_inc(sq_used.sem, 1)
                    n_sq[0] += 1
                n_norm[0] += 1

            def row_norms(n):
                R = NT * n
                for m in range(n):
                    sq_ready.next(pe)
                    if m == 0 and n_norm[0]:
                        pe.wait_ge(std_done.sem, n_norm[0])
                    for t in range(NT):
                        j = NT * m + t
                        i = pe.matmul(ps[0:R, 7, 0:P], stair[:, 31 - j:31 - j + R],
                                      sq[:, n_sq[0] % 4, t * P:(t + 1) * P], start=j == 0, stop=j == R - 1)
                    i.then_inc(sq_used.sem, 1)
                    n_sq[0] += 1
                n_norm[0] += 1
                pe.wait_ge(rec_done.sem, n_norm[0])
                for m in range(n):
                    bc_used.ring(pe, 3)
                    for t in range(NT):
                        j = NT * m + t
                        i = pe.matmul(ps[:, 1 + m % 3, t * P:(t + 1) * P], ident[0:R, j:j + 1].broadcast_to([R, P]),
                                      rstd[0:R, 0:P], start=True, stop=True)
                    i.then_inc(bc_done.sem, 1)

            def attention(q, k, v, extra=None, beside=None):
                def finish(i):
                    t, h = i // 4, i % 4
                    r, prb, pTb = 64 * (h % 2), (pr2 if extra else pr), (pT2 if extra else pT)
                    at_norm.next(pe)
                    if i >= 1:
                        pe.wait_ge(at_copied.sem, i)
                    for kt in range(t + 1):
                        m = pe.transpose(ps[:, 6, kt * P:(kt + 1) * P], prb[:, i % 2, kt * P:(kt + 1) * P], ident[:])
                    m.then_inc(at_turn.sem, 1)
                    at_copied.next(pe)
                    if i >= 1:
                        pe.wait_ge(at_out.sem, i)
                    for kt in range(t + 1):
                        m = pe.matmul(ps[r:r + 64, 7, 0:P], v(kt, h), pTb[:, i % 2, kt, :],
                                      start=kt == 0, stop=kt == t)
                    m.then_inc(at_pv.sem, 1)

                for i in range(17):
                    if i < 16:
                        t, h = i // 4, i % 4
                        r, K = 64 * (h % 2), (t + 1) * P
                        if i >= 2:
                            pe.wait_ge(lg_max.sem, i - 1)
                        m = pe.matmul(ps[:, 4 + i % 2, 0:K], q(h)[r:r + 64, t * P:(t + 1) * P], k(h)[r:r + 64, 0:K],
                                      start=True, stop=extra is None)
                        if extra:
                            pe.matmul(ps[:, 4 + i % 2, 0:K], fsel[0:4, h, t * P:(t + 1) * P], ones[0:4, 0:K],
                                      start=False, stop=False)
                            m = pe.matmul(ps[:, 4 + i % 2, 0:K], hsel[:, h, :], fneg[0:4, 0:K],
                                          start=False, stop=True)
                        m.then_inc(lg_done.sem, 1)
                    if beside:
                        beside(i)
                    if i >= 1:
                        finish(i - 1)

            n_mod = [0]

            def modulate(b, n=1):
                for i in range(n_mod[0], n_mod[0] + n):
                    ada_ready.next(pe)
                    for j in range(ADA_W // P):
                        m = pe.matmul(ps[:, b, i * (ADA_W // P) + j:i * (ADA_W // P) + j + 1],
                                      ada_sum[:, j * P:(j + 1) * P], ones[:, 0:1], start=True, stop=True)
                    m.then_inc(ada_used.sem, 1)
                n_mod[0] += n
                if n_mod[0] in (NA_PROJ, NA):
                    pe.drain().then_inc(mod_done.sem, 1)

            def ffn():
                tile(first=True)
                for j in range(3):
                    tile()
                with loop(pe, NF // 2 - 1, {mm_free: 4, w_lo: 4}) as i:
                    for j in range(4):
                        tile()
                place[1] += NF
                base = mm_free.seen[id(pe)]
                pe.wait_ge(mm_free.sem, base[0] + base[1] + 4)

                def down(k, first=False, last=False):
                    w = parts_ready()
                    act_ready.next(pe)
                    for d in range(KD):
                        m = product(ps[:, d, :], wh[:, w, d, :], ah[:, k], wl[:, w, d, :], al[:, k], first, last)
                        if last:
                            m.then_inc(down_done.sem, 1)
                    if last:
                        pe.drain().then_inc(mm_done.sem, 1)
                    else:
                        m.then_inc(mm_done.sem, 1)

                for j in range(2):
                    down(slice(j * T, (j + 1) * T), first=j == 0)
                with loop(pe, NF // 2 - 2, {act_ready: 2, w_lo: 2}) as i:
                    for j in range(2):
                        down(bass.ds(i * (2 * T) + (j + 2) * T, T))
                for j in range(NF - 2, NF):
                    down(slice(j * T, (j + 1) * T), last=j == NF - 1)
                place[1] += NF

            for p in range(2):
                pe.sem_inc(w_free[p].sem, 1)
            pe.wait_ge(const_ready.sem, 1)
            pe.wait_ge(p_loaded.sem, 16 * DEPTH * PARAM_LOADS)
            for n in range(8):
                pe.transpose(ps[:, 4 + n % 4, 0:P] if n < 4 else ps[:, 4 + n % 4, P:2 * P],
                             prow[:, n // 4, (n // 2) % 2, n % 2, :], ident[:]).then_inc(pt_done.sem, 1)
            pe.wait_ge(x_loaded.sem, 16)
            xs = arena[:, 0:NT * D].rearrange("p (n d) -> p n d", n=NT)
            for k in range(KD):
                if k >= 4:
                    pe.wait_ge(xt_copied.sem, k - 3)
                for n in range(NT):
                    m = pe.transpose(ps[:, k % 4, n * P:(n + 1) * P], xs[:, n, k * P:(k + 1) * P], ident[:])
                m.then_inc(xt_done.sem, 1)
            end(1)

            with pe.Fori(0, DEPTH) as l:
                begin(l * (SLOTS_1 // 2))
                norm(KD)
                tile(first=True)
                for n in range(3):
                    tile()
                tile(64)
                tile(64)
                tile(4, beside=4)
                token_tile(68)
                def index(i):
                    t, h = 1 + i // 4, i % 4
                    if i == 0:
                        ix_go.next(pe)
                    if i >= 2:
                        pe.wait_ge(ix_relu.sem, i - 1)
                    r, K = 64 * (h % 2), (t + 1) * P
                    pe.matmul(ps[:, 4 + 2 * (h % 2), 0:K], saqi[r:r + 64, h // 2, t * P:(t + 1) * P],
                              saki[r:r + 64, 0:K], start=True, stop=True).then_inc(ix_done.sem, 1)

                for n in range(22):
                    tile()
                    if n % 5 == 0:
                        modulate(5)
                    if 1 <= n <= 12:
                        index(n - 1)
                token_tile(P)
                token_tile(P)
                place[1] += 16

                small_copied.next(pe)
                pe.wait_ge(ix_relu.sem, 12)
                attention(lambda h: saq[:, h // 2, :], lambda h: sak, lambda kt, h: sav[:, kt, :],
                          beside=lambda i: modulate(0) if i in (5, 12) else None)

                g_cum.next(pe)
                pe.wait_ge(at_copied.sem, 16)
                for n in range(NT):
                    for o, src in enumerate((gg, bet)):
                        m = pe.matmul(ps[:, 6, 8 * n + 4 * o:8 * n + 4 * o + 4], src[0:4, n * P:(n + 1) * P],
                                      ident[0:4, 0:4], start=True, stop=True)
                m.then_inc(g_turn.sem, 1)
                pe.wait_ge(at_out.sem, 16)
                row_norms(8)
                for h in range(4):
                    q, k, v = dnT[:, h, :], dnT[:, 4 + h, :], dnT[:, 8 + h, :]
                    if h:
                        dn_u.next(pe)
                    pe.matmul(ps[:, 4, :], hsel[:, h, :], gg[0:4, :], start=True, stop=True)
                    pe.matmul(ps[:, 5, :], hsel[:, h, :], bet[0:4, :], start=True, stop=True).then_inc(dn_bc.sem, 1)
                    dn_q.next(pe)
                    g_cols.next(pe) if h == 0 else None
                    for n in range(NT):
                        m = pe.matmul(ps[:, 6, n * P:(n + 1) * P], k[:, n * P:(n + 1) * P], k[:, n * P:(n + 1) * P],
                                      start=True, stop=True)
                    m.then_inc(dn_gram.sem, 1)
                    for n in range(NT):
                        m = pe.matmul(ps[:, 7, n * P:(n + 1) * P], k[:, n * P:(n + 1) * P], q[:, n * P:(n + 1) * P],
                                      start=True, stop=True)
                    m.then_inc(dn_gram.sem, 1)
                    dn_bc_used.next(pe)
                    for n in range(NT):
                        m = pe.transpose(ps[:, 4, n * P:(n + 1) * P], k[:, n * P:(n + 1) * P], ident[:])
                    m.then_inc(dn_turn.sem, 1)
                    for n in range(NT):
                        m = pe.transpose(ps[:, 5, n * P:(n + 1) * P], v[:, n * P:(n + 1) * P], ident[:])
                    m.then_inc(dn_turn.sem, 1)
                    dn_r.next(pe)
                    for n in range(NT):
                        m = pe.transpose(ps[:, 6, n * P:(n + 1) * P], Rm[:, n, :], ident[:])
                    m.then_inc(dn_rt.sem, 1)
                    dn_turned.next(pe)
                    dn_t.next(pe)
                    for i in range(1, 6):
                        if i % 3 == 2:
                            modulate(0)
                        dn_c.next(pe)
                        if i > 1:
                            dn_updt.next(pe)
                        for n in range(NT):
                            m = pe.matmul(ps[:, 4, n * P:(n + 1) * P], Cm[i % 2][:, n, :], Tm[:, n, :],
                                          start=True, stop=True)
                        m.then_inc(dn_x.sem, 1)
                        dn_xc.next(pe)
                        if i > 1:
                            dn_upd.next(pe)
                        if i < 5:
                            for n in range(NT):
                                m = pe.matmul(ps[:, 5, n * P:(n + 1) * P], Rm[:, n, :], Xm[:, n, :],
                                              start=True, stop=True)
                            m.then_inc(dn_yt.sem, 1)
                        for n in range(NT):
                            m = pe.matmul(ps[:, 6, n * P:(n + 1) * P], Xm[:, n, :], Rm[:, n, :],
                                          start=True, stop=True)
                        m.then_inc(dn_y.sem, 1)
                    dn_upd.next(pe)
                    for n in range(NT):
                        pe.matmul(ps[:, 4, n * P:(n + 1) * P], Rm[:, n, :], vb[:, n, :], start=True, stop=True)
                    for n in range(NT):
                        m = pe.matmul(ps[:, 5, n * P:(n + 1) * P], kb[:, n, :], Rm[:, n, :], start=True, stop=True)
                    m.then_inc(dn_kb.sem, 1)
                dn_u.next(pe)
                for c in range(NC):
                    r, n, par_ = C * (c % 2), c // 2, c % 2
                    if c == 0:
                        rc_s.next(pe)
                    for h in range(4):
                        m = pe.matmul(ps[r:r + C, 4, h * P:(h + 1) * P], dnT[:, 4 + h, c * C:(c + 1) * C], S[:, h, :],
                                      start=True, stop=True)
                    m.then_inc(rc_ws.sem, 1)
                    rc_u.next(pe)
                    if c >= 2:
                        pe.wait_ge(rc_oc.sem, c - 1)
                    bo = 5 + 2 * (c % 2)
                    for h in range(4):
                        pe.matmul(ps[:, bo, h * C:(h + 1) * C], S[:, h, :], dnT[:, h, c * C:(c + 1) * C],
                                  start=True, stop=False)
                        m = pe.matmul(ps[:, bo, h * C:(h + 1) * C], u[r:r + C, par_, h, :],
                                      qkm[r:r + C, h, n, r:r + C], start=False, stop=True)
                    m.then_inc(rc_o.sem, 1)
                    for h in range(4):
                        m = pe.matmul(ps[:, 6, h * P:(h + 1) * P], kd[r:r + C, h, n, :], u[r:r + C, par_, h, :],
                                      start=True, stop=True)
                    m.then_inc(rc_ds.sem, 1)
                    rc_s.next(pe)
                pe.wait_ge(rc_oc.sem, NC)
                row_norms(4)

                for q in range(2):
                    for i in range(7):
                        if (q, i) in ((0, 1), (0, 5), (1, 3)):
                            modulate(0)
                        hg_qk.next(pe)
                        for h in range(2):
                            g_ = 7 * 2 * q + 2 * i + h
                            if g_ >= 4:
                                pe.wait_ge(hg_pred.sem, g_ - 3)
                            r, o = 64 * h, (7 * q + i) % 2
                            for n in range(NT):
                                m = pe.matmul(ps[:, 4 - 2 * o + h, n * P:(n + 1) * P],
                                              ke[o][r:r + 64, n * P:(n + 1) * P],
                                              qe[o][r:r + 64, n * P:(n + 1) * P], start=True, stop=True)
                            m.then_inc(hg_gram.sem, 1)
                    hg_kd.next(pe)
                    for n in range(NT):
                        m = pe.transpose(ps[:, 6, n * P:(n + 1) * P], hkd[:, n * P:(n + 1) * P], ident[:])
                    m.then_inc(hg_turn.sem, 1)
                    hg_turned.next(pe)
                pe.wait_ge(hg_pred.sem, 28)
                for c in range(NC):
                    r, n = C * (c % 2), c // 2
                    for h in range(4):
                        ro, q = 64 * (h % 2), h // 2
                        m = pe.matmul(ps[ro:ro + 64, 4 + c % 2, (c // 2) * P + q * 64:(c // 2) * P + q * 64 + 64],
                                      kdt[r:r + C, q, n, ro:ro + 64], hgi[r:r + C, n, h * 64:h * 64 + 64],
                                      start=True, stop=True)
                m.then_inc(hg_ds.sem, 1)
                hg_s.next(pe)
                for q in range(2):
                    for n in range(NT):
                        for h in (2 * q, 2 * q + 1):
                            r = 64 * (h % 2)
                            pe.matmul(ps[r:r + 64, 4 + q, n * P:(n + 1) * P], hgi[:, n, h * 64:h * 64 + 64],
                                      Ah[:, h, n, :], start=True, stop=False)
                            for c in (2 * n, 2 * n + 1):
                                m = pe.matmul(ps[r:r + 64, 4 + q, c * C:(c + 1) * C], hS[r:r + 64, c, q, :],
                                              hqd[r:r + 64, q, c * C:(c + 1) * C], start=False, stop=c % 2 == 1)
                    m.then_inc(hg_o.sem, 1)
                norm(1, bdones[:])
                norm(1, bdones[:])

                mix_ready.next(pe)
                for n in range(4):
                    out_pair(oT)
                norm(KD)
                norm(KD)
                ffn()
                norm(KD)
                end(l + 2)

            with pe.Fori(0, DEPTH) as l:
                begin(l * (SLOTS_2 // 2) + DEPTH * SLOTS_1 // 2)
                norm(KD)
                ffn()
                norm(KD)
                tile(first=True)
                for n in range(5):
                    tile()
                norm(1, bdones[:])
                norm(1, bdones[:])
                tile()
                tile()
                norm(1, bdones[:])
                norm(1, bdones[:])
                for n in range(8):
                    tile()
                for n in range(4):
                    token_tile(P)
                place[1] += 10
                small_lo.next(pe)
                for k in range(KD):
                    m = product(ps[0:4, 4, :], wsh[:, k, :], hh[:, k, :], wsl[:, k, :], hl[:, k, :],
                                k == 0, k == KD - 1)
                m.then_inc(small_done.sem, 1)
                small2_copied.next(pe)
                pe.wait_ge(small_loaded.sem, l * 80 + 80)
                for j in range(4):
                    if j:
                        lr_sig.next(pe)
                    pe.matmul(ps[:, 4, :], wg[:, 0, j, :], uT[:, j, :], start=True, stop=True)
                    pe.matmul(ps[:, 5, :], wg[:, 1, j, :], uT[:, j, :], start=True, stop=True)\
                        .then_inc(lr_gates.sem, 1)
                lr_sig.next(pe)
                norm(4)
                pe.wait_ge(std_done.sem, n_norm[0])
                for h in range(4):
                    r, q = 64 * (h % 2), h // 2
                    for b in range(NT):
                        N = T - b * P
                        sb_used.ring(pe, NT)
                        pe.matmul(ps[:, b, 0:N], sbk[r:r + 64, q, b * P:(b + 1) * P], sbq[r:r + 64, q, b * P:T],
                                  start=True, stop=True).then_inc(sb_z.sem, 1)
                    sb_l.next(pe, NT)
                    for b in range(NT):
                        N = T - b * P
                        sb_min.ring(pe, 1)
                        pe.matmul(ps[:, 6, 0:N], sbk[r:r + 64, q, b * P:(b + 1) * P], sbq[r:r + 64, q, b * P:T],
                                  start=True, stop=False)
                        for j in range(b, NT):
                            m = pe.matmul(ps[:, 6, (j - b) * P:N], negtri[:] if j == b else negones[:],
                                          Lb[:, j, 0:T - j * P], start=False, stop=j == NT - 1)
                        m.then_inc(sb_p.sem, 1)
                        sb_w.next(pe)
                        if b == 0:
                            sb_out.ring(pe, 1)
                        pe.matmul(ps[r:r + 64, 7, b * P:T], vtok[:, b, h * 64:h * 64 + 64], wsb[:, b % 2, 0:N],
                                  start=b == 0, stop=b == NT - 1).then_inc(sb_pv.sem, 1)
                sb_out.ring(pe, 1)
                norm(2)
                ff_sel.next(pe)
                pe.wait_ge(std_done.sem, n_norm[0])
                attention(lambda h: fxq[:, h // 2, :], lambda h: fxk[:, h // 2, :],
                          lambda kt, h: vtok[:, kt, 256 + h * 64:256 + h * 64 + 64], extra=True)
                pe.wait_ge(at_out.sem, 16)
                norm(2)
                mix_ready.next(pe)
                for n in range(4):
                    out_pair(o2)
                norm(KD)
                ffn()
                end(l + 4)

            for n in range(2 * NT):
                if n >= 4:
                    pe.wait_ge(out_cp.sem, n - 3)
                for k in range(4):
                    m = pe.transpose(ps[:, n % 4, k * P:(k + 1) * P],
                                     xT[:, 4 * (n % 2) + k, (n // 2) * P:(n // 2 + 1) * P], ident[:])
                m.then_inc(out_tr.sem, 1)

        @block.vector
        def _(v):
            link = Order(v, dve_order)

            def begin():
                for x in scoped:
                    x.restart(id(v))
                mm_done.seen[id(v)][1] = 1
                n_mm[0] = n_split[0] = 0
                half[:] = [0, 0]
                v.sem_inc(mm_free.sem, 4)

            def end(go):
                v.drain().then_inc(layer_end.sem, 1)
                v.wait_ge(layer_go.sem, go)

            n_mm = [0]
            n_split = [0]
            half = [0, 0]

            def split(whole=False):
                p, h = half
                w = n_split[0] % 2
                n_split[0] += 1
                w_hi.next(v)
                v.tensor_tensor(wl[:, w, :, :], wring[:, p, h, :, :], wh[:, w, :, :].bitcast(F32), ALU.subtract)\
                    .then_inc(w_lo.sem, 1)
                if h or whole:
                    v.drain().then_inc(w_free[p].sem, 1)
                    half[:] = [1 - p, 0]
                else:
                    half[1] = 1

            def filled():
                mm_done.next(v)
                b = n_mm[0] % 4
                n_mm[0] += 1
                return b

            def root():
                v.drain()
                std_done.next(v)
                v.reciprocal(rstd[:, :], std[:, :]).then_inc(rec_done.sem, 1)
                rec_done.next(v)

            def row_roots(n):
                std_done.next(v)
                v.reciprocal(rstd[0:NT * n, 0:P], std[0:NT * n, 0:P]).then_inc(rec_done.sem, 1)
                rec_done.next(v)

            def factors(m):
                bc_done.next(v)
                return ps[:, 1 + m % 3, :]

            def pre_norm(g, shift=None):
                root()

                def low(k):
                    h_hi.next(v)
                    if shift is None:
                        i = v.tensor_tensor(hl[:, k, :], sq[:, k % 4, :], hh[:, k, :].bitcast(F32), ALU.subtract)
                    else:
                        i = v.scalar_tensor_tensor(hl[:, k, :], sq[:, k % 4, :], shift(k), hh[:, k, :].bitcast(F32),
                                                   ALU.add, ALU.subtract)
                    i.then_inc(h_ready.sem, 1)

                for k in range(KD + 1):
                    if k < KD:
                        v.scalar_tensor_tensor(sq[:, k % 4, :], xT[:, k, :], g(k), rstd[:, :], ALU.mult, ALU.mult)\
                            .then_inc(h_sum.sem, 1)
                    if k:
                        low(k - 1)
                v.drain()

            def post_norm(g):
                root()
                for k in range(KD):
                    v.scalar_tensor_tensor(hT[:, k, :], hT[:, k, :], g(k), rstd[:, :], ALU.mult, ALU.mult)
                v.drain()
                for k in range(KD):
                    v.tensor_tensor(xT[:, k, :], xT[:, k, :], hT[:, k, :], ALU.add).then_inc(x_ready.sem, 1)
                v.drain()

            def taps(dst, b, w, n, bias=None):
                if bias is None:
                    link(v.tensor_scalar(dst, ps[:, b, :], w(n - 1), None, ALU.mult))
                else:
                    link(v.tensor_scalar(dst, ps[:, b, :], w(n - 1), bias, ALU.mult, ALU.add))
                for s_ in range(1, n):
                    i = v.scalar_tensor_tensor(dst[:, s_:T], ps[:, b, 0:T - s_], w(n - 1 - s_), dst[:, s_:T],
                                               ALU.mult, ALU.add)
                    if s_ < n - 1:
                        link(i)
                return i

            def free():
                v.drain().then_inc(mm_free.sem, 1)

            def softmax(lgb, prb, mxb, smb, mask, dst):
                def top(i):
                    t, h = i // 4, i % 4
                    K = (t + 1) * P
                    lg_done.next(v)
                    if i >= 2:
                        v.wait_ge(at_exp.sem, i - 1)
                    link(v.tensor_tensor(lgb[:, i % 2, 0:K], ps[:, 4 + i % 2, 0:K], mask(t), ALU.add))
                    link(v.tensor_reduce(mxb[:, i % 2, 0:1], lgb[:, i % 2, 0:K], AX, ALU.max))
                    v.tensor_scalar(mxb[:, i % 2, 1:2], mxb[:, i % 2, 0:1], -1.0, None, ALU.mult)\
                        .then_inc(lg_max.sem, 1)

                def scale(i):
                    K = (i // 4 + 1) * P
                    at_exp.next(v)
                    link(v.reciprocal(smb[:, i % 2, 1:2], smb[:, i % 2, 0:1]))
                    v.tensor_scalar(prb[:, i % 2, 0:K], prb[:, i % 2, 0:K], smb[:, i % 2, 1:2], None, ALU.mult)\
                        .then_inc(at_norm.sem, 1)
                    at_pv.next(v)
                    t, h = i // 4, i % 4
                    r = 64 * (h % 2)
                    v.tensor_copy(dst[r:r + 64, h // 2, t * P:(t + 1) * P], ps[r:r + 64, 7, 0:P])\
                        .then_inc(at_out.sem, 1)

                for i in range(17):
                    if i < 16:
                        top(i)
                    if i >= 1:
                        scale(i - 1)

            def ffn(tap=None):
                def w(i, j, h):
                    def at_(s_):
                        o = (A_TAP + 2 * NF * s_ if s_ < 2 else P + B_TAP) + h * NF + j
                        return par[:, :, :].rearrange("p a b -> p (a b)")[:, bass.ds(i * 2 + o, 1)]
                    return at_

                with loop(v, NF // 2, {mm_done: 4, w_hi: 4, dve_order: 12 if tap else 4, act_gelu: 2}) as i:
                    def product(j):
                        act_gelu.next(v)
                        link(v.tensor_tensor(conv[:, 0, j, :], conv[:, 0, j, :], conv[:, 1, j, :], ALU.mult))
                        k = bass.ds(i * (2 * T) + j * T, T)
                        link(v.tensor_copy(ah[:, k], conv[:, 0, j, :]))
                        v.tensor_tensor(al[:, k], conv[:, 0, j, :], ah[:, k].bitcast(F32), ALU.subtract)\
                            .then_inc(act_ready.sem, 1)

                    for j in range(2):
                        for h in range(2):
                            split()
                            if j and h:
                                product(0)
                            b = filled()
                            if tap:
                                taps(conv[:, h, j, :], b, w(i, j, h), 3)
                            else:
                                v.tensor_copy(conv[:, h, j, :], ps[:, b, :])
                            free()
                        v.sem_inc(act_in.sem, 1)
                    product(1)
                    v.drain()
                v.drain().then_inc(w_free[0].sem, 1)
                half[:] = [1, 0]
                with loop(v, NF // 2 - 1, {w_hi: 2}):
                    split(whole=True)
                    split(whole=True)
                split(whole=True)
                mm_done.seen[id(v)][1] += NF

            for n in range(8):
                v.wait_ge(pt_done.sem, 8)
                src = ps[:, 4 + n % 4, 0:P] if n < 4 else ps[:, 4 + n % 4, P:2 * P]
                v.tensor_copy(pall[:, n // 4, (n // 2) % 2, n % 2, :], src).then_inc(pt_copied.sem, 1)
            v.wait_ge(pt_copied.sem, 8)
            link(v.tensor_copy(hgw[:, 0:4], pall[:, 0, 0, 1, B_LB:B_LB + 4]))
            v.tensor_copy(cs[:, :], pall[:, 1, 0, 1, B2_C:B2_C + 8])
            link(v.tensor_tensor(hgw[:, 12:14], hgw[:, 0:2], hgw[:, 2:4], ALU.max))
            for o in range(2):
                v.tensor_tensor(hgw[:, 4 + 2 * o:6 + 2 * o], hgw[:, 2 * o:2 * o + 2], hgw[:, 12:14], ALU.subtract)
            v.drain().then_inc(pt_copied.sem, 1)
            for k in range(KD):
                v.wait_ge(xt_done.sem, k + 1)
                v.tensor_copy(xT[:, k, :], ps[:, k % 4, :]).then_inc(xt_copied.sem, 1)
            v.wait_ge(c_act.sem, 1)
            link(v.tensor_tensor(hgw[:, 12:14], hgw[:, 8:10], hgw[:, 10:12], ALU.add))
            link(v.reciprocal(hgw[:, 12:14], hgw[:, 12:14]))
            for o in range(2):
                v.tensor_tensor(hgw[:, 4 + 2 * o:6 + 2 * o], hgw[:, 8 + 2 * o:10 + 2 * o], hgw[:, 12:14], ALU.mult)
            v.drain()
            link(v.tensor_tensor(hgw[:, 14:16], hgw[:, 4:6], hgw[:, 6:8], ALU.add))
            v.tensor_tensor(lbs[:, 0, :], hgw[:, 4:6], hgw[:, 4:6], ALU.subtract)
            v.tensor_tensor(lbs[:, 1, :], hgw[:, 14:16], hgw[:, 4:6], ALU.subtract)
            end(1)

            with v.Fori(0, DEPTH) as l:
                begin()
                v.tensor_copy(par[:, :, :], pall[:, 0, bass.ds(l, 1), :, :].rearrange("p o a b -> p (o a) b"))
                v.tensor_copy(lb[:, 0, :], lbs[:, bass.ds(l, 1), :].rearrange("p o a -> p (o a)"))
                v.tensor_copy(head[:, 0:3], tiny[:, bass.ds(l, 1), 0:3].rearrange("p o a -> p (o a)"))
                v.drain()
                link(v.tensor_scalar(lb[:, 1, :], lb[:, 0, :], -1.0, 1.0, ALU.mult, ALU.add))
                v.drain().then_inc(par_ready.sem, 1)
                split()
                pre_norm(lambda k: par[:, 0, A_G + k:A_G + k + 1])

                for j in range(2):
                    split()
                    b = filled()
                    v.tensor_scalar(saq[:, j, :], ps[:, b, :], 0.125, None, ALU.mult)
                    free()
                for j in range(2):
                    split()
                    b = filled()
                    v.tensor_copy(saqi[:, j, :], ps[:, b, :])
                    free()
                for dst in (sak, saki):
                    split()
                    b = filled()
                    v.tensor_copy(dst[0:64, :], ps[0:64, b, :])
                    v.tensor_copy(dst[64:128, :], ps[0:64, b, :])
                    free()
                split()
                b = filled()
                v.tensor_copy(bet[0:4, :], ps[0:4, b, :])
                v.tensor_scalar(gg[0:4, :], ps[0:4, 4, :], head[:, 1:2], None, ALU.add)
                free()
                split()
                b = filled()
                small = ps[:, b, 0:4 * 68].rearrange("p (n c) -> p n c", n=NT)
                v.tensor_copy(sav[:, :, :], small[:, :, 0:64])
                v.tensor_scalar(sawi[:, :, :], small[:, :, 64:68], 0.0625, None, ALU.mult)
                free()
                v.sem_inc(ix_go.sem, 1)

                def choice():
                    for t in range(1, NT):
                        K = (t + 1) * P
                        sc = score[:, t - 1, 0:K]
                        ix_relu.next(v, 4)
                        link(v.tensor_scalar(sc, rl[:, 0, 0:K], sawi[:, t, 0:1], None, ALU.mult))
                        for h in range(1, 4):
                            link(v.scalar_tensor_tensor(sc, rl[:, h, 0:K], sawi[:, t, h:h + 1], sc,
                                                        ALU.mult, ALU.add))
                        v.sem_inc(ix_used.sem, 1)
                        link(v.memset(score[0:64, t - 1, t * P + 64:K], OUTSIDE))
                        yield
                        for n in range(TOPK // 8):
                            link(v.max(m8[:, n % 2, :], sc))
                            link(v.match_replace(sc, m8[:, n % 2, :], sc, TAKEN))
                            yield
                        link(v.tensor_scalar(sc, sc, 0.5 * (TAKEN + OUTSIDE), NEG, ALU.is_gt, ALU.mult))

                picks = choice()

                def pick(n):
                    for _ in range(n):
                        next(picks, None)

                for j in range(12):
                    split()
                    b = filled()
                    if j >= 2:
                        v.wait_ge(silu_done.sem, j - 1)
                    taps(cbuf[:, j % 2, :], b, lambda s_: par[:, 1, B_DNC + 12 * s_ + j:B_DNC + 12 * s_ + j + 1], 4)
                    free()
                    v.sem_inc(conv_done.sem, 1)
                    if j >= 6:
                        pick(1 if j == 6 else 4)
                for n, dst in enumerate([zT[:, j, :] for j in range(4)] + [hgq[:, j, :] for j in range(2)] + \
                        [hgf[:, j, :] for j in range(2)] + [hgg[:, j, :] for j in range(2)]):
                    split()
                    b = filled()
                    v.tensor_copy(dst, ps[:, b, :])
                    free()
                    v.sem_inc(conv_done.sem, 1)
                    pick(4)
                for j in range(2):
                    if j == 0:
                        split()
                    b = filled()
                    v.tensor_copy(hgi[:, :, j * P:(j + 1) * P], ps[:, b, :].rearrange("p (n c) -> p n c", n=NT))
                    free()
                v.wait_ge(silu_done.sem, 20)
                mod_done.next(v)
                cut = NA_PROJ * ADA_W // P
                v.tensor_copy(mods[:, bass.ds(l, 1), 0:cut].rearrange("p o a -> p (o a)"), ps[:, 5, 0:cut])
                v.drain().then_inc(small_copied.sem, 1)

                pick(3 * (TOPK // 8 + 1) + 1)
                softmax(lg, pr, mx, sm, lambda t: score[:, t - 1, 0:(t + 1) * P] if t else chunkadd[:],
                        oT[:, 4:6, :])

                v.sem_inc(g_in.sem, 1)
                g_soft.next(v)
                link(v.tensor_scalar(head[:, 3:4], head[:, 3:4], -1.0, None, ALU.mult))
                link(v.scalar_tensor_tensor(gg[0:4, :], gg[0:4, :], 0.0, gtmp[0:4, :], ALU.max, ALU.add))
                link(v.tensor_scalar(gg[0:4, :], gg[0:4, :], head[:, 3:4], None, ALU.mult))
                v.tensor_tensor_scan(gg[0:4, :], reset[0:4, :], gg[0:4, :], 0.0, ALU.mult, ALU.add)\
                    .then_inc(g_cum.sem, 1)
                g_turn.next(v)
                v.tensor_copy(gcol[:, :, :], ps[:, 6, 0:32].rearrange("p (n c) -> p n c", n=NT))\
                    .then_inc(g_cols.sem, 1)
                g_ecol.next(v)
                g_cols.next(v)
                link(v.tensor_tensor(begcol[:, :, :], egcol[:, :, :], gcol[:, :, 4:8], ALU.mult))
                row_roots(8)
                for j in range(8):
                    f = factors(j)
                    v.scalar_tensor_tensor(dnT[:, j, :], dnT[:, j, :], P ** -0.5 if j < 4 else 1.0, f,
                                           ALU.mult, ALU.mult).then_inc(bc_used.sem, 1)
                v.drain()
                for h in range(4):
                    q, k, vv = dnT[:, h, :], dnT[:, 4 + h, :], dnT[:, 8 + h, :]
                    v.sem_inc(dn_q.sem, 1)
                    dn_bc.next(v)
                    for n in range(NT):
                        v.tensor_scalar(dec[:, n, :], ps[:, 4, n * P:(n + 1) * P], gcol[:, n, h:h + 1], 0.0,
                                        ALU.subtract, ALU.min)
                    v.drain().then_inc(dn_sub.sem, 1)
                    dn_exp.next(v, 2)
                    link(v.tensor_tensor(dec[:, :, :], dec[:, :, :],
                                         bdcausal[:, None, :].broadcast_to([P, NT, P]), ALU.mult))
                    v.tensor_copy(kdc[0:64, :, None], dec[0:64, :, 63:64])
                    v.tensor_copy(kdc[64:128, :, None], dec[64:128, :, 127:128])
                    v.tensor_copy(egl[:, h, :, None], eg[:, :].rearrange("p (n c) -> p n c", c=C)[:, :, C - 1:C])
                    dn_gram.next(v)
                    link(v.tensor_tensor(mt[:, :, :].rearrange("p a b -> p (a b)"), ps[:, 6, :],
                                         dec[:, :, :].rearrange("p a b -> p (a b)"), ALU.mult))
                    link(v.tensor_tensor(mt[:, :, :].rearrange("p a b -> p (a b)"), ps[:, 5, :],
                                         mt[:, :, :].rearrange("p a b -> p (a b)"), ALU.mult))
                    dn_gram.next(v)
                    v.tensor_tensor(qkm[:, h, :, :].rearrange("p a b -> p (a b)"), ps[:, 7, :],
                                    dec[:, :, :].rearrange("p a b -> p (a b)"), ALU.mult)
                    v.drain().then_inc(dn_bc_used.sem, 1)
                    def part(i):
                        return v.tensor_tensor(Cm[i % 2], mt[:, :, :], level[:, i:i + 1, :].broadcast_to([P, NT, P]),
                                               ALU.mult)

                    link(part(0))
                    link(v.tensor_tensor(Rm[:, :, :], ident[:, None, :].broadcast_to([P, NT, P]), Cm[0],
                                         ALU.subtract))
                    v.sem_inc(dn_r.sem, 1)
                    v.tensor_tensor(q, q, eg[:, :], ALU.mult)
                    dn_turn.next(v)
                    for n in range(NT):
                        v.tensor_scalar(kd[:, h, n, :], ps[:, 4, n * P:(n + 1) * P], kdc[:, n:n + 1], None, ALU.mult)
                        v.tensor_scalar(kb[:, n, :], ps[:, 4, n * P:(n + 1) * P], begcol[:, n, h:h + 1], None, ALU.mult)
                    dn_turn.next(v)
                    for n in range(NT):
                        v.tensor_scalar(vb[:, n, :], ps[:, 5, n * P:(n + 1) * P], gcol[:, n, 4 + h:5 + h], None,
                                        ALU.mult)
                    v.drain().then_inc(dn_turned.sem, 1)
                    part(1).then_inc(dn_c.sem, 1)
                    dn_rt.next(v)
                    v.tensor_copy(Tm[:, :, :].rearrange("p a b -> p (a b)"), ps[:, 6, :]).then_inc(dn_t.sem, 1)
                    dn_t.next(v)
                    for i in range(1, 6):
                        if i < 5:
                            part(i + 1).then_inc(dn_c.sem, 1)
                            dn_yt.next(v)
                            v.tensor_tensor(Tm[:, :, :].rearrange("p a b -> p (a b)"),
                                            Tm[:, :, :].rearrange("p a b -> p (a b)"), ps[:, 5, :], ALU.subtract)\
                                .then_inc(dn_updt.sem, 1)
                        dn_y.next(v)
                        v.tensor_tensor(Rm[:, :, :].rearrange("p a b -> p (a b)"),
                                        Rm[:, :, :].rearrange("p a b -> p (a b)"), ps[:, 6, :], ALU.subtract)
                        v.drain().then_inc(dn_upd.sem, 1)
                    dn_kb.next(v)
                    v.tensor_copy(vv, ps[:, 4, :])
                    v.tensor_copy(k, ps[:, 5, :])
                    v.drain().then_inc(dn_u.sem, 1)
                v.memset(S[:, :, :], 0.0).then_inc(rc_s.sem, 1)
                rc_s.next(v)
                for c in range(NC):
                    r, n, par_ = C * (c % 2), c // 2, c % 2
                    u0 = dnT[r:r + C, 8:12, n * P:(n + 1) * P]
                    rc_ws.next(v)
                    v.tensor_tensor(u[r:r + C, par_, :, :], u0,
                                    ps[r:r + C, 4, :].rearrange("p (h c) -> p h c", h=4), ALU.subtract)\
                        .then_inc(rc_u.sem, 1)
                    rc_ds.next(v)
                    for h in range(4):
                        v.scalar_tensor_tensor(S[:, h, :], S[:, h, :], egl[:, h, c:c + 1],
                                               ps[:, 6, h * P:(h + 1) * P], ALU.mult, ALU.add)
                    v.drain().then_inc(rc_s.sem, 1)
                v.wait_ge(rc_oc.sem, NC)
                row_roots(4)
                for h in range(4):
                    i = v.scalar_tensor_tensor(oraw[:, h, :], oraw[:, h, :], par[:, 1, B_DNN:B_DNN + 1], factors(h),
                                               ALU.mult, ALU.mult)
                    i.then_inc(bc_used.sem, 1)
                    v.drain()
                    v.tensor_tensor(oT[:, h, :], oraw[:, h, :], zT[:, h, :], ALU.mult)
                v.drain()

                v.memset(Ah[:, :, :, :], 0.0)
                for o in range(2):
                    v.memset(qe[o], 0.0)
                    v.memset(ke[o], 0.0)
                v.drain()
                for q in range(2):
                    v.sem_inc(hg_f.sem, 1)
                    hg_sig.next(v, 2)
                    v.tensor_scalar(hk[:, :], hk[:, :], lb[:, 1, q:q + 1], None, ALU.mult)
                    link(v.tensor_scalar(hs1[:, :], hs1[:, :], lb[:, 1, q:q + 1], lb[:, 0, q:q + 1], ALU.mult, ALU.add))
                    v.tensor_scalar(hs1[:, :], hs1[:, :], 2.0 ** -63, None, ALU.max).then_inc(hg_ln.sem, 1)
                    hg_b.next(v)
                    link(v.tensor_tensor_scan(hb[:, :], reset[:, :], hs1[:, :], 0.0, ALU.mult, ALU.add))

                    def blocks(x, L):
                        return x.rearrange("p (n o c) -> p n o c", o=2, c=L)

                    def differences(i):
                        L = LEVELS[i]
                        b4, e4 = blocks(hb[:, :], L), blocks(he[(7 * q + i) % 2], L)
                        ref = b4[:, :, 0, L - 1:L].broadcast_to([P, T // (2 * L), L])
                        v.tensor_tensor(e4[:, :, 1, :], b4[:, :, 1, :], ref, ALU.subtract)
                        v.tensor_tensor(e4[:, :, 0, :], ref, b4[:, :, 0, :], ALU.subtract)
                        v.drain().then_inc(hg_sub.sem, 1)

                    def scaled(i):
                        o = (7 * q + i) % 2
                        if i < 6:
                            L = LEVELS[i]
                            e4 = blocks(he[o], L)
                            hg_exp.next(v)
                            v.tensor_tensor(blocks(qe[o], L)[:, :, 1, :], blocks(hgq[:, q, :], L)[:, :, 1, :],
                                            e4[:, :, 1, :], ALU.mult)
                            v.tensor_tensor(blocks(ke[o], L)[:, :, 0, :], blocks(hk[:, :], L)[:, :, 0, :],
                                            e4[:, :, 0, :], ALU.mult)
                        else:
                            v.tensor_copy(qe[o], hgq[:, q, :])
                            v.tensor_copy(ke[o], hk[:, :])
                        v.drain().then_inc(hg_qk.sem, 1)

                    def selected(i):
                        mask = level[:, i:i + 1, :] if i < 6 else ident[:, None, :]
                        v.wait_ge(hg_gram.sem, 14 * q + 2 * i + 2)
                        for h in range(2):
                            v.copy_predicated(Ah[:, 2 * q + h, :, :], mask.bitcast(I32).broadcast_to([P, NT, P]),
                                              ps[:, 4 - 2 * ((7 * q + i) % 2) + h, :]
                                              .rearrange("p (a b) -> p a b", a=NT)).then_inc(hg_pred.sem, 1)

                    differences(0)
                    scaled(0)
                    for i in range(6):
                        if i < 5:
                            differences(i + 1)
                        selected(i)
                        scaled(i + 1)
                    selected(6)
                    b3 = hb[:, :].rearrange("p (n c) -> p n c", c=C)
                    v.tensor_tensor(he[q].rearrange("p (n c) -> p n c", c=C),
                                    b3[:, :, C - 1:C].broadcast_to([P, NC, C]), b3, ALU.subtract)
                    v.drain().then_inc(hg_dec.sem, 1)
                    hg_edec.next(v)
                    v.tensor_tensor(hqd[:, q, :], hgq[:, q, :], hs1[:, :], ALU.mult)
                    v.tensor_copy(hgl[:, q, :, None], hs1[:, :].rearrange("p (n c) -> p n c", c=C)[:, :, C - 1:C])
                    v.tensor_tensor(hkd[:, :], hk[:, :], he[q], ALU.mult).then_inc(hg_kd.sem, 1)
                    hg_turn.next(v)
                    v.tensor_copy(kdt[:, q, :, :].rearrange("p a b -> p (a b)"), ps[:, 6, :])
                    v.drain().then_inc(hg_turned.sem, 1)
                hg_ds.next(v)
                link(v.memset(hS[:, 0, :, :], 0.0))
                for c in range(1, NC):
                    for q in range(2):
                        i = v.scalar_tensor_tensor(
                            hS[:, c, q, :], hS[:, c - 1, q, :], hgl[:, q, c - 1:c],
                            ps[:, 4 + (c - 1) % 2, ((c - 1) // 2) * P + q * 64:((c - 1) // 2) * P + q * 64 + 64],
                            ALU.mult, ALU.add)
                    link(i)
                v.drain().then_inc(hg_s.sem, 1)
                for q in range(2):
                    hg_o.next(v)
                    v.tensor_copy(ho[:, q, :], ps[:, 4 + q, :]).then_inc(hg_oc.sem, 1)
                hg_oc.next(v, 2)
                for q in range(2):
                    root()
                    link(v.scalar_tensor_tensor(ho[:, q, :], ho[:, q, :], par[:, 1, B_HGN:B_HGN + 1], rstd[:, :],
                                                ALU.mult, ALU.mult))
                    v.tensor_tensor(oT[:, 6 + q, :], ho[:, q, :], hgg[:, q, :], ALU.mult)
                mod_done.next(v)
                v.tensor_copy(mods[:, bass.ds(l, 1), cut:].rearrange("p o a -> p (o a)"), ps[:, 0, cut:ADA // P])
                v.drain().then_inc(mix_ready.sem, 1)

                for k in range(KD):
                    b = filled()
                    v.tensor_copy(hT[:, k, :], ps[:, b, :])
                    free()
                    v.sem_inc(y_ready.sem, 1)
                split()
                post_norm(lambda k: par[:, 0, A_G + 8 + k:A_G + 9 + k])
                pre_norm(lambda k: par[:, 0, A_G + 16 + k:A_G + 17 + k])
                ffn(True)
                for n, k in enumerate((7, 0, 1, 2, 3, 4, 5, 6)):
                    if n == 0:
                        down_done.next(v, 8)
                    v.tensor_copy(hT[:, k, :], ps[:, k, :]).then_inc(y_ready.sem, 1)
                v.drain()
                post_norm(lambda k: par[:, 0, A_G + 24 + k:A_G + 25 + k])
                end(l + 2)

            def gated(src, j, k):
                return v.scalar_tensor_tensor(xT[:, k, :], src, cG[:, j, k:k + 1], xT[:, k, :], ALU.mult, ALU.add)

            with v.Fori(0, DEPTH) as l:
                begin()
                v.tensor_copy(par[:, :, :], pall[:, 1, bass.ds(l, 1), :, :].rearrange("p o a b -> p (o a) b"))
                v.tensor_copy(head[:, 0:3], tiny[:, bass.ds(l, 1), 0:3].rearrange("p o a -> p (o a)"))
                v.drain().then_inc(par_ready.sem, 1)
                link(v.tensor_tensor(modP[:, :], mods[:, bass.ds(l, 1), :].rearrange("p o a -> p (o a)"),
                                     par[:, 0, A2_ADA:A2_ADA + 72], ALU.add))
                m4 = modP[:, :].rearrange("p (j w k) -> p j w k", j=3, w=3)
                v.tensor_scalar(cA[:, :, :], m4[:, :, 1, :], 1.0, None, ALU.add)
                v.tensor_scalar(cG[:, :, :], m4[:, :, 2, :], 1.0, None, ALU.add)
                v.drain()
                v.tensor_tensor(cA[:, :, :], cA[:, :, :],
                                par[:, 0, A2_G:A2_G + 24].rearrange("p (j k) -> p j k", j=3), ALU.mult)
                for j in (0, 2):
                    v.tensor_scalar(cG[:, j, :], cG[:, j, :], 0.5, None, ALU.mult)
                v.drain()

                def mod_norm(j):
                    pre_norm(lambda k: cA[:, j, k:k + 1], lambda k: modP[:, 24 * j + k:24 * j + k + 1])

                split()
                mod_norm(0)
                ffn()
                down_done.next(v, 8)
                for k in (7, 0, 1, 2, 3, 4, 5, 6):
                    gated(ps[:, k, :], 0, k)
                v.memset(wg[:, :, :, :], 0.0)
                v.drain()
                for k in range(KD):
                    v.sem_inc(x_ready.sem, 1)
                small_hi.next(v)
                v.tensor_tensor(wsl[:, :, :], wsm[:, :, :], wsh[:, :, :].bitcast(F32), ALU.subtract)\
                    .then_inc(small_lo.sem, 1)
                split()
                mod_norm(1)
                for j in range(2):
                    split()
                    b = filled()
                    v.tensor_scalar(sbq[:, j, :], ps[:, b, :], 0.125, None, ALU.mult)
                    free()
                for j in range(2):
                    split()
                    b = filled()
                    v.tensor_copy(sbk[:, j, :], ps[:, b, :])
                    free()

                def fx_norm(j):
                    dst = (fxq if j < 2 else fxk)[:, j % 2, :]
                    root()
                    g_ = par[:, 1, B2_QK + j // 2:B2_QK + j // 2 + 1]
                    link(v.scalar_tensor_tensor(dst, dst, g_, rstd[:, :], ALU.mult, ALU.mult))
                    if j < 2:
                        link(v.tensor_scalar(dst, dst, 0.125, None, ALU.mult))

                for m in range(2):
                    for j in range(2):
                        split()
                        b = filled()
                        v.tensor_copy((fxk if m else fxq)[:, j, :], ps[:, b, :])
                        free()
                    v.sem_inc(fx_raw.sem, 1)
                    fx_norm(2 * m)
                    v.sem_inc(fx_raw.sem, 1)
                    fx_norm(2 * m + 1)
                for j in range(4):
                    split()
                    b = filled()
                    taps(uT[:, j, :], b, lambda s_: par[:, 1, B2_CW + 4 * s_ + j:B2_CW + 4 * s_ + j + 1], 4,
                         par[:, 1, B2_CB + j:B2_CB + j + 1])
                    free()
                for j in range(4):
                    split()
                    b = filled()
                    v.tensor_copy(gT[:, j, :], ps[:, b, :])
                    free()
                    v.sem_inc(conv_done.sem, 1)
                for j in range(4):
                    if j < 3:
                        split()
                    b = filled()
                    v.tensor_copy(vtok[:, :, j * P:(j + 1) * P], ps[:, b, :].rearrange("p (n c) -> p n c", n=NT))
                    free()
                small_done.next(v)
                v.tensor_scalar(fF[0:4, :], ps[0:4, 4, :], head[:, 2:3], None, ALU.add)
                v.drain()
                v.sem_inc(small2_copied.sem, 1)

                g_abs.next(v)
                x_, z_, z2, sr = hgw[:, 4:8], hgw[:, 8:12], hgw[:, 0:4], hgw[:, 12:16]
                link(v.tensor_scalar(z_, x_, 2.0, None, ALU.add))
                link(v.reciprocal(z_, z_))
                link(v.tensor_tensor(z_, z_, x_, ALU.mult))
                link(v.tensor_tensor(z2, z_, z_, ALU.mult))
                link(v.tensor_scalar(sr, z2, 1.0 / 15, 1.0 / 13, ALU.mult, ALU.add))
                for o in (11, 9, 7, 5, 3, 1):
                    link(v.tensor_tensor(sr, sr, z2, ALU.mult))
                    link(v.tensor_scalar(sr, sr, 1.0 / o, None, ALU.add))
                link(v.tensor_tensor(sr, sr, z_, ALU.mult))
                link(v.tensor_scalar(z_, par[:, 1, B2_LAM:B2_LAM + 4], -1.0, 0.0, ALU.mult, ALU.max))
                link(v.tensor_scalar(sr, sr, 8.0, None, ALU.mult))
                link(v.scalar_tensor_tensor(sr, z_, 4.0, sr, ALU.mult, ALU.add))
                v.sem_inc(g_soft.sem, 1)
                g_gelu.next(v, 4)
                for j in range(4):
                    lr_tanh.next(v)
                    lr_sig.next(v)
                    link(v.tensor_scalar(rec[:, :], tt[:, :], 1.0, None, ALU.add))
                    link(v.reciprocal(rec[:, :], rec[:, :]))
                    v.tensor_scalar(aa[:, :], rec[:, :], 2.0, -1.0, ALU.mult, ALU.add)
                    link(v.scalar_tensor_tensor(bt[:, :], rt[:, :], 2.0, rec[:, :], ALU.mult, ALU.mult))
                    link(v.tensor_tensor(bt[:, :], bt[:, :], it[:, :], ALU.mult))
                    v.sem_inc(lr_b.sem, 1)
                    link(v.tensor_tensor(bt[:, :], bt[:, :], uT[:, j, :], ALU.mult))
                    link(v.tensor_tensor_scan(rec[:, :], aa[:, :], bt[:, :], 0.0, ALU.mult, ALU.add))
                    link(v.tensor_tensor(uT[:, j, :], rec[:, :], gT[:, j, :], ALU.mult))
                v.sem_inc(lr_y.sem, 1)

                def out_norm(srcs, first):
                    root()
                    for j, src in enumerate(srcs):
                        v.scalar_tensor_tensor(o2[:, first + j, :], src,
                                               par[:, 1, B2_GM + first + j:B2_GM + first + j + 1], rstd[:, :],
                                               ALU.mult, ALU.mult)
                    v.drain()

                out_norm([uT[:, j, :] for j in range(4)], 0)
                for h in range(4):
                    r, q = 64 * (h % 2), h // 2
                    for b in range(NT):
                        N = T - b * P
                        sb_sp.next(v)
                        link(v.scalar_tensor_tensor(Lb[:, b, 0:N], ps[:, b, 0:N], 0.0, sbt[:, b, 0:N],
                                                    ALU.max, ALU.add))
                        v.sem_inc(sb_used.sem, 1)
                        v.tensor_tensor(Lb[:, b, 0:P], Lb[:, b, 0:P], strict[:], ALU.mult).then_inc(sb_l.sem, 1)
                    for b in range(NT):
                        N = T - b * P
                        sb_p.next(v)
                        if b >= 2:
                            v.wait_ge(sb_pv.sem, NT * h + b - 1)
                        v.tensor_scalar(wsb[:, b % 2, 0:N], ps[:, 6, 0:N], 0.0, None, ALU.min)\
                            .then_inc(sb_min.sem, 1)
                        sb_exp.next(v)
                        link(v.tensor_tensor(wsb[:, b % 2, 0:P], wsb[:, b % 2, 0:P], strict[:], ALU.mult))
                        v.sem_inc(sb_w.sem, 1)
                    sb_pv.next(v, NT)
                    v.tensor_copy(o2[r:r + 64, 4 + q, :], ps[r:r + 64, 7, :]).then_inc(sb_out.sem, 1)
                sb_out.next(v, 4)
                out_norm([o2[:, 4 + j, :] for j in range(2)], 4)
                v.sem_inc(ff_in.sem, 1)
                ff_ln.next(v)
                link(v.scalar_tensor_tensor(fF[0:4, :], fF[0:4, :], 0.0, ftmp[0:4, :], ALU.min, ALU.subtract))
                link(v.tensor_tensor_scan(fF[0:4, :], ones[0:4, :], fF[0:4, :], 0.0, ALU.mult, ALU.add))
                v.tensor_scalar(fneg[0:4, :], fF[0:4, :], -1.0, None, ALU.mult)
                for h in range(4):
                    v.tensor_scalar(fsel[0:4, h, :], fF[0:4, :], ident[0:4, h:h + 1], None, ALU.mult)
                v.drain().then_inc(ff_sel.sem, 1)
                softmax(lg2, pr2, mx2, sm2, lambda t: causaladd[:, (NT - 1 - t) * P:T], o2[:, 6:8, :])
                v.drain()
                out_norm([o2[:, 6 + j, :] for j in range(2)], 6)
                v.sem_inc(mix_ready.sem, 1)
                for k in range(KD):
                    b = filled()
                    gated(ps[:, b, :], 1, k)
                    free()
                    v.sem_inc(x_ready.sem, 1)
                split()
                mod_norm(2)
                ffn()
                down_done.next(v, 8)
                for k in range(KD):
                    gated(ps[:, k, :], 2, k)
                end(l + 4)

            res = arena[:, 0:NT * D].rearrange("p (n d) -> p n d", n=2 * NT)
            for n in range(2 * NT):
                v.wait_ge(out_tr.sem, n + 1)
                v.tensor_copy(res[:, n, :], ps[:, n % 4, :]).then_inc(out_cp.sem, 1)
            v.wait_ge(out_cp.sem, 2 * NT)


_INS = ["x", "w_in", "dn_conv", "dn_a_log", "dn_dt_bias", "dn_norm", "hg_lb", "hg_norm", "w_out", "g_mix_pre",
        "g_mix_post", "g_ffn_pre", "g_ffn_post", "ffn_w_up", "ffn_conv", "ffn_w_down", "c_2", "w_ada_2",
        "b_ada_2", "g_norm_2", "w_ffn_up_2", "w_ffn_down_2", "w_in_2", "b_fgate_2", "conv_w_2", "conv_b_2",
        "w_rgate_2", "b_rgate_2", "w_igate_2", "b_igate_2", "lru_lambda_2", "g_qk_2", "g_mix_out_2", "w_out_2"]


def kernel(**inputs):
    import numpy as _np
    import concourse.bacc as _bacc
    from concourse import mybir as _mybir
    from concourse.bass_utils import run_bass_kernel_spmd as _run

    nc = _bacc.Bacc("TRN2", target_bir_lowering=False, num_devices=1)
    arrays, args = {}, {}
    for name in _INS:
        arr = _np.ascontiguousarray(inputs[name])
        arrays[f"in_{name}"] = arr
        args[name] = nc.dram_tensor(f"in_{name}", arr.shape, _mybir.dt.from_np(arr.dtype), kind="ExternalInput").ap()
    res = nc.dram_tensor("out_x", (1, T, D), _mybir.dt.float32, kind="ExternalOutput").ap()
    program(nc, args, res)
    r = _run(nc, [arrays], core_ids=[0])
    return r.results[0]["out_x"]
```
